# Optimizing a Trainium2 kernel written in Bass

```python
import jax, jax.numpy as jnp
from jax import lax
import numpy as np

D_MODEL = 2048
BATCH = 1
SEQ = 256
DEPTH = 1
DEC_BATCH = 8
DEC_SEQ = 4
PAST_LEN = 2048
PAGE_SIZE = 128

CONV_WIDTH = D_MODEL // 2
CONV_K = 3
POOL_WIDTH = D_MODEL // 2
POOL_WINDOWS = (2, 4, 8, 16)
N_POOL_GROUPS = 4
POOL_GROUP = POOL_WIDTH // N_POOL_GROUPS
POOL_STATE = 15
CHUNK = 128
GMLP_WIDTH = D_MODEL // 2
GMLP_HEAD = 128
GMLP_HEADS = GMLP_WIDTH // GMLP_HEAD
N_BRANCH = 3
IN_COLS = 3 * CONV_WIDTH + POOL_WIDTH + 2 * GMLP_WIDTH + N_BRANCH * D_MODEL
N_GROUPS_MOE = 4
EXP_PER_GROUP = 4
N_EXPERTS = N_GROUPS_MOE * EXP_PER_GROUP
TOP_K = 2
D_FF_EXPERT = D_MODEL // 4
EPS = 1e-6

kernel_name = 'hybrid_conv_pool_gmlp_hmoe_step'

def rmsnorm(x, g):
    xf = x.astype(jnp.float32)
    r = lax.rsqrt(jnp.mean(xf * xf, axis=-1, keepdims=True) + EPS)
    return (xf * r).astype(x.dtype) * g

def conv_mixer(bg, cg, hc, conv_w, prev):
    z = cg * hc
    zz = jnp.concatenate([prev.astype(z.dtype), z], axis=1)
    L = z.shape[1]
    y = sum(conv_w[k] * zz[:, k:k + L] for k in range(CONV_K))
    return bg * y, zz[:, L:]

def pool_mixer(p, prev, pos0, pool_w, pool_scale):
    B, L, _ = p.shape
    pp = jnp.concatenate([prev.astype(p.dtype), p], axis=1)
    cs = jnp.pad(jnp.cumsum(pp.astype(jnp.float32), axis=1), ((0, 0), (1, 0), (0, 0)))
    end = cs[:, POOL_STATE + 1:POOL_STATE + 1 + L]
    t = jnp.arange(L)
    means = []
    for g, w in enumerate(POOL_WINDOWS):
        sl = slice(g * POOL_GROUP, (g + 1) * POOL_GROUP)
        start = cs[:, POOL_STATE + 1 - w:POOL_STATE + 1 - w + L, sl]
        cnt = jnp.minimum(pos0 + t + 1, w).astype(jnp.float32)[None, :, None]
        means.append((end[..., sl] - start) / cnt)
    mean = jnp.concatenate(means, axis=-1).astype(p.dtype)
    d = (mean - p).reshape(B, L, N_POOL_GROUPS, POOL_GROUP)
    y = jnp.einsum('blgi,gio->blgo', d, pool_w).reshape(B, L, POOL_WIDTH) * pool_scale
    return y, pp[:, L:]

def gmlp_mixer(u, v, g_v, w_s, b_s):
    B, L, _ = v.shape
    vn = rmsnorm(v, g_v)
    lc = min(L, CHUNK)
    nc = L // lc
    mask = jnp.tril(jnp.ones((lc, lc), dtype=bool))
    ws = jnp.where(mask[None], w_s[:, :lc, :lc], 0)
    vr = vn.reshape(B, nc, lc, GMLP_HEADS, GMLP_HEAD)
    s = jnp.einsum('hts,bnshc->bnthc', ws, vr) + b_s[:, :lc].T[None, None, :, :, None]
    return u * s.reshape(B, L, GMLP_WIDTH), vn

def hier_moe(h, w_rg, b_rg, w_re, b_re, w_gate, w_up, w_down):
    B, L, D = h.shape
    t = h.reshape(-1, D)
    n = t.shape[0]
    grp_logits = (t @ w_rg + b_rg).astype(jnp.float32)
    grp_prob = jax.nn.softmax(grp_logits, axis=-1)
    _, gsel = lax.top_k(grp_logits, 1)
    gp = jnp.take_along_axis(grp_prob, gsel, axis=1)
    exp_logits = (t @ w_re + b_re).astype(jnp.float32).reshape(n, N_GROUPS_MOE, EXP_PER_GROUP)
    idx = jnp.broadcast_to(gsel[:, :, None], (n, 1, EXP_PER_GROUP))
    sel_logits = jnp.take_along_axis(exp_logits, idx, axis=1)[:, 0]
    top_v, top_i = lax.top_k(sel_logits, TOP_K)
    top_w = jax.nn.softmax(top_v, axis=-1) * gp
    expert_id = gsel * EXP_PER_GROUP + top_i
    combine = jnp.sum(jax.nn.one_hot(expert_id, N_EXPERTS, dtype=jnp.float32) * top_w[..., None], axis=1)
    a = jnp.einsum('nd,edf->enf', t, w_gate)
    b = jnp.einsum('nd,edf->enf', t, w_up)
    hid = jax.nn.silu(a) * b * combine.T.astype(t.dtype)[:, :, None]
    y = jnp.einsum('enf,efd->nd', hid, w_down)
    return y.reshape(B, L, D)

def decoder_layer(x, c, prev_conv, prev_pool, pos0, w_ada, b_ada, g_norm1, w_in, conv_w, pool_w, pool_scale,
                  g_v, w_s, b_s, w_br, w_o, g_norm2, w_rg, b_rg, w_re, b_re, w_gate, w_up, w_down):
    mod = (c @ w_ada + b_ada)[:, None, :]
    sh1, sc1, gt1, sh2, sc2, gt2 = jnp.split(mod, 6, axis=-1)
    h = rmsnorm(x, g_norm1) * (1 + sc1) + sh1
    proj = h @ w_in
    cuts = [CONV_WIDTH, 2 * CONV_WIDTH, 3 * CONV_WIDTH, 3 * CONV_WIDTH + POOL_WIDTH,
            3 * CONV_WIDTH + POOL_WIDTH + GMLP_WIDTH, 3 * CONV_WIDTH + POOL_WIDTH + 2 * GMLP_WIDTH]
    bg, cg, hc, p, u, v, gates = jnp.split(proj, cuts, axis=-1)
    y_a, conv_state = conv_mixer(bg, cg, hc, conv_w, prev_conv)
    y_b, pool_state = pool_mixer(p, prev_pool, pos0, pool_w, pool_scale)
    y_c, v_rows = gmlp_mixer(u, v, g_v, w_s, b_s)
    branches = jnp.einsum('blnw,nwd->blnd', jnp.stack([y_a, y_b, y_c], axis=2), w_br)
    gate = jax.nn.sigmoid(gates.reshape(gates.shape[0], gates.shape[1], N_BRANCH, D_MODEL))
    merged = jnp.sum(gate * branches, axis=2)
    x = x + gt1 * (merged @ w_o)
    h2 = rmsnorm(x, g_norm2) * (1 + sc2) + sh2
    x = x + gt2 * hier_moe(h2, w_rg, b_rg, w_re, b_re, w_gate, w_up, w_down)
    return x, conv_state, pool_state, v_rows

def run_trunk(x, c, state_conv, state_pool, pos0, weights, g_final):
    convs, pools, vs = [], [], []
    for l in range(DEPTH):
        lw = [w[l] for w in weights]
        x, cst, pst, vr = decoder_layer(x, c, state_conv[l], state_pool[l], pos0, *lw)
        convs.append(cst)
        pools.append(pst)
        vs.append(vr)
    return rmsnorm(x, g_final), jnp.stack(convs), jnp.stack(pools), jnp.stack(vs)

def setup_inputs(seed: int = 0) -> dict:
    key = jax.random.key(seed)
    ks = jax.random.split(key, 32)
    f32 = jnp.float32

    def nrm(k, shape, scale=1.0):
        return jax.random.normal(k, shape, f32) * scale

    D = D_MODEL
    return {
        'x_prompt': nrm(ks[0], (BATCH, SEQ, D)),
        'x_sample': nrm(ks[1], (DEC_BATCH, DEC_SEQ, D)),
        'c_prompt': nrm(ks[2], (BATCH, D)),
        'c_sample': nrm(ks[3], (DEC_BATCH, D)),
        'state_conv': nrm(ks[4], (DEPTH, DEC_BATCH, CONV_K - 1, CONV_WIDTH)),
        'state_pool': nrm(ks[5], (DEPTH, DEC_BATCH, POOL_STATE, POOL_WIDTH)),
        'w_ada': nrm(ks[6], (DEPTH, D, 6 * D), 0.2 * D ** -0.5),
        'b_ada': nrm(ks[7], (DEPTH, 6 * D), 0.01),
        'g_norm1': 1.0 + nrm(ks[8], (DEPTH, D), 0.05),
        'w_in': nrm(ks[9], (DEPTH, D, IN_COLS), D ** -0.5),
        'conv_w': nrm(ks[10], (DEPTH, CONV_K, CONV_WIDTH), CONV_K ** -0.5),
        'pool_w': nrm(ks[11], (DEPTH, N_POOL_GROUPS, POOL_GROUP, POOL_GROUP), POOL_GROUP ** -0.5),
        'pool_scale': 1.0 + nrm(ks[12], (DEPTH, POOL_WIDTH), 0.1),
        'g_v': 1.0 + nrm(ks[13], (DEPTH, GMLP_WIDTH), 0.05),
        'w_s': nrm(ks[14], (DEPTH, GMLP_HEADS, CHUNK, CHUNK), CHUNK ** -0.5),
        'b_s': 1.0 + nrm(ks[15], (DEPTH, GMLP_HEADS, CHUNK), 0.1),
        'w_br': nrm(ks[16], (DEPTH, N_BRANCH, CONV_WIDTH, D), CONV_WIDTH ** -0.5),
        'w_o': nrm(ks[17], (DEPTH, D, D), D ** -0.5),
        'g_norm2': 1.0 + nrm(ks[18], (DEPTH, D), 0.05),
        'w_rg': nrm(ks[19], (DEPTH, D, N_GROUPS_MOE), D ** -0.5),
        'b_rg': nrm(ks[20], (DEPTH, N_GROUPS_MOE), 0.01),
        'w_re': nrm(ks[21], (DEPTH, D, N_EXPERTS), D ** -0.5),
        'b_re': nrm(ks[22], (DEPTH, N_EXPERTS), 0.01),
        'w_gate': nrm(ks[23], (DEPTH, N_EXPERTS, D, D_FF_EXPERT), D ** -0.5),
        'w_up': nrm(ks[24], (DEPTH, N_EXPERTS, D, D_FF_EXPERT), D ** -0.5),
        'w_down': nrm(ks[25], (DEPTH, N_EXPERTS, D_FF_EXPERT, D), D_FF_EXPERT ** -0.5),
        'g_final': 1.0 + nrm(ks[26], (D,), 0.05),
    }

def reference(x_prompt, x_sample, c_prompt, c_sample, state_conv, state_pool, w_ada, b_ada, g_norm1, w_in,
              conv_w, pool_w, pool_scale, g_v, w_s, b_s, w_br, w_o, g_norm2, w_rg, b_rg, w_re, b_re,
              w_gate, w_up, w_down, g_final):
    weights = (w_ada, b_ada, g_norm1, w_in, conv_w, pool_w, pool_scale, g_v, w_s, b_s, w_br, w_o, g_norm2,
               w_rg, b_rg, w_re, b_re, w_gate, w_up, w_down)
    zero_conv = jnp.zeros((DEPTH, x_prompt.shape[0], CONV_K - 1, CONV_WIDTH), x_prompt.dtype)
    zero_pool = jnp.zeros((DEPTH, x_prompt.shape[0], POOL_STATE, POOL_WIDTH), x_prompt.dtype)
    y_prompt, conv_p, pool_p, _ = run_trunk(x_prompt, c_prompt, zero_conv, zero_pool, 0, weights, g_final)
    y_sample, conv_s, pool_s, v_s = run_trunk(x_sample, c_sample, state_conv, state_pool, PAST_LEN, weights, g_final)
    return (y_prompt, y_sample, conv_p, pool_p, conv_s, pool_s, v_s)


_drawn_inputs = setup_inputs


def setup_inputs(seed=0):
    import zlib

    import numpy as np

    out = dict(_drawn_inputs(seed))
    spreads = {}
    factors = {'b_ada': 2.971,
     'pool_scale': 4.403,
     'b_s': 4.389,
     'g_norm2': 4.323,
     'b_rg': 8.0,
     'b_re': 8.0}
    for name, (base, spread) in spreads.items():
        noise = np.random.default_rng([zlib.crc32(name.encode()), seed]).standard_normal(out[name].shape)
        drawn = base * np.exp(spread * noise) if base else spread * noise
        out[name] = __import__('jax').numpy.asarray(drawn.astype(out[name].dtype))
    for name, factor in factors.items():
        out[name] = (out[name] * factor).astype(out[name].dtype)
    return out
```

```python
from contextlib import ExitStack

import concourse.bass as bass
from concourse import mybir
from concourse.bass import ds

F32 = mybir.dt.float32
F32R = mybir.dt.float32r
I32 = mybir.dt.int32
ALU = mybir.AluOpType
ACT = mybir.ActivationFunctionType
AX_X = mybir.AxisListType.X

P = 128
D = 2048
KT = D // P
TP = 256
NB, NL = 8, 4
TS = NB * NL
T = TP + TS
TT = [(0, P), (P, P), (TP, TS)]
NSEQ = 1 + NB
W = D // 2
WT = W // P
NPAR = 4
PST = 15
HALF = 8
NSPL = 3
NE, EPG, NG = 16, 4, 4
FF = D // 4
FT = FF // P
CAP = 64
EPS = 1e-6
BIG = 3.0e38

KB = 1024
ADA1_BLOCKS = 8
ADA_CHUNKS = 4
MIX_TILES = 48
MIX_RING = 6
MIX_IT = MIX_TILES // MIX_RING
MIX_HALVES = 2 * MIX_TILES
GATE_HALVES = 9
WO_BASE = MIX_HALVES + KT * GATE_HALVES
WO_HALVES = 2 * KT
ALL_HALVES = WO_BASE + WO_HALVES

C_BADA, C_G1, C_G2, C_GF, C_GV, C_PS, C_CW = 0, 96, 112, 128, 144, 152, 160
N_PAR = 184
SH1, SC1, GT1, SH2, SC2, GT2 = (KT * i for i in range(6))


class Tally:

    def __init__(self, eng, sem):
        self.eng, self.sem, self.n, self.at = eng, sem, 0, None

    def loop(self, reg, per):
        self.at, self.reg, self.per, self.k = self.n, reg, per, 0

    def end(self, count):
        assert self.k == self.per, (self.k, self.per)
        self.n, self.at = self.at + self.per * count, None

    def link(self, ins):
        ins.then_inc(self.sem, 1)
        if self.at is None:
            self.n += 1
            self.eng.wait_ge(self.sem, self.n)
        else:
            self.k += 1
            self.eng.wait_ge(self.sem, self.reg * self.per + (self.at + self.k))


def build(nc, x_in, c_in, conv_in, pool_in, par_in, inv_in, w_ada, w_mix, w_gt, w_br, w_o, pool_w, w_s, b_s,
          w_r, b_r, w_gate, w_up, w_down, y_out, conv_out, pool_out, v_out):
    ctx = ExitStack()
    with ctx:
        base = (nc.sbuf_base + 31) // 32 * 32

        def at(name, off, shape, dt=F32):
            return nc.alloc_sbuf_tensor_at(name, shape, dt, offset=base + off)

        def size(shape):
            n = 4
            for s in shape[1:]:
                n *= s
            return n

        def region(off, end, *parts):
            out = []
            for name, shape, dt in parts:
                out.append(at(name, off, shape, dt))
                off += (size(shape) + 31) // 32 * 32
            assert off <= end, (parts[0][0], off, end)
            return out

        o_m = 52 * KB
        o_s = o_m + KT * T * 4
        o_h = o_s + 2 * NSPL * HALF * P * 4 + 2 * KB
        o_y = o_h + 2 * KT * T * 4
        o_p = o_y + 3 * KT * T * 4
        o_end = 229344 - base

        ring8 = [at(f"ring{k}", 8 * KB * k, [P, 4, 512]) for k in range(12)]
        mixw = [at(f"mixw{k}", 8 * KB * k, [P, KT, P]) for k in range(MIX_RING)]
        brw = at("brw", 24 * KB, [P, 3 * WT, P])
        adaw = [at(f"adaw{k}", (36 + 8 * k) * KB, [P, 4, 512]) for k in range(2)]
        dring = [at(f"dring{k}", 8 * KB * k, [P, D]) for k in range(12)]

        wst, = region(48 * KB, 52 * KB, ("wst", [P, WT, P], F32))
        merged, = region(o_m, o_s, ("merged", [P, KT, T], F32))
        o_x = o_m
        zzs, ctmp, pp, pa, pb_, pps0, pps1, pst0, pst1 = region(
            o_x, o_x + 3 * 4 * KB,
            ("zzs", [P, WT, NB, 6], F32), ("ctmp", [P, T], F32), ("pp", [P, 16 + TP], F32),
            ("pa", [P, 16 + TP + NB * 20], F32), ("pb_", [P, 16 + TP + NB * 20], F32),
            ("pps0", [P, NB, 20], F32), ("pps1", [P, NB, 20], F32),
            ("pst0", [P, (1 + NB) * PST], F32), ("pst1", [P, (1 + NB) * PST], F32))
        pps, pst = [pps0, pps1], [pst0, pst1]
        vsq, = region(o_x, o_x + 12 * KB, ("vsq", [P, WT, T], F32))
        vtok, = region(o_x, o_x + 12 * KB, ("vtok", [P, 3, W], F32))
        bd, bs = region(o_x + 12 * KB, o_s, ("bd", [TS, WT, TS], F32), ("bs", [P, WT, P], F32))
        wh, wl = region(o_s, o_h, ("wh", [P, NSPL, HALF, P], F32R), ("wl", [P, NSPL, HALF, P], F32R))
        hh, hl = region(o_h, o_y, ("hh", [P, KT, T], F32R), ("hl", [P, KT, T], F32R))
        mh, ml = region(o_h, o_y, ("mh", [P, KT, T], F32R), ("ml", [P, KT, T], F32R))
        proj, = region(o_y, o_p, ("proj", [P, MIX_TILES, T], F32))
        ysp, = region(o_y, o_p, ("ysp", [P, MIX_TILES, T], F32R))
        xa, sq1 = region(o_y, o_p, ("xa", [P, KT, T], F32), ("sq1", [P, KT, T], F32))
        x1, acc, h2 = region(o_y, o_p, ("x1", [P, KT, T], F32), ("acc", [P, KT, T], F32), ("h2", [P, KT, T], F32))
        sq2, = region(o_y + KT * T * 4, o_p, ("sq2", [P, KT, T], F32))
        xg, = region(o_y + 2 * KT * T * 4, o_p, ("xg", [P, KT, EPG * CAP], F32))
        htok, ye, gus, sT0, sT1, hid, sg = region(
            o_h, o_y, ("htok", [P, 3, D], F32), ("ye", [P, D // 2], F32), ("gus", [P, FF], F32),
            ("sT0", [P, T], F32), ("sT1", [P, T], F32), ("hid", [P, FT, CAP], F32), ("sg", [P, FT, CAP], F32))
        sT = [sT0, sT1]
        (mod, par, ident, ones, tri, iota, sel9, wr, br, valid, lg, mk, cb, rk, sc, rnd) = region(
            o_p, o_end, ("mod", [P, 6 * KT, NSEQ], F32), ("par", [P, N_PAR], F32), ("ident", [P, P], F32),
            ("ones", [P, P], F32), ("tri", [P, P], F32), ("iota", [P, CAP], F32), ("sel9", [P, NSEQ], F32),
            ("wr", [P, KT, 20], F32), ("br", [P, 20], F32), ("valid", [P, 3], F32), ("lg", [P, 3, 20], F32),
            ("mk", [P, 3, NE], F32), ("cb", [P, 3, NE], F32), ("rk", [P, 3, NE], F32),
            ("sc", [P, 3, 40], F32), ("rnd", [P, 8], I32))
        o_q = o_p + sum((size(s) + 31) // 32 * 32 for s in (
            [P, 6 * KT, NSEQ], [P, N_PAR], [P, P], [P, P], [P, P], [P, CAP], [P, NSEQ], [P, KT, 20], [P, 20], [P, 3],
            [P, 3, 20], [P, 3, NE], [P, 3, NE], [P, 3, NE], [P, 3, 40], [P, 8]))
        cT, part = region(o_q, o_end, ("cT", [P, KT, 32], F32), ("part", [P, 512], F32))
        o_q2 = o_q + 4 * KB
        a1, a2, v_var, v_rs, v_t = region(
            o_q2, o_end, ("a1", [P, KT, NSEQ], F32), ("a2", [P, KT, NSEQ], F32), ("v_var", [P, T], F32),
            ("v_rs", [P, T], F32), ("v_t", [P, T], F32))
        sig, gt = region(o_q2, o_end, ("sig", [P, 3, T], F32), ("gt", [P, 2, T], F32))
        pw, inv, cst = region(o_q2, o_end, ("pw", [P, NPAR, 2, 2, P], F32), ("inv", [P, NPAR, 16], F32),
                              ("cst", [P, WT, 1 + NB, 2], F32))
        oh, gc = region(o_q, o_end, ("oh", [P, 3, EPG * CAP], F32), ("gc", [P, 3, EPG, 2, CAP], F32))

        bank = [ctx.enter_context(nc.psum_tensor(f"bank{k}", [P, 512], F32)) for k in range(8)]

        def sem(name):
            return ctx.enter_context(nc.semaphore(name))

        x_loaded, c_loaded, par_loaded, mixpar_loaded, x1_loaded = (
            sem(n) for n in ("x_loaded", "c_loaded", "par_loaded", "mixpar_loaded", "x1_loaded"))
        slot_loaded = [sem(f"slot_loaded{k}") for k in range(12)]
        mix_loaded = [sem(f"mix_loaded{k}") for k in range(MIX_RING)]
        br_loaded = sem("br_loaded")
        ada_loaded = [sem("ada_loaded0"), sem("ada_loaded1")]
        pps_loaded = [sem("pps_loaded0"), sem("pps_loaded1")]
        stores = sem("stores")
        pst_stored = [sem("pst_stored0"), sem("pst_stored1")]
        v_stored, conv_stored = sem("v_stored"), sem("conv_stored")
        w_used = sem("w_used")
        ada_used = sem("ada_used")
        ada_sel = sem("ada_sel")
        sums_done, pool_mm, vtr_done, mix_mm = (sem(n) for n in ("sums_done", "pool_mm", "vtr_done", "mix_mm"))
        logits_done, htr_done, rank_done = sem("logits_done"), sem("htr_done"), sem("rank_done")
        gath_done, tr_done, st_done, scat_done, moe_used = (
            sem(n) for n in ("gath_done", "tr_done", "st_done", "scat_done", "moe_used"))
        sq_ready, std_ready, part_ready, hh_ready, hi_ready = (
            sem(n) for n in ("sq_ready", "std_ready", "part_ready", "hh_ready", "hi_ready"))
        tile_saved = sem("tile_saved")
        yb_ready, vtok_a, sig_ready, mh_ready, htok_a, exp_ready = (
            sem(n) for n in ("yb_ready", "vtok_a", "sig_ready", "mh_ready", "htok_a", "exp_ready"))
        xg_a, gu_saved, sg_ready, st_ready, ye_a = (
            sem(n) for n in ("xg_a", "gu_saved", "sg_ready", "st_ready", "ye_a"))
        dch, var_ready, mod_ready, h_ready, hl_ready, lo_ready = (
            sem(n) for n in ("dch", "var_ready", "mod_ready", "h_ready", "hl_ready", "lo_ready"))
        vn_ready, vtok_d, yc_ready, merged_ready, ml_ready, x1_ready, h2_ready, htok_d = (
            sem(n) for n in ("vn_ready", "vtok_d", "yc_ready", "merged_ready", "ml_ready", "x1_ready", "h2_ready",
                             "htok_d"))
        exp_in, mk_ready, rounds_ready, oh_ready, gc_ready, xg_d, hid_ready, ye_d, acc_ready, zero_ready, y_ready = (
            sem(n) for n in ("exp_in", "mk_ready", "rounds_ready", "oh_ready", "gc_ready", "xg_d", "hid_ready",
                             "ye_d", "acc_ready", "zero_ready", "y_ready"))
        pch, consts, masked, ya_ready, d_ready, ybs_ready, ycs_ready = (
            sem(n) for n in ("pch", "consts", "masked", "ya_ready", "d_ready", "ybs_ready", "ycs_ready"))

        def mix_unit(it, k):
            if k >= 2 * MIX_RING:
                it, k = it + 1, k - 2 * MIX_RING
            s, h = k // 2, k % 2
            return (mixw[s][:, HALF * h:HALF * (h + 1), :], mix_loaded[s], it * 16 + 16, it * (2 * MIX_RING) + k, k % NSPL)

        def gate_unit(ot, k):
            if k >= GATE_HALVES:
                ot, k = ot + 1, k - GATE_HALVES
            u = ot * GATE_HALVES + (MIX_HALVES + k)
            if k < 6:
                return (mixw[k // 2][:, HALF * (k % 2):HALF * (k % 2 + 1), :], mix_loaded[k // 2],
                        ot * 16 + 16 * (MIX_IT + 1), u, k % NSPL)
            return brw[:, HALF * (k - 6):HALF * (k - 5), :], br_loaded, ot * 16 + 16, u, k % NSPL

        def wo_unit(v, k):
            if k >= 6:
                v, k = v + 1, k - 6
            s, h = k // 2, k % 2
            return (mixw[s][:, HALF * h:HALF * (h + 1), :], mix_loaded[s], v * 16 + 16 * (MIX_IT + KT + 1),
                    v * 6 + (WO_BASE + k), k % NSPL)

        def mix_then_gates(it, k):
            return mix_unit(it, k) if it < MIX_IT - 1 or k < 2 * MIX_RING else gate_unit(0, k - 2 * MIX_RING)

        def gates_then_wo(ot, k):
            return gate_unit(ot, k) if ot < KT - 1 or k < GATE_HALVES else wo_unit(0, k - GATE_HALVES)

        from_one = {"tensor": (ada_sel, tr_done, gath_done, st_done), "scalar": (part_ready, st_ready, ye_a), "vector": (mod_ready, merged_ready, hid_ready, acc_ready, ye_d)}

        def slot_uses(k):
            return 16 * (ADA1_BLOCKS // 2) if k < 8 else 0

        block = ctx.enter_context(nc.Block())

        @block.sync
        def _(sp):
            sp.dma_start(xa[:], x_in).then_inc(x_loaded, 16)
            sp.dma_start(cT[:], c_in).then_inc(c_loaded, 16)
            sp.dma_start(par[:], par_in).then_inc(par_loaded, 16)
            sp.dma_start(wr[:], w_r).then_inc(par_loaded, 16)
            sp.dma_start(br[:], b_r.partition_broadcast(P)).then_inc(par_loaded, 16)

            def ada_src(blk, j):
                return w_ada.rearrange("(k p) n -> p k n", p=P)[:, 4 * j:4 * j + 4, blk]

            for k in range(8):
                sp.dma_start(ring8[k][:], ada_src(slice(KT * P * (k // 4), KT * P * (k // 4) + 512), k % 4))\
                    .then_inc(slot_loaded[k], 16)
            with sp.Fori(0, 3) as it:
                for k in range(8):
                    sp.wait_ge(ada_used, it * 8 + (k + 1))
                    sp.dma_start(ring8[k][:], ada_src(ds(it * 512 + (512 + KT * P * (k // 4)), 512), k % 4))\
                        .then_inc(slot_loaded[k], 16)

            for k in range(MIX_RING):
                sp.wait_ge(ada_used, 24 + k + 1)
                sp.dma_start(mixw[k][:], w_mix[k]).then_inc(mix_loaded[k], 16)
            sp.wait_ge(ada_used, 32)
            sp.dma_start(wst[:], w_s).then_inc(mixpar_loaded, 16)
            sp.dma_start(bs[:], b_s.partition_broadcast(P)).then_inc(mixpar_loaded, 16)
            sp.dma_start(zzs[:], conv_in).then_inc(mixpar_loaded, 16)
            sp.wait_ge(h_ready, 4)
            sp.dma_start(pw[:], pool_w).then_inc(mixpar_loaded, 16)
            sp.dma_start(inv[:], inv_in).then_inc(mixpar_loaded, 16)
            sp.wait_ge(consts, 1)
            for b in range(NB):
                sp.dma_start(bd[NL * b:NL * b + NL, :, NL * b:NL * b + NL], w_s[0:NL, :, 0:NL])\
                    .then_inc(mixpar_loaded, 16)
            with sp.Fori(1, MIX_IT) as it:
                for k in range(MIX_RING):
                    sp.wait_ge(lo_ready, it * 12 + (2 * k + 2 - 12))
                    sp.dma_start(mixw[k][:], w_mix[ds(it * MIX_RING + k, 1)].rearrange("a p k c -> p (a k) c"))\
                        .then_inc(mix_loaded[k], 16)

            def gate_load(ot, n, at_value):
                sp.wait_ge(lo_ready, at_value)
                sp.dma_start(mixw[n][:], w_gt[ds(ot * 3 + n, 1)].rearrange("a p k c -> p (a k) c"))\
                    .then_inc(mix_loaded[n], 16)

            def br_load(ot):
                sp.wait_ge(lo_ready, ot * GATE_HALVES + MIX_HALVES)
                sp.dma_start(brw[:], w_br[ds(ot, 1)].rearrange("a p k c -> p (a k) c")).then_inc(br_loaded, 16)

            def ada_load(ot, j):
                sp.wait_ge(ada_used, ot * 4 + (32 + j - 1))
                sp.dma_start(adaw[j % 2][:], ada_src(ds(ot * 512 + ADA1_BLOCKS * 512, 512), j))\
                    .then_inc(ada_loaded[j % 2], 16)

            for n in range(3):
                gate_load(0, n, 2 * (MIX_TILES - MIX_RING + n) + 2)
            br_load(0)
            sp.wait_ge(mix_mm, WT)
            ada_load(0, 0)
            ada_load(0, 1)
            with sp.Fori(0, KT - 1) as ot:
                ada_load(ot, 2)
                ada_load(ot, 3)
                for n in range(3):
                    gate_load(ot + 1, n, ot * GATE_HALVES + (MIX_HALVES + 2 * n + 2))
                ada_load(ot + 1, 0)
                ada_load(ot + 1, 1)
                br_load(ot + 1)
            ada_load(KT - 1, 2)
            ada_load(KT - 1, 3)

            def wo_load(v, s):
                sp.wait_ge(lo_ready, v * 6 + (WO_BASE + 2 * s + 2 - 6))
                sp.dma_start(mixw[s][:], w_o[ds(v * 3 + s, 1)].rearrange("a p k c -> p (a k) c"))\
                    .then_inc(mix_loaded[s], 16)

            for s in range(3):
                sp.wait_ge(lo_ready, WO_BASE - GATE_HALVES + 2 * s + 2)
                sp.dma_start(mixw[s][:], w_o[s]).then_inc(mix_loaded[s], 16)

            def expert_load(n, c):
                k = (c + 3) % 12
                e = ds(n, 1)
                if c < 8:
                    src = (w_up if c % 2 else w_gate)[e].rearrange("a (k p) n -> p (a k) n", p=P)
                    sp.dma_start(ring8[k][:], src[:, 4 * (c // 2):4 * (c // 2) + 4, :]).then_inc(slot_loaded[k], 16)
                else:
                    src = w_down[e].rearrange("a (k p) n -> p (a k) n", p=P)
                    sp.dma_start(dring[k][:], src[:, c - 8, :]).then_inc(slot_loaded[k], 16)

            sp.wait_ge(lo_ready, WO_BASE)
            sp.wait_ge(ada_used, 32 + 4 * KT)
            for c in range(3):
                expert_load(0, c)
            sp.wait_ge(merged_ready, KT + 1)
            sp.dma_start(x1[:], x_in).then_inc(x1_loaded, 16)
            sp.wait_ge(ml_ready, 4)
            for c in (3, 4):
                expert_load(0, c)
            with sp.Fori(1, 5) as v:
                for s in range(3):
                    wo_load(v, s)
            wo_load(5, 0)
            sp.wait_ge(lo_ready, ALL_HALVES)
            sp.wait_ge(w_used, ALL_HALVES + NSPL)
            for c in range(5, 12):
                expert_load(0, c)
            with sp.Fori(1, NE) as n:
                for c in range(12):
                    sp.wait_ge(moe_used, n * 12 + (c + 1 - 12))
                    expert_load(n, c)
            sp.wait_ge(rounds_ready, 1)
            rounds = sp.value_load(rnd[0:1, 0:1], min_val=1, max_val=-(-T // CAP))
            with sp.If(rounds > 1):
                with sp.Fori(1, rounds) as r:
                    with sp.Fori(0, NE) as n:
                        for c in range(12):
                            sp.wait_ge(moe_used, r * (12 * NE) + n * 12 + (c + 1 - 12))
                            expert_load(n, c)
            for q in range(4):
                sp.wait_ge(y_ready, q + 1)
                sp.dma_start(y_out[:, 4 * q:4 * q + 4, :], h2[:, 4 * q:4 * q + 4, :]).then_inc(stores, 16)
            sp.wait_ge(stores, 16 * 4)
            sp.wait_ge(conv_stored, 16)
            sp.wait_ge(v_stored, 16)
            for k in range(2):
                sp.wait_ge(pst_stored[k], 16 * WT // 2)

        @block.gpsimd
        def _(gp):
            chain = Tally(gp, pch)

            def select(m, pattern, base_, mult, op, fill):
                return gp.affine_select(out=m, in_=m, compare_op=op, fill=fill, base=base_, pattern=pattern,
                                        channel_multiplier=mult)

            gp.memset(bd[:], 0.0)
            gp.memset(ident[:], 0.0)
            gp.memset(sel9[:], 0.0)
            gp.memset(tri[:], 1.0)
            gp.memset(valid[:], 1.0)
            chain.link(gp.memset(ones[:], 1.0))
            select(ident[:], [[-1, P]], 0, 1, ALU.not_equal, 1.0)
            for q in range(4):
                chain.link(select(sel9[:], [[-1, NSEQ]], -32 * q, 1, ALU.not_equal, 1.0))
            select(tri[:], [[1, P]], 0, -1, ALU.is_gt, 0.0)
            select(valid[:, 2:3], [[0, 1]], TS, -1, ALU.is_gt, 0.0)
            gp.iota(iota[:], [[1, CAP]], base=0, channel_multiplier=0,
                    allow_small_or_imprecise_dtypes=True).then_inc(consts, 1)

            gp.wait_ge(mixpar_loaded, 16 * (5 + NB))
            select(wst[:], [[0, WT], [1, P]], 0, -1, ALU.is_ge, 0.0)
            select(bd[:], [[0, WT], [1, TS]], 0, -1, ALU.is_ge, 0.0).then_inc(masked, 1)

            def smp(ap):
                return ap[:, TP:T].rearrange("p (b l) -> p b l", l=NL)

            gp.wait_ge(tile_saved, MIX_RING + 3 * WT)
            for f in range(WT):
                cg, hc, bg = proj[:, f, :], proj[:, WT + f, :], proj[:, 2 * WT + f, :]
                zs = zzs[:, f]
                cw = [par[:, C_CW + 3 * f + k:C_CW + 3 * f + k + 1] for k in range(3)]

                chain.link(gp.tensor_tensor(cg, cg, hc, ALU.mult))
                chain.link(gp.tensor_copy(zs[:, :, 2:6], smp(cg)))
                gp.tensor_copy(cst[:, f, 0, :], cg[:, TP - 2:TP])
                gp.tensor_copy(cst[:, f, 1:1 + NB, :], zs[:, :, 4:6])
                chain.link(gp.tensor_scalar(hc, cg, cw[2], 0.0, ALU.mult, ALU.add))
                for k in (1, 0):
                    d = 2 - k
                    chain.link(gp.tensor_scalar(ctmp[:, 0:TP - d], cg[:, 0:TP - d], cw[k], 0.0, ALU.mult, ALU.add))
                    chain.link(gp.tensor_tensor(hc[:, d:TP], hc[:, d:TP], ctmp[:, 0:TP - d], ALU.add))
                    chain.link(gp.tensor_scalar(smp(ctmp), zs[:, :, k:k + NL], cw[k], 0.0, ALU.mult, ALU.add))
                    chain.link(gp.tensor_tensor(smp(hc), smp(hc), smp(ctmp), ALU.add))
                chain.link(gp.tensor_tensor(bg, bg, hc, ALU.mult))
                yh, yl = ysp[:, f, :], ysp[:, WT + f, :]
                chain.link(gp.tensor_copy(yh, bg))
                chain.link(gp.tensor_tensor(yl, bg, yh.bitcast(F32), ALU.subtract))
            gp.memset(pp[:, 0:16], 0.0).then_inc(ya_ready, 1)
            gp.wait_ge(ya_ready, 1)
            gp.dma_start(conv_out, cst[:]).then_inc(conv_stored, 16)

            for f in range(2):
                gp.dma_start(pps[f][:], pool_in[f]).then_inc(pps_loaded[f], 16)
            gp.wait_ge(tile_saved, MIX_RING + 4 * WT)
            NPP = 16 + TP
            for f in range(WT):
                g, n = f // 2, f // 2 + 1
                p_t = proj[:, 3 * WT + f, :]
                p_s = p_t[:, TP:T].rearrange("p (b l) -> p b l", l=NL)
                ps_ = pps[f % 2]
                st = pst[f % 2]
                gp.wait_ge(pps_loaded[f % 2], 16 * (f // 2 + 1))
                gp.tensor_copy(pp[:, 16:NPP], p_t[:, 0:TP])
                chain.link(gp.tensor_copy(ps_[:, :, 16:20], p_s))
                if f >= 2:
                    gp.wait_ge(pst_stored[f % 2], 16 * (f // 2))
                gp.tensor_copy(st[:, 0:PST], p_t[:, TP - PST:TP])
                chain.link(gp.tensor_copy(st[:, PST:].rearrange("p (b l) -> p b l", l=PST), ps_[:, :, 5:20]))
                gp.dma_start(pool_out[f], st[:]).then_inc(pst_stored[f % 2], 16)
                src, src_s, bufs = pp[:], ps_[:], [pa, pb_]
                for k in range(n):
                    s_, lo = 1 << k, (1 << (k + 1)) - 1
                    dst = bufs[k % 2][:, 0:NPP]
                    dst_s = bufs[k % 2][:, NPP:].rearrange("p (b l) -> p b l", l=20)
                    gp.tensor_tensor(dst[:, lo:NPP], src[:, lo:NPP], src[:, lo - s_:NPP - s_], ALU.add)
                    chain.link(gp.tensor_tensor(dst_s[:, :, lo:20], src_s[:, :, lo:20], src_s[:, :, lo - s_:20 - s_],
                                                ALU.add))
                    src, src_s = dst, dst_s
                mean, mean_s = bufs[n % 2][:, 0:NPP], bufs[n % 2][:, NPP:].rearrange("p (b l) -> p b l", l=20)
                gp.tensor_scalar(mean[:, 32:NPP], src[:, 32:NPP], 1.0 / (1 << n), 0.0, ALU.mult, ALU.add)
                gp.tensor_tensor(mean[:, 16:32], src[:, 16:32], inv[:, g, :], ALU.mult)
                chain.link(gp.tensor_scalar(mean_s[:, :, 16:20], src_s[:, :, 16:20], 1.0 / (1 << n), 0.0,
                                            ALU.mult, ALU.add))
                chain.link(gp.tensor_tensor(p_t[:, 0:TP], mean[:, 16:NPP], pp[:, 16:NPP], ALU.subtract))
                gp.tensor_tensor(p_s, mean_s[:, :, 16:20], ps_[:, :, 16:20], ALU.subtract).then_inc(d_ready, 1)
                if f + 2 < WT:
                    gp.wait_ge(d_ready, f + 1)
                    gp.dma_start(ps_[:], pool_in[f + 2]).then_inc(pps_loaded[f % 2], 16)

            gp.wait_ge(vn_ready, WT)
            gp.dma_start(v_out, proj[:, 4 * WT:5 * WT, TP:T]).then_inc(v_stored, 16)

            for f in range(WT):
                gp.wait_ge(yb_ready, f + 1)
                gp.wait_ge(pool_mm, min(WT, 2 * (f // 2) + 2))
                gp.tensor_copy(ysp[:, 3 * WT + f, :], proj[:, 2 * WT + f, :]).then_inc(ybs_ready, 1)
                gp.wait_ge(ybs_ready, 2 * f + 1)
                gp.tensor_tensor(ysp[:, 2 * WT + f, :], proj[:, 2 * WT + f, :],
                                 ysp[:, 3 * WT + f, :].bitcast(F32), ALU.subtract).then_inc(ybs_ready, 1)
            gp.wait_ge(v_stored, 16)
            gp.wait_ge(vtr_done, 6)
            for f in range(WT):
                gp.wait_ge(yc_ready, f + 1)
                gp.tensor_copy(ysp[:, 4 * WT + f, :], proj[:, 5 * WT + f, :]).then_inc(ycs_ready, 1)
                gp.wait_ge(ycs_ready, 2 * f + 1)
                gp.tensor_tensor(ysp[:, 5 * WT + f, :], proj[:, 5 * WT + f, :],
                                 ysp[:, 4 * WT + f, :].bitcast(F32), ALU.subtract).then_inc(ycs_ready, 1)

        @block.scalar
        def _(act):
            act.sem_inc(tile_saved, MIX_RING)
            act.sem_inc(sig_ready, 3)
            for s in from_one["scalar"]:
                act.sem_inc(s, 1)

            def split_hi(unit):
                src, loaded, value, u, b = unit
                act.wait_ge(loaded, value)
                act.wait_ge(w_used, u + 1)
                act.activation(wh[:, b], src, ACT.Copy).then_inc(hi_ready, 1)

            def root(n):
                act.wait_ge(var_ready, n)
                act.activation(v_rs[:], v_var[:], ACT.Sqrt).then_inc(std_ready, 1)

            def save_part(n):
                act.wait_ge(ada_used, n * 4 + 4)
                act.wait_ge(ada_sel, n + 1)
                act.activation(part[:], bank[6][:], ACT.Copy).then_inc(part_ready, 1)

            act.wait_ge(x_loaded, 16)
            for q in range(4):
                act.activation(sq1[:, 4 * q:4 * q + 4, :], xa[:, 4 * q:4 * q + 4, :], ACT.Square).then_inc(sq_ready, 1)
            root(1)
            with act.Fori(0, ADA1_BLOCKS) as n:
                save_part(n)
            for q in range(4):
                act.wait_ge(h_ready, q + 1)
                act.activation(hh[:, 4 * q:4 * q + 4, :], xa[:, 4 * q:4 * q + 4, :], ACT.Copy).then_inc(hh_ready, 1)
            for k in range(NSPL):
                split_hi(mix_unit(0, k))

            def mix_step(it, s, unit):
                split_hi(unit(it, 2 * s + 3))
                act.wait_ge(w_used, it * 12 + (2 * s + 2 + NSPL))
                act.activation(proj[:, ds(it * MIX_RING + s, 1), :].rearrange("p a t -> p (a t)"),
                               bank[s][:, 0:T], ACT.Copy).then_inc(tile_saved, 1)
                split_hi(unit(it, 2 * s + 4))

            with act.Fori(0, MIX_IT - 1) as it:
                for s in range(MIX_RING):
                    mix_step(it, s, mix_unit)

            def save_vtok(u):
                tt, half_ = u // 2, u % 2
                n = TT[tt][1]
                act.wait_ge(vtr_done, u + 1)
                act.activation(vtok[0:n, tt, 512 * half_:512 * half_ + 512], bank[6 + half_][0:n, :], ACT.Copy)\
                    .then_inc(vtok_a, 1)

            for s in range(MIX_RING):
                mix_step(MIX_IT - 1, s, mix_then_gates)
                if s == 0:
                    for f in range(WT):
                        act.wait_ge(pool_mm, f + 1)
                        act.activation(proj[:, 2 * WT + f, :], bank[6 + f % 2][:, 0:T], ACT.Copy,
                                       scale=par[:, C_PS + f:C_PS + f + 1]).then_inc(yb_ready, 1)
                    act.wait_ge(d_ready, WT)
                    for k in range(2):
                        act.wait_ge(pst_stored[k], 16 * WT // 2)
                    act.activation(vsq[:], proj[:, 4 * WT:5 * WT, :], ACT.Square).then_inc(sq_ready, 1)
                if s == 1:
                    root(2)
                if s >= 3:
                    save_vtok(2 * (s - 3))

            def gates_step(ot, unit):
                for n in range(3):
                    split_hi(unit(ot, 2 * n + 3))
                    act.wait_ge(w_used, ot * GATE_HALVES + (MIX_HALVES + 2 * n + 2 + NSPL))
                    act.wait_ge(merged_ready, ot + 1)
                    act.activation(sig[:, n, :], bank[n][:, 0:T], ACT.Sigmoid).then_inc(sig_ready, 1)
                    split_hi(unit(ot, 2 * n + 4))
                save_part(ot + ADA1_BLOCKS)
                for k in (9, 10, 11):
                    split_hi(unit(ot, k))

            with act.Fori(0, KT - 1) as ot:
                gates_step(ot, gate_unit)
            gates_step(KT - 1, gates_then_wo)
            for q in range(4):
                act.wait_ge(merged_ready, KT + 1)
                act.activation(mh[:, 4 * q:4 * q + 4, :], merged[:, 4 * q:4 * q + 4, :], ACT.Copy).then_inc(mh_ready, 1)
            with act.Fori(0, 4) as v:
                for k in range(3, 9):
                    split_hi(wo_unit(v, k))
            for k in range(3, 8):
                split_hi(wo_unit(4, k))

            for q in range(4):
                act.wait_ge(x1_ready, 3 + 4 * (q + 1))
                act.activation(sq2[:, 4 * q:4 * q + 4, :], x1[:, 4 * q:4 * q + 4, :], ACT.Square).then_inc(sq_ready, 1)
            root(3)
            for u in range(0, 12, 2):
                act.wait_ge(htr_done, u + 1)
                n = TT[u // 4][1]
                act.activation(htok[0:n, u // 4, 512 * (u % 4):512 * (u % 4) + 512], bank[2 + u % 2][0:n, :],
                               ACT.Copy).then_inc(htok_a, 1)
            act.wait_ge(exp_in, 1)
            act.activation(sc[:, :, 31:36], sc[:, :, 26:31], ACT.Exp).then_inc(exp_ready, 1)

            def experts(i):
                for q in range(4):
                    act.wait_ge(gath_done, i * 8 + (2 * q + 1) + 1)
                    act.activation(xg[:, 4 * q:4 * q + 2, :],
                                   bank[4].rearrange("p (a n) -> p a n", a=2) if q % 2 == 0 else
                                   bank[6].rearrange("p (a n) -> p a n", a=2), ACT.Copy).then_inc(xg_a, 1)
                for e in range(EPG):
                    m1 = i * EPG + (e + 1)
                    act.wait_ge(moe_used, m1 * 12 - 4)
                    act.wait_ge(tr_done, i * EPG + e + 1)
                    act.activation(gus[:], bank[0][:], ACT.Copy).then_inc(gu_saved, 1)
                    act.wait_ge(st_done, m1 + 1)
                    act.activation(sT[e % 2][:], bank[0][:, 0:T], ACT.Copy).then_inc(st_ready, 1)
                    act.wait_ge(tr_done, m1 + 1)
                    act.wait_ge(hid_ready, i * EPG + e + 1)
                    act.activation(sg[:], bank[1].rearrange("p (f c) -> p f c", f=FT)[:, :, 0:CAP], ACT.Silu)\
                        .then_inc(sg_ready, 1)
                    act.wait_ge(moe_used, m1 * 12)
                    act.activation(ye[:, 0:512], bank[2][:], ACT.Copy).then_inc(ye_a, 1)

            act.wait_ge(rounds_ready, 1)
            rounds = act.value_load(rnd[0:1, 0:1], min_val=1, max_val=-(-T // CAP))
            with act.Fori(0, rounds) as r:
                with act.Fori(0, NG) as g:
                    experts(r * NG + g)
            for q in range(4):
                act.wait_ge(h2_ready, q + 1)
                act.activation(sq2[:, 4 * q:4 * q + 4, :], x1[:, 4 * q:4 * q + 4, :], ACT.Square).then_inc(sq_ready, 1)
            root(4)

        @block.vector
        def _(dve):
            chain = Tally(dve, dch)
            dve.sem_inc(x1_ready, 3)
            for s in from_one["vector"]:
                dve.sem_inc(s, 1)

            def tt(out, a, b, op):
                return dve.tensor_tensor(out, a, b, op)

            def split_lo(unit):
                src, _, _, u, b = unit
                dve.wait_ge(hi_ready, u + 1)
                tt(wl[:, b], src, wh[:, b].bitcast(F32), ALU.subtract).then_inc(lo_ready, 1)

            def rsqrt(sums, n, k):
                dve.tensor_scalar(v_var[:], sums, 1.0 / n, EPS, ALU.mult, ALU.add).then_inc(var_ready, 1)
                dve.wait_ge(std_ready, k)
                chain.link(dve.reciprocal(v_rs[:], v_rs[:]))
                chain.link(tt(v_t[:], v_rs[:], v_rs[:], ALU.mult))
                chain.link(tt(v_t[:], v_t[:], v_var[:], ALU.mult))
                chain.link(dve.tensor_scalar(v_t[:], v_t[:], -0.5, 1.5, ALU.mult, ALU.add))
                chain.link(tt(v_rs[:], v_rs[:], v_t[:], ALU.mult))

            def smp(ap):
                return ap.rearrange("p (b l) -> p b l", l=NL)

            def seqs(ap):
                return ap[:, 1:NSEQ].unsqueeze(2).broadcast_to([P, NB, NL])

            def save_mod(n, chunk):
                dve.wait_ge(ada_sel, n + 1 + 1)
                bias = par[:, ds(chunk, 4)].unsqueeze(2).broadcast_to([P, 4, NSEQ])
                tt(mod[:, ds(chunk, 4), :], bank[7][:, 0:4 * NSEQ].rearrange("p (c s) -> p c s", s=NSEQ), bias, ALU.add)\
                    .then_inc(mod_ready, 1)

            def scales(a, first, g):
                chain.link(dve.scalar_tensor_tensor(a[:], mod[:, first:first + KT, :], 1.0,
                                                    par[:, g:g + KT].unsqueeze(2).broadcast_to([P, KT, NSEQ]),
                                                    ALU.add, ALU.mult))

            def modulate(dst, src, a, shift):
                for q in range(4):
                    for f in range(4 * q, 4 * q + 4):
                        dve.tensor_scalar(dst[:, f, 0:TP], src[:, f, 0:TP], a[:, f, 0:1], mod[:, shift + f, 0:1],
                                          ALU.mult, ALU.add)
                        chain.link(tt(smp(dst[:, f, TP:T]), smp(src[:, f, TP:T]), seqs(a[:, f, :]), ALU.mult))
                        last = tt(smp(dst[:, f, TP:T]), smp(dst[:, f, TP:T]), seqs(mod[:, shift + f, :]), ALU.add)
                    last.then_inc(h_ready, 1)

            dve.wait_ge(sums_done, 1)
            rsqrt(bank[0][:, 0:T], D, 1)
            chain.link(tt(xa[:], xa[:], v_rs[:].unsqueeze(1).broadcast_to([P, KT, T]), ALU.mult))
            dve.wait_ge(par_loaded, 48)
            with dve.Fori(0, ADA1_BLOCKS // 2) as it:
                save_mod(it * 2, it * 4)
                save_mod(it * 2 + 1, it * 4 + KT)
            dve.wait_ge(mod_ready, ADA1_BLOCKS + 1)
            scales(a1, SC1, C_G1)
            modulate(xa, xa, a1, SH1)
            for q in range(4):
                dve.wait_ge(hh_ready, q + 1)
                sl = slice(4 * q, 4 * q + 4)
                tt(hl[:, sl, :], xa[:, sl, :], hh[:, sl, :].bitcast(F32), ALU.subtract).then_inc(hl_ready, 1)
            for k in range(NSPL):
                split_lo(mix_unit(0, k))
            with dve.Fori(0, MIX_IT - 1) as it:
                for k in range(3, 15):
                    split_lo(mix_unit(it, k))
            for s in range(MIX_RING):
                for k in (2 * s + 3, 2 * s + 4):
                    split_lo(mix_then_gates(MIX_IT - 1, k))
                if s == 1:
                    dve.wait_ge(sums_done, 2)
                    rsqrt(bank[7][:, 0:T], W, 2)
                    for f in range(WT):
                        v = proj[:, 4 * WT + f, :]
                        dve.scalar_tensor_tensor(v, v, par[:, C_GV + f:C_GV + f + 1], v_rs[:], ALU.mult, ALU.mult)\
                            .then_inc(vn_ready, 1)
                if s >= 3:
                    u = 2 * (s - 3) + 1
                    n = TT[u // 2][1]
                    dve.wait_ge(vtr_done, u + 1)
                    dve.tensor_copy(vtok[0:n, u // 2, 512:1024], bank[7][0:n, :]).then_inc(vtok_d, 1)
            for h in range(WT):
                dve.wait_ge(mix_mm, h + 1)
                b = bank[4 + h % 4]
                u = proj[:, 5 * WT + h, :]
                tt(b[:, 0:TP].rearrange("p (n t) -> p n t", n=2), b[:, 0:TP].rearrange("p (n t) -> p n t", n=2),
                   bs[:, h, :].unsqueeze(1).broadcast_to([P, 2, P]), ALU.add)
                chain.link(tt(smp(b[:, TP:T]), smp(b[:, TP:T]), bs[:, h, 0:NL].unsqueeze(1).broadcast_to([P, NB, NL]),
                              ALU.add))
                tt(u, b[:, 0:T], u, ALU.mult).then_inc(yc_ready, 1)

            def gates_step(ot, unit):
                split_lo(unit(ot, 3))
                for k in range(4, 10):
                    split_lo(unit(ot, k))
                br0 = ot * GATE_HALVES + (MIX_HALVES + 6 + NSPL)
                dst = merged[:, ds(ot, 1), :].rearrange("p a t -> p (a t)")
                dve.wait_ge(sig_ready, ot * 3 + (3 + 3))
                dve.wait_ge(w_used, br0 + 1)
                tt(gt[:, 0, :], bank[3][:, 0:T], sig[:, 0, :], ALU.mult)
                split_lo(unit(ot, 10))
                dve.wait_ge(w_used, br0 + 2)
                chain.link(tt(gt[:, 1, :], bank[4][:, 0:T], sig[:, 1, :], ALU.mult))
                chain.link(tt(dst, gt[:, 0, :], gt[:, 1, :], ALU.add))
                split_lo(unit(ot, 11))
                save_mod(ot + ADA1_BLOCKS, ot * 4 + 2 * KT)
                dve.wait_ge(w_used, br0 + 3)
                chain.link(tt(gt[:, 0, :], bank[5][:, 0:T], sig[:, 2, :], ALU.mult))
                tt(dst, dst, gt[:, 0, :], ALU.add).then_inc(merged_ready, 1)

            with dve.Fori(0, KT - 1) as ot:
                chain.loop(ot, 3)
                gates_step(ot, gate_unit)
            chain.end(KT - 1)
            gates_step(KT - 1, gates_then_wo)
            for q in range(4):
                dve.wait_ge(mh_ready, q + 1)
                sl = slice(4 * q, 4 * q + 4)
                tt(ml[:, sl, :], merged[:, sl, :], mh[:, sl, :].bitcast(F32), ALU.subtract).then_inc(ml_ready, 1)

            def save_x1(v, s):
                o1 = ds(v * 3 + s, 1)
                gate1 = mod[:, ds(v * 3 + (GT1 + s), 1), :].rearrange("p a s -> p (a s)")
                dst = x1[:, o1, :].rearrange("p a t -> p (a t)")
                dve.wait_ge(w_used, v * 6 + (WO_BASE + 2 * s + 2 + NSPL))
                dve.scalar_tensor_tensor(dst[:, 0:TP], bank[s][:, 0:TP], gate1[:, 0:1], dst[:, 0:TP], ALU.mult, ALU.add)
                dve.wait_ge(x1_ready, v * 3 + (s + 3))
                chain.link(tt(smp(v_t[:, 0:TS]), smp(bank[s][:, TP:T]), seqs(gate1), ALU.mult))
                tt(dst[:, TP:T], dst[:, TP:T], v_t[:, 0:TS], ALU.add).then_inc(x1_ready, 1)

            dve.wait_ge(x1_loaded, 16)
            with dve.Fori(0, 4) as v:
                chain.loop(v, 3)
                for s in range(3):
                    for k in (2 * s + 3, 2 * s + 4):
                        split_lo(wo_unit(v, k))
                    save_x1(v, s)
            chain.end(4)
            for s in range(3):
                for k in (2 * s + 3, 2 * s + 4)[:1 if s == 2 else 2]:
                    split_lo(wo_unit(4, k))
                save_x1(4, s)
            save_x1(5, 0)

            dve.wait_ge(sums_done, 3)
            rsqrt(bank[0][:, 0:T], D, 3)
            scales(a2, SC2, C_G2)
            chain.link(tt(h2[:], x1[:], v_rs[:].unsqueeze(1).broadcast_to([P, KT, T]), ALU.mult))
            modulate(h2, h2, a2, SH2)
            for u in range(1, 12, 2):
                dve.wait_ge(htr_done, u + 1)
                n = TT[u // 4][1]
                dve.tensor_copy(htok[0:n, u // 4, 512 * (u % 4):512 * (u % 4) + 512], bank[3][0:n, :]).then_inc(htok_d, 1)

            dve.memset(ye[:], 0.0)
            dve.memset(sT[1][:], 0.0)
            chain.link(dve.memset(lg[:], 0.0))
            dve.wait_ge(logits_done, 1)
            for t_, (_, n) in enumerate(TT):
                last = tt(lg[0:n, t_, :], bank[1][0:n, 32 * t_:32 * t_ + 20], br[0:n, :], ALU.add)
            chain.link(last)

            def col(a, n=1):
                return sc[:, :, a:a + n]

            def wide(ap, n):
                return ap.broadcast_to([P, 3, n])

            def first_of(eq, one, taken):
                chain.link(dve.tensor_copy(col(one), col(eq)))
                chain.link(dve.tensor_copy(col(taken), col(eq)))
                for j in range(1, 4):
                    chain.link(tt(col(one + j), col(eq + j), col(taken), ALU.is_gt))
                    chain.link(tt(col(taken), col(taken), col(eq + j), ALU.max))

            def reduce(out, src, op):
                chain.link(dve.tensor_reduce(out, src, AX_X, op))

            def top_of(src, m, eq, one, taken):
                reduce(col(m), src, ALU.max)
                chain.link(tt(col(eq, 4), src, wide(col(m), 4), ALU.is_equal))
                first_of(eq, one, taken)

            G_MAX, EQ, OHG, TAKEN, SEL, M1, OH1, M2, OH2 = 0, 1, 5, 9, 10, 14, 15, 19, 20
            top_of(lg[:, :, 0:4], G_MAX, EQ, OHG, TAKEN)
            chain.link(tt(col(26, 4), lg[:, :, 0:4], wide(col(G_MAX), 4), ALU.subtract))
            by_group = mk[:].rearrange("p t (g j) -> p t g j", g=NG)

            def spread(dst, four):
                dve_ = dst.rearrange("p t (g j) -> p t g j", g=NG)
                return tt(dve_, col(OHG, 4).unsqueeze(3).broadcast_to([P, 3, NG, EPG]),
                          four.unsqueeze(2).broadcast_to([P, 3, NG, EPG]), ALU.mult)

            chain.link(tt(by_group, lg[:, :, 4:20].rearrange("p t (g j) -> p t g j", g=NG),
                          col(OHG, 4).unsqueeze(3).broadcast_to([P, 3, NG, EPG]), ALU.mult))
            reduce(col(SEL, 4), by_group.rearrange("p t g j -> p t j g"), ALU.add)
            top_of(col(SEL, 4), M1, EQ, OH1, TAKEN)
            chain.link(dve.scalar_tensor_tensor(col(SEL, 4), col(OH1, 4), -BIG, col(SEL, 4), ALU.mult, ALU.add))
            top_of(col(SEL, 4), M2, EQ, OH2, TAKEN)
            tt(col(30), col(M2), col(M1), ALU.subtract).then_inc(exp_in, 1)
            dve.wait_ge(exp_ready, 1)
            reduce(col(36), col(31, 4), ALU.add)
            chain.link(dve.tensor_scalar(col(37), col(35), 1.0, None, ALU.add))
            chain.link(tt(col(36), col(36), col(37), ALU.mult))
            chain.link(dve.reciprocal(col(36), col(36)))
            chain.link(tt(col(37), col(36), col(35), ALU.mult))
            chain.link(tt(col(EQ, 4), col(OH1, 4), wide(col(36), 4), ALU.mult))
            chain.link(tt(col(26, 4), col(OH2, 4), wide(col(37), 4), ALU.mult))
            chain.link(tt(col(EQ, 4), col(EQ, 4), col(26, 4), ALU.add))
            chain.link(tt(col(OH1, 4), col(OH1, 4), col(OH2, 4), ALU.add))
            chain.link(tt(col(OHG, 4), col(OHG, 4), valid[:].unsqueeze(2).broadcast_to([P, 3, 4]), ALU.mult))
            chain.link(spread(cb[:], col(EQ, 4)))
            spread(mk[:], col(OH1, 4)).then_inc(mk_ready, 1)
            dve.wait_ge(rank_done, 1)
            chain.link(dve.scalar_tensor_tensor(rk[:], bank[1][:, 0:3 * NE].rearrange("p (t e) -> p t e", e=NE), 1.0,
                                                mk[:], ALU.add, ALU.mult))
            chain.link(dve.tensor_scalar(rk[:], rk[:], -1.0, None, ALU.add))
            chain.link(dve.tensor_reduce(sc[:, 0, 0:1], bank[1][:, 64:64 + NE], AX_X, ALU.max))
            chain.link(dve.tensor_scalar(sc[:, 0, 1:6], iota[:, 0:5], float(CAP), None, ALU.mult))
            chain.link(tt(sc[:, 0, 1:6], sc[:, 0, 0:1].broadcast_to([P, 5]), sc[:, 0, 1:6], ALU.is_gt))
            chain.link(dve.tensor_reduce(sc[:, 0, 6:7], sc[:, 0, 1:6], AX_X, ALU.add))
            dve.tensor_copy(rnd[:, 0:1], sc[:, 0, 6:7]).then_inc(rounds_ready, 1)
            dve.memset(acc[:], 0.0).then_inc(zero_ready, 1)
            dve.wait_ge(zero_ready, 1)

            def save_scat(j, total):
                dve.wait_ge(scat_done, total + (j + 1))
                b = 4 + 2 * (j % 2)
                pair = acc[:].rearrange("p (h j) t -> p h j t", h=2)[:, :, j, :]
                for h in range(2):
                    last = tt(pair[:, h, :], bank[b + h][:, 0:T], pair[:, h, :], ALU.add)
                last.then_inc(acc_ready, 1)

            def experts(i, g):
                four = ds(g * EPG, EPG)
                dve.wait_ge(gath_done, i * 8 + 1)
                tt(oh[:].rearrange("p t (e c) -> p t e c", e=EPG),
                   iota[:].unsqueeze(1).unsqueeze(1).broadcast_to([P, 3, EPG, CAP]),
                   rk[:, :, four].unsqueeze(3).broadcast_to([P, 3, EPG, CAP]), ALU.is_equal).then_inc(oh_ready, 1)
                dve.wait_ge(oh_ready, i + 1)
                dve.wait_ge(st_done, i * EPG + 1)
                for c in range(2):
                    last = tt(gc[:, :, :, c, :], oh[:].rearrange("p t (e c) -> p t e c", e=EPG),
                              cb[:, :, four].unsqueeze(3).broadcast_to([P, 3, EPG, CAP]), ALU.mult)
                last.then_inc(gc_ready, 1)
                for q in range(4):
                    dve.wait_ge(gath_done, i * 8 + (2 * q + 2) + 1)
                    dve.tensor_copy(xg[:, 4 * q + 2:4 * q + 4, :],
                                    bank[5 if q % 2 == 0 else 7].rearrange("p (a n) -> p a n", a=2)).then_inc(xg_d, 1)
                for e in range(EPG):
                    m1 = i * EPG + (e + 1)
                    for j in range(8):
                        save_scat(j, i * (8 * EPG) + 8 * e)
                    dve.wait_ge(sg_ready, m1)
                    tt(hid[:], sg[:], bank[1].rearrange("p (f c) -> p f c", f=FT)[:, :, CAP:2 * CAP], ALU.mult)\
                        .then_inc(hid_ready, 1)
                    dve.wait_ge(moe_used, m1 * 12)
                    dve.tensor_copy(ye[:, 512:1024], bank[3][:]).then_inc(ye_d, 1)

            rounds = dve.value_load(rnd[0:1, 0:1], min_val=1, max_val=-(-T // CAP))
            with dve.Fori(0, rounds) as r:
                with dve.Fori(0, NG) as g:
                    experts(r * NG + g, g)
                dve.tensor_scalar(rk[:], rk[:], -float(CAP), None, ALU.add).then_inc(zero_ready, 1)
                dve.wait_ge(zero_ready, r + 2)
            for j in range(8):
                save_scat(j, rounds * (8 * NE))

            dve.wait_ge(acc_ready, rounds * (8 * NE) + 8 + 1)
            for q in range(4):
                for f in range(4 * q, 4 * q + 4):
                    dve.scalar_tensor_tensor(x1[:, f, 0:TP], acc[:, f, 0:TP], mod[:, GT2 + f, 0:1], x1[:, f, 0:TP],
                                             ALU.mult, ALU.add)
                    chain.link(tt(smp(acc[:, f, TP:T]), smp(acc[:, f, TP:T]), seqs(mod[:, GT2 + f, :]), ALU.mult))
                    last = tt(x1[:, f, TP:T], x1[:, f, TP:T], acc[:, f, TP:T], ALU.add)
                last.then_inc(h2_ready, 1)
            dve.wait_ge(sums_done, 4)
            rsqrt(bank[0][:, 0:T], D, 4)
            for f in range(KT):
                last = dve.scalar_tensor_tensor(h2[:, f, :], x1[:, f, :], par[:, C_GF + f:C_GF + f + 1], v_rs[:],
                                                ALU.mult, ALU.mult)
                if f % 4 == 3:
                    last.then_inc(y_ready, 1)

        @block.tensor
        def _(pe):
            pe.sem_inc(w_used, NSPL)
            for s in from_one["tensor"]:
                pe.sem_inc(s, 1)
            mm = pe.matmul

            def sums(src, n, b, q_of):
                for f in range(n):
                    if f % q_of == 0:
                        sums.quarter += 1
                        pe.wait_ge(sq_ready, sums.quarter)
                    last = mm(bank[b][:, 0:T], ones[:], src[:, f, :], start=f == 0, stop=f == n - 1)
                last.then_inc(sums_done, 1)

            sums.quarter = 0

            def ada_chunk(buf, j, loaded, value):
                pe.wait_ge(loaded, value)
                for q in range(4):
                    last = mm(bank[6][32 * q:32 * q + 32, :], cT[:, 4 * j + q, :], buf[:, q, :], start=j == 0,
                              stop=j == ADA_CHUNKS - 1, tile_position=(0, 32 * q))
                last.then_inc(ada_used, 1)

            def ada_select(n):
                pe.wait_ge(part_ready, n + 1 + 1)
                pe.wait_ge(mod_ready, n + 1)
                for c in range(4):
                    last = mm(bank[7][:, NSEQ * c:NSEQ * c + NSEQ], part[:, P * c:P * c + P], sel9[:], start=True, stop=True)
                last.then_inc(ada_sel, 1)

            pe.wait_ge(consts, 1)
            sums(sq1, KT, 0, 4)
            pe.wait_ge(c_loaded, 16)
            with pe.Fori(0, ADA1_BLOCKS // 2) as it:
                for b in range(2):
                    n = it * 2 + b
                    pe.wait_ge(part_ready, n + 1)
                    for j in range(ADA_CHUNKS):
                        ada_chunk(ring8[4 * b + j], j, slot_loaded[4 * b + j], it * 16 + 16)
                    ada_select(n)

            def half(unit, b, hi, lo, first, start, stop):
                _, _, _, u, s = unit
                pe.wait_ge(lo_ready, u + 1)
                for k in range(HALF):
                    out = bank[b][:, 0:T]
                    mm(out, wh[:, s, k, :], hi[:, first + k, :], start=start and k == 0, stop=False)
                    mm(out, wh[:, s, k, :], lo[:, first + k, :], start=False, stop=False)
                    last = mm(out, wl[:, s, k, :], hi[:, first + k, :], start=False, stop=stop and k == HALF - 1)
                last.then_inc(w_used, 1)

            def tile(unit_of, it, k, b, hi, lo):
                half(unit_of(it, k), b, hi, lo, 0, True, False)
                half(unit_of(it, k + 1), b, hi, lo, HALF, False, True)

            pe.wait_ge(hl_ready, 4)

            def mix_tile(it, s):
                pe.wait_ge(tile_saved, it * MIX_RING + (s + 1))
                tile(mix_unit, it, 2 * s, s, hh, hl)

            with pe.Fori(0, MIX_IT - 1) as it:
                for s in range(MIX_RING):
                    mix_tile(it, s)

            def vtr(u):
                tt, half_ = u // 2, u % 2
                c0, n = TT[tt]
                if tt >= 1:
                    pe.wait_ge(vtok_a if half_ == 0 else vtok_d, tt)
                for f in range(4):
                    last = mm(bank[6 + half_][0:n, P * f:P * f + P], proj[:, 4 * WT + 4 * half_ + f, c0:c0 + n],
                              ident[:], start=True, stop=True)
                last.then_inc(vtr_done, 1)

            for s in range(MIX_RING):
                mix_tile(MIX_IT - 1, s)
                if s == 0:
                    pe.wait_ge(masked, 1)
                    for f in range(WT):
                        g = f // 2
                        pe.wait_ge(d_ready, 2 * g + 2)
                        if f >= 2:
                            pe.wait_ge(yb_ready, f - 1)
                        for k in range(2):
                            last = mm(bank[6 + f % 2][:, 0:T], pw[:, g, k, f % 2, :], proj[:, 3 * WT + 2 * g + k, :],
                                      start=k == 0, stop=k == 1)
                        last.then_inc(pool_mm, 1)
                if s == 1:
                    pe.wait_ge(yb_ready, WT)
                    sums(vsq, WT, 7, WT)
                if s == 3:
                    pe.wait_ge(vn_ready, WT)
                if s >= 3:
                    vtr(2 * (s - 3))
                    vtr(2 * (s - 3) + 1)
            pe.wait_ge(vtok_a, 3)
            pe.wait_ge(vtok_d, 3)
            for h in range(WT):
                b = bank[4 + h % 4]
                if h >= 4:
                    pe.wait_ge(yc_ready, h - 3)
                elif h < 2:
                    pe.wait_ge(tile_saved, MIX_RING + MIX_TILES)
                for c in range(2):
                    mm(b[:, P * c:P * c + P], vtok[:, c, P * h:P * h + P], wst[:, h, :], start=True, stop=True)
                mm(b[:, TP:T], vtok[0:TS, 2, P * h:P * h + P], bd[:, h, :], start=True, stop=True).then_inc(mix_mm, 1)

            def branch(ot, n):
                pe.wait_ge([ya_ready, ybs_ready, ycs_ready][n], [1, 2 * WT, 2 * WT][n])
                hi0, lo0 = [(0, WT), (3 * WT, 2 * WT), (4 * WT, 5 * WT)][n]
                half(gate_unit(ot, 6 + n), 3 + n, ysp[:, hi0:hi0 + WT, :], ysp[:, lo0:lo0 + WT, :], 0, True, True)

            def gates_step(ot):
                for n in range(3):
                    pe.wait_ge(sig_ready, ot * 3 + (n + 1))
                    tile(gate_unit, ot, 2 * n, n, hh, hl)
                    if n == 0:
                        pe.wait_ge(part_ready, ot + ADA1_BLOCKS + 1)
                        for j in range(2):
                            ada_chunk(adaw[j], j, ada_loaded[j], ot * 32 + 16)
                for j in range(2, 4):
                    ada_chunk(adaw[j % 2], j, ada_loaded[j % 2], ot * 32 + 32)
                pe.wait_ge(merged_ready, ot + 1)
                for n in range(3):
                    branch(ot, n)
                    if n == 1:
                        ada_select(ot + ADA1_BLOCKS)

            pe.wait_ge(yc_ready, WT)
            with pe.Fori(0, KT) as ot:
                gates_step(ot)

            pe.wait_ge(ml_ready, 4)
            with pe.Fori(0, 5) as v:
                for s in range(3):
                    pe.wait_ge(x1_ready, v * 3 + (s + 1))
                    tile(wo_unit, v, 2 * s, s, mh, ml)
            pe.wait_ge(x1_ready, 16)
            tile(wo_unit, 5, 0, 0, mh, ml)

            pe.wait_ge(x1_ready, 19)
            sums(sq2, KT, 0, 4)
            pe.wait_ge(h_ready, 8)
            for t_, (c0, n) in enumerate(TT):
                for k in range(KT):
                    last = mm(bank[1][0:n, 32 * t_:32 * t_ + 20], h2[:, k, c0:c0 + n], wr[:, k, :], start=k == 0,
                              stop=k == KT - 1)
            last.then_inc(logits_done, 1)
            for u in range(12):
                c0, n = TT[u // 4]
                if u >= 2:
                    pe.wait_ge(htok_d if u % 2 else htok_a, u // 2)
                for f in range(4):
                    last = mm(bank[2 + u % 2][0:n, P * f:P * f + P], h2[:, 4 * (u % 4) + f, c0:c0 + n], ident[:],
                              start=True, stop=True)
                last.then_inc(htr_done, 1)
            pe.wait_ge(mk_ready, 1)
            for t_ in range(3):
                for s in range(t_ + 1):
                    mm(bank[1][:, NE * t_:NE * t_ + NE], tri[:] if s == t_ else ones[:], mk[:, s, :], start=s == 0,
                       stop=s == t_)
            for s in range(3):
                last = mm(bank[1][:, 64:64 + NE], ones[:], mk[:, s, :], start=s == 0, stop=s == 2)
            last.then_inc(rank_done, 1)

            def scatter(j, e_before, total):
                b = 4 + 2 * (j % 2)
                pe.wait_ge(acc_ready, total + max(j - 1, 0) + 1)
                for h in range(2):
                    rows = slice(64 * h, 64 * h + 64)
                    last = mm(bank[b + h][:, 0:T], ye[rows, P * j:P * j + P], sT[e_before % 2][rows, :], start=True,
                              stop=True, tile_position=(64 * h, 0))
                last.then_inc(scat_done, 1)

            def experts(i):
                pe.wait_ge(oh_ready, i + 1)
                pe.wait_ge(acc_ready, i * (8 * EPG) + 1)
                for dp in range(8):
                    b = [4, 5, 6, 7][dp % 4]
                    if dp >= 4:
                        pe.wait_ge(xg_d if dp % 2 else xg_a, i * 4 + (dp // 2 - 1))
                    for d in range(2):
                        for t_, (_, n) in enumerate(TT):
                            last = mm(bank[b][:, 256 * d:256 * d + 256],
                                      htok[0:n, t_, P * (2 * dp + d):P * (2 * dp + d) + P], oh[0:n, t_, :],
                                      start=t_ == 0, stop=t_ == 2)
                    last.then_inc(gath_done, 1)
                pe.wait_ge(xg_a, i * 4 + 4)
                pe.wait_ge(xg_d, i * 4 + 4)
                for e in range(EPG):
                    m = i * EPG + e
                    slots = slice(CAP * e, CAP * e + CAP)
                    pe.wait_ge(st_ready, m + 1)
                    if e == 0:
                        pe.wait_ge(gc_ready, i + 1)
                    for c in range(4):
                        pe.wait_ge(slot_loaded[(2 * c + 3) % 12], m * 16 + (16 + slot_uses((2 * c + 3) % 12)))
                        pe.wait_ge(slot_loaded[(2 * c + 4) % 12], m * 16 + (16 + slot_uses((2 * c + 4) % 12)))
                        gate, up = ring8[(2 * c + 3) % 12], ring8[(2 * c + 4) % 12]
                        for k in range(4):
                            kt = 4 * c + k
                            a = mm(bank[0][0:CAP, :], xg[:, kt, slots], gate[:, k, :], start=kt == 0, stop=kt == KT - 1,
                                   tile_position=(0, 0))
                            b = mm(bank[0][CAP:2 * CAP, :], xg[:, kt, slots], up[:, k, :], start=kt == 0,
                                   stop=kt == KT - 1, tile_position=(0, CAP))
                        a.then_inc(moe_used, 1)
                        b.then_inc(moe_used, 1)
                        if c == 0:
                            pe.wait_ge(ye_a, m + 1)
                            pe.wait_ge(ye_d, m + 1)
                        for j in (2 * c, 2 * c + 1):
                            scatter(j, e + 1, m * 8)
                    pe.wait_ge(gu_saved, m + 1)
                    for t_, (c0, n) in enumerate(TT):
                        last = mm(bank[0][:, c0:c0 + n], gc[0:n, t_, e].rearrange("p d c -> p (d c)"), ident[0:n, 0:n],
                                  start=True, stop=True)
                    last.then_inc(st_done, 1)
                    for f in range(FT):
                        last = mm(bank[1][:, P * f:P * f + P], gus[:, P * f:P * f + P], ident[:], start=True, stop=True)
                    last.then_inc(tr_done, 1)
                    pe.wait_ge(hid_ready, m + 1 + 1)
                    for c in range(FT):
                        k = (c + 11) % 12
                        pe.wait_ge(slot_loaded[k], m * 16 + (16 + slot_uses(k)))
                        for b in range(2):
                            for h in range(2):
                                last = mm(bank[2 + b][CAP * h:CAP * h + CAP, :], hid[:, c, :],
                                          dring[k][:, 1024 * h + 512 * b:1024 * h + 512 * b + 512], start=c == 0,
                                          stop=c == FT - 1, tile_position=(0, CAP * h))
                        last.then_inc(moe_used, 1)

            pe.wait_ge(htok_a, 6)
            pe.wait_ge(htok_d, 6)
            pe.wait_ge(rounds_ready, 1)
            rounds = pe.value_load(rnd[0:1, 0:1], min_val=1, max_val=-(-T // CAP))
            pe.wait_ge(zero_ready, 1)
            with pe.Fori(0, rounds) as r:
                with pe.Fori(0, NG) as g:
                    experts(r * NG + g)
            pe.wait_ge(ye_a, rounds * NE + 1)
            pe.wait_ge(ye_d, rounds * NE + 1)
            for j in range(8):
                scatter(j, NE - 1, rounds * (8 * NE))
            sums(sq2, KT, 0, 4)


def kernel(x_prompt, x_sample, c_prompt, c_sample, state_conv, state_pool, w_ada, b_ada, g_norm1, w_in,
           conv_w, pool_w, pool_scale, g_v, w_s, b_s, w_br, w_o, g_norm2, w_rg, b_rg, w_re, b_re,
           w_gate, w_up, w_down, g_final):
    import numpy as np
    import concourse.bacc as bacc
    from concourse.bass_utils import run_bass_kernel_spmd

    (x_prompt, x_sample, c_prompt, c_sample, state_conv, state_pool, w_ada, b_ada, g_norm1, w_in, conv_w, pool_w,
     pool_scale, g_v, w_s, b_s, w_br, w_o, g_norm2, w_rg, b_rg, w_re, b_re, w_gate, w_up, w_down, g_final) = (
        np.asarray(a) for a in (
            x_prompt, x_sample, c_prompt, c_sample, state_conv, state_pool, w_ada, b_ada, g_norm1, w_in, conv_w, pool_w,
            pool_scale, g_v, w_s, b_s, w_br, w_o, g_norm2, w_rg, b_rg, w_re, b_re, w_gate, w_up, w_down, g_final))

    def tiles(a):
        return a.reshape(-1, P, *a.shape[1:]).swapaxes(0, 1)

    x = np.concatenate([x_prompt.reshape(TP, D), x_sample.reshape(TS, D)]).T
    c = np.pad(np.concatenate([c_prompt, c_sample]).T, ((0, 0), (0, 32 - NSEQ)))
    conv = np.pad(tiles(state_conv[0].transpose(2, 0, 1)), ((0, 0), (0, 0), (0, 0), (0, NL)))
    pool = np.pad(tiles(state_pool[0].transpose(2, 0, 1)), ((0, 0), (0, 0), (0, 0), (1, NL))).swapaxes(0, 1)
    params = np.concatenate(
        [tiles(v[0]) for v in (b_ada, g_norm1, g_norm2)] + [tiles(g_final)] + [tiles(v[0]) for v in (g_v, pool_scale)]
        + [tiles(conv_w[0].T).reshape(P, -1)], axis=1)
    inv = np.array([[1.0 / min(t + 1, 2 << g) for t in range(16)] for g in range(NPAR)], np.float32)
    inv = np.broadcast_to(inv, (P, NPAR, 16))
    w_t = w_in[0].reshape(KT, P, -1, P).transpose(2, 1, 0, 3)
    bg, cg, hc, pl, u, v = (w_t[WT * k:WT * k + WT] for k in range(6))
    w_mix = np.concatenate([cg, hc, bg, pl, v, u])
    w_gt = w_t[MIX_TILES:].reshape(3, KT, P, KT, P).swapaxes(0, 1).reshape(3 * KT, P, KT, P)
    w_brt = w_br[0].reshape(3 * WT, P, KT, P).transpose(2, 1, 0, 3)
    w_ot = w_o[0].reshape(KT, P, KT, P).transpose(2, 1, 0, 3)
    pw = pool_w[0].reshape(NPAR, 2, P, 2, P).transpose(2, 0, 1, 3, 4)
    arrays = {
        "x": tiles(x), "c": tiles(c), "conv": conv, "pool": pool, "params": params, "inv": inv, "w_ada": w_ada[0],
        "w_mix": w_mix, "w_gt": w_gt, "w_br": w_brt, "w_o": w_ot, "pool_w": pw, "w_s": w_s[0].transpose(2, 0, 1),
        "b_s": b_s[0], "w_r": tiles(np.concatenate([w_rg[0], w_re[0]], axis=1)),
        "b_r": np.concatenate([b_rg[0], b_re[0]]), "w_gate": w_gate[0], "w_up": w_up[0], "w_down": w_down[0],
    }
    arrays = {f"in_{k}": np.ascontiguousarray(a) for k, a in arrays.items()}
    outs = {"y": (P, KT, T), "conv_state": (P, WT, 1 + NB, 2), "pool_state": (WT, P, (1 + NB) * PST), "v": (P, WT, TS)}

    nc = bacc.Bacc("TRN2", target_bir_lowering=False, num_devices=1)
    args = [nc.dram_tensor(k, a.shape, mybir.dt.from_np(a.dtype), kind="ExternalInput").ap() for k, a in arrays.items()]
    args += [nc.dram_tensor(f"out_{k}", s, F32, kind="ExternalOutput").ap() for k, s in outs.items()]
    build(nc, *args)
    got = run_bass_kernel_spmd(nc, [arrays], core_ids=[0]).results[0]

    y = got["out_y"].transpose(2, 1, 0).reshape(T, D)
    conv = got["out_conv_state"].transpose(2, 3, 1, 0).reshape(1 + NB, 2, W)
    pool = got["out_pool_state"].reshape(WT, P, 1 + NB, PST).transpose(2, 3, 0, 1).reshape(1 + NB, PST, W)
    v = got["out_v"].transpose(2, 1, 0).reshape(1, NB, NL, W)
    return (y[:TP].reshape(1, TP, D), y[TP:].reshape(NB, NL, D), conv[:1][None], pool[:1][None], conv[1:][None],
            pool[1:][None], v)
```

```python
from contextlib import ExitStack

import concourse.bass as bass
from concourse import mybir
from concourse.bass import ds

F32 = mybir.dt.float32
F32R = mybir.dt.float32r
I32 = mybir.dt.int32
ALU = mybir.AluOpType
ACT = mybir.ActivationFunctionType
AX_X = mybir.AxisListType.X

P = 128
D = 2048
KT = D // P
TP = 256
NB, NL = 8, 4
TS = NB * NL
T = TP + TS
TT = [(0, P), (P, P), (TP, TS)]
NSEQ = 1 + NB
W = D // 2
WT = W // P
NPAR = 4
PST = 15
HALF = 8
NSPL = 3
NE, EPG, NG = 16, 4, 4
NR = NG + NE
FF = D // 4
FT = FF // P
CAP = 64
TLO_A = 1280
EPS = 1e-6
BIG = 3.0e38

KB = 1024
SQ_BEFORE = 5
ADA1_BLOCKS = 8
ADA_CHUNKS = 4
MIX_TILES = 48
MIX_RING = 6
MIX_IT = MIX_TILES // MIX_RING
MIX_HALVES = 2 * MIX_TILES
GATE_HALVES = 9
WO_BASE = MIX_HALVES + KT * GATE_HALVES
WO_HALVES = 2 * KT
ALL_HALVES = WO_BASE + WO_HALVES

C_BADA, C_G1, C_G2, C_GF, C_GV, C_PS, C_CW = 0, 96, 112, 128, 144, 152, 160
N_PAR = 184
SH1, SC1, GT1, SH2, SC2, GT2 = (KT * i for i in range(6))


class Tally:

    def __init__(self, eng, sem):
        self.eng, self.sem, self.n, self.at = eng, sem, 0, None

    def loop(self, reg, per):
        self.at, self.reg, self.per, self.k = self.n, reg, per, 0

    def end(self, count):
        assert self.k == self.per, (self.k, self.per)
        self.n, self.at = self.at + self.per * count, None

    def link(self, ins):
        ins.then_inc(self.sem, 1)
        self.after()

    def after(self):
        if self.at is None:
            self.n += 1
            self.eng.wait_ge(self.sem, self.n)
        else:
            self.k += 1
            self.eng.wait_ge(self.sem, self.reg * self.per + (self.at + self.k))


def build(nc, x_in, c_in, conv_in, pool_in, par_in, inv_in, w_ada, w_mix, w_gt, w_br, w_o, pool_w, w_s, b_s,
          w_r, b_r, w_gate, w_up, w_down, y_out, conv_out, pool_out, v_out):
    ctx = ExitStack()
    with ctx:
        base = (nc.sbuf_base + 31) // 32 * 32

        def at(name, off, shape, dt=F32):
            return nc.alloc_sbuf_tensor_at(name, shape, dt, offset=base + off)

        def size(shape):
            n = 4
            for s in shape[1:]:
                n *= s
            return n

        def region(off, end, *parts):
            out = []
            for name, shape, dt in parts:
                out.append(at(name, off, shape, dt))
                off += (size(shape) + 31) // 32 * 32
            assert off <= end, (parts[0][0], off, end)
            return out

        UNITS = [(t_, q) for q in range(4) for t_ in range(3)]

        o_m = 52 * KB
        o_s = o_m + KT * T * 4
        o_h = o_s + 2 * NSPL * HALF * P * 4 + 2 * KB
        o_y = o_h + 2 * KT * T * 4
        o_p = o_y + 3 * KT * T * 4
        o_end = 229344 - base

        ring8 = [at(f"ring{k}", 8 * KB * k, [P, 4, 512]) for k in range(12)]
        mixw = [at(f"mixw{k}", 8 * KB * k, [P, KT, P]) for k in range(MIX_RING)]
        brw = at("brw", 24 * KB, [P, 3 * WT, P])
        adaw = [at(f"adaw{k}", (36 + 8 * k) * KB, [P, 4, 512]) for k in range(2)]
        dring = [at(f"dring{k}", 8 * KB * k, [P, D]) for k in range(12)]

        wst, = region(48 * KB, 52 * KB, ("wst", [P, WT, P], F32))
        merged, = region(o_m, o_s, ("merged", [P, KT, T], F32))
        o_x = o_m
        zzs, cst, ctmp, pp, pa, pb_, pps0, pps1, pst0, pst1 = region(
            o_x, o_x + 3 * 4 * KB,
            ("zzs", [P, WT, NB, 6], F32), ("cst", [P, WT, 1 + NB, 2], F32), ("ctmp", [P, T], F32), ("pp", [P, 16 + TP], F32),
            ("pa", [P, 16 + TP + NB * 20], F32), ("pb_", [P, 16 + TP + NB * 20], F32),
            ("pps0", [P, NB, 20], F32), ("pps1", [P, NB, 20], F32),
            ("pst0", [P, (1 + NB) * PST], F32), ("pst1", [P, (1 + NB) * PST], F32))
        pps, pst = [pps0, pps1], [pst0, pst1]
        vsq, = region(o_x, o_x + 12 * KB, ("vsq", [P, WT, T], F32))
        vtok, = region(o_x, o_x + 12 * KB, ("vtok", [P, 3, W], F32))
        bd, bs = region(o_x + 12 * KB, o_s, ("bd", [TS, WT, TS], F32), ("bs", [P, WT, P], F32))
        wh, wl = region(o_s, o_h, ("wh", [P, NSPL, HALF, P], F32R), ("wl", [P, NSPL, HALF, P], F32R))
        hh, hl = region(o_h, o_y, ("hh", [P, KT, T], F32R), ("hl", [P, KT, T], F32R))
        mh, ml = region(o_h, o_y, ("mh", [P, KT, T], F32R), ("ml", [P, KT, T], F32R))
        proj, = region(o_y, o_p, ("proj", [P, MIX_TILES, T], F32))
        ysp, = region(o_y, o_p, ("ysp", [P, MIX_TILES, T], F32R))
        xa, sq1 = region(o_y, o_p, ("xa", [P, KT, T], F32), ("sq1", [P, KT, T], F32))
        x1, = region(o_y, o_p, ("x1", [P, KT, T], F32))
        h2, = region(o_y + 2 * KT * T * 4, o_p, ("h2", [P, KT, T], F32))
        thi, ye, sT0, sT1, tlo_a = region(
            o_h, o_y, ("thi", [P, 3, D], F32R), ("ye", [P, D // 2], F32), ("sT0", [P, T], F32), ("sT1", [P, T], F32),
            ("tlo_a", [P, TLO_A], F32R))
        sq4, = region(o_h, o_y, ("sq4", [P, KT, T], F32))
        tlo, gus = region(o_y + KT * T * 4, o_y + 2 * KT * T * 4, ("tlo", [P, 2, D], F32R), ("gus", [P, FF], F32))
        xg, hid, sg = region(o_y + 2 * KT * T * 4, o_p, ("xg", [P, KT, EPG * CAP], F32), ("hid", [P, FT, CAP], F32),
                             ("sg", [P, FT, CAP], F32))
        sT = [sT0, sT1]
        lasting = (
            ("wr", [P, KT, 32], F32), ("mod", [P, 6 * KT, NSEQ], F32), ("par", [P, N_PAR], F32), ("ident", [P, P], F32),
            ("ones", [P, P], F32), ("tri", [P, P], F32), ("iota", [P, CAP], F32), ("sel", [P, NR], F32),
            ("w4", [P, 4], F32), ("br", [P, NR], F32), ("valid", [P, 3], F32), ("lg", [P, 3, NR], F32),
            ("mk", [P, 3, NE], F32), ("cb", [P, 3, NE], F32), ("rk", [P, 3, NE + EPG], F32),
            ("sc", [P, 3, 40], F32), ("rnd", [P, 8], I32))
        wr, mod, par, ident, ones, tri, iota, sel, w4, br, valid, lg, mk, cb, rk, sc, rnd = region(o_p, o_end, *lasting)
        scaled, = region(o_p, o_p + size([P, KT, 32]), ("scaled", [P, 2, 2, TS], F32))
        o_q = o_p + sum((size(shape) + 31) // 32 * 32 for _, shape, _ in lasting)
        cT, part = region(o_q, o_end, ("cT", [P, KT, 32], F32), ("part", [P, 512], F32))
        o_q2 = o_q + 4 * KB
        a1, a2, v_var, v_rs, v_t = region(
            o_q2, o_end, ("a1", [P, KT, NSEQ], F32), ("a2", [P, KT, NSEQ], F32), ("v_var", [P, T], F32),
            ("v_rs", [P, T], F32), ("v_t", [P, T], F32))
        sig, gt = region(o_q2, o_end, ("sig", [P, 3, T], F32), ("gt", [P, 2, T], F32))
        pw, inv = region(o_q2, o_end, ("pw", [P, NPAR, 2, 2, P], F32), ("inv", [P, NPAR, 16], F32))
        sqs, sqt, lgp = region(o_q, o_q2, ("sqs", [P, T], F32), ("sqt", [P, T], F32), ("lgp", [P, T], F32))
        oh, gc, tlo_b = region(o_q, o_end, ("oh", [P, 3, EPG * CAP], F32R), ("gc", [P, 3, EPG, CAP], F32),
                               ("tlo_b", [P, D - TLO_A], F32R))

        def rest_rows(t_, f0, n):
            if t_ < 2:
                return tlo[:, t_, f0:f0 + n]
            return tlo_a[0:TS, f0:f0 + n] if f0 < TLO_A else tlo_b[0:TS, f0 - TLO_A:f0 - TLO_A + n]

        print('FREE', o_end - o_q)
        bank = [ctx.enter_context(nc.psum_tensor(f"bank{k}", [P, 512], F32)) for k in range(8)]

        def sem(name):
            return ctx.enter_context(nc.semaphore(name))

        x_loaded, c_loaded, par_loaded, mixpar_loaded, x1_loaded = (
            sem(n) for n in ("x_loaded", "c_loaded", "par_loaded", "mixpar_loaded", "x1_loaded"))
        slot_loaded = [sem(f"slot_loaded{k}") for k in range(12)]
        mix_loaded = [sem(f"mix_loaded{k}") for k in range(MIX_RING)]
        br_loaded = sem("br_loaded")
        ada_loaded = [sem("ada_loaded0"), sem("ada_loaded1")]
        pps_loaded = [sem("pps_loaded0"), sem("pps_loaded1")]
        stores = sem("stores")
        pst_stored = [sem("pst_stored0"), sem("pst_stored1")]
        v_stored, conv_stored = sem("v_stored"), sem("conv_stored")
        w_used = sem("w_used")
        ada_used = sem("ada_used")
        ada_sel = sem("ada_sel")
        sums_done, pool_mm, vtr_done, mix_mm = (sem(n) for n in ("sums_done", "pool_mm", "vtr_done", "mix_mm"))
        logit_sums, logits_done, htr_done, rank_done = (sem(n) for n in ("logit_sums", "logits_done", "htr_done", "rank_done"))
        gath_done, tr_done, st_done, scat_done, moe_used = (
            sem(n) for n in ("gath_done", "tr_done", "st_done", "scat_done", "moe_used"))
        sq_ready, std_ready, part_ready, hh_ready, hi_ready = (
            sem(n) for n in ("sq_ready", "std_ready", "part_ready", "hh_ready", "hi_ready"))
        hp_ready = sem("hp_ready")
        tile_saved = sem("tile_saved")
        yb_ready, vtok_a, sig_ready, mh_ready, thi_ready, exp_ready, lgp_ready = (
            sem(n) for n in ("yb_ready", "vtok_a", "sig_ready", "mh_ready", "thi_ready", "exp_ready", "lgp_ready"))
        xg_a, gu_saved, sg_ready, st_ready, ye_a = (
            sem(n) for n in ("xg_a", "gu_saved", "sg_ready", "st_ready", "ye_a"))
        dch, var_ready, mod_ready, h_ready, hl_ready, lo_ready, rs_ready = (
            sem(n) for n in ("dch", "var_ready", "mod_ready", "h_ready", "hl_ready", "lo_ready", "rs_ready"))
        vn_ready, vtok_d, yc_ready, merged_ready, ml_ready, x1_ready, tlo_ready = (
            sem(n) for n in ("vn_ready", "vtok_d", "yc_ready", "merged_ready", "ml_ready", "x1_ready", "tlo_ready"))
        exp_in, mk_ready, rounds_ready, oh_ready, gc_ready, xg_d, hid_ready, ye_d, acc_ready, round_ready, y_ready = (
            sem(n) for n in ("exp_in", "mk_ready", "rounds_ready", "oh_ready", "gc_ready", "xg_d", "hid_ready",
                             "ye_d", "acc_ready", "round_ready", "y_ready"))
        pch, consts, masked, ya_ready, d_ready, ybs_ready, ycs_ready, sqs_ready, hs_ready, tlp_ready, yp_ready = (
            sem(n) for n in ("pch", "consts", "masked", "ya_ready", "d_ready", "ybs_ready", "ycs_ready", "sqs_ready",
                             "hs_ready", "tlp_ready", "yp_ready"))

        def mix_unit(it, k):
            if k >= 2 * MIX_RING:
                it, k = it + 1, k - 2 * MIX_RING
            s, h = k // 2, k % 2
            return (mixw[s][:, HALF * h:HALF * (h + 1), :], mix_loaded[s], it * 16 + 16, it * (2 * MIX_RING) + k, k % NSPL)

        def gate_unit(ot, k):
            if k >= GATE_HALVES:
                ot, k = ot + 1, k - GATE_HALVES
            u = ot * GATE_HALVES + (MIX_HALVES + k)
            if k < 6:
                return (mixw[k // 2][:, HALF * (k % 2):HALF * (k % 2 + 1), :], mix_loaded[k // 2],
                        ot * 16 + 16 * (MIX_IT + 1), u, k % NSPL)
            return brw[:, HALF * (k - 6):HALF * (k - 5), :], br_loaded, ot * 16 + 16, u, k % NSPL

        def wo_unit(v, k):
            if k >= 6:
                v, k = v + 1, k - 6
            s, h = k // 2, k % 2
            return (mixw[s][:, HALF * h:HALF * (h + 1), :], mix_loaded[s], v * 16 + 16 * (MIX_IT + KT + 1),
                    v * 6 + (WO_BASE + k), k % NSPL)

        def mix_then_gates(it, k):
            return mix_unit(it, k) if it < MIX_IT - 1 or k < 2 * MIX_RING else gate_unit(0, k - 2 * MIX_RING)

        def gates_then_wo(ot, k):
            return gate_unit(ot, k) if ot < KT - 1 or k < GATE_HALVES else wo_unit(0, k - GATE_HALVES)

        from_one = {"tensor": (ada_sel, tr_done, gath_done, st_done), "scalar": (part_ready, st_ready, ye_a), "vector": (mod_ready, merged_ready, hid_ready, acc_ready, ye_d)}

        def slot_uses(k):
            return 16 * (ADA1_BLOCKS // 2) if k < 8 else 0

        block = ctx.enter_context(nc.Block())

        @block.sync
        def _(sp):
            sp.dma_start(xa[:], x_in).then_inc(x_loaded, 16)
            sp.dma_start(cT[:], c_in).then_inc(c_loaded, 16)
            sp.dma_start(par[:], par_in).then_inc(par_loaded, 16)
            sp.dma_start(wr[:], w_r).then_inc(par_loaded, 16)
            sp.dma_start(br[:], b_r.partition_broadcast(P)).then_inc(par_loaded, 16)

            def ada_src(blk, j):
                return w_ada.rearrange("(k p) n -> p k n", p=P)[:, 4 * j:4 * j + 4, blk]

            for k in range(8):
                sp.dma_start(ring8[k][:], ada_src(slice(KT * P * (k // 4), KT * P * (k // 4) + 512), k % 4))\
                    .then_inc(slot_loaded[k], 16)
            with sp.Fori(0, 3) as it:
                for k in range(8):
                    sp.wait_ge(ada_used, it * 8 + (k + 1))
                    sp.dma_start(ring8[k][:], ada_src(ds(it * 512 + (512 + KT * P * (k // 4)), 512), k % 4))\
                        .then_inc(slot_loaded[k], 16)

            for k in range(MIX_RING):
                sp.wait_ge(ada_used, 24 + k + 1)
                sp.dma_start(mixw[k][:], w_mix[k]).then_inc(mix_loaded[k], 16)
            sp.wait_ge(ada_used, 32)
            sp.dma_start(wst[:], w_s).then_inc(mixpar_loaded, 16)
            sp.dma_start(bs[:], b_s.partition_broadcast(P)).then_inc(mixpar_loaded, 16)
            sp.dma_start(zzs[:], conv_in).then_inc(mixpar_loaded, 16)
            sp.wait_ge(h_ready, 4)
            sp.wait_ge(hp_ready, 4)
            sp.dma_start(pw[:], pool_w).then_inc(mixpar_loaded, 16)
            sp.dma_start(inv[:], inv_in).then_inc(mixpar_loaded, 16)
            sp.wait_ge(consts, 1)
            for b in range(NB):
                sp.dma_start(bd[NL * b:NL * b + NL, :, NL * b:NL * b + NL], w_s[0:NL, :, 0:NL])\
                    .then_inc(mixpar_loaded, 16)
            with sp.Fori(1, MIX_IT) as it:
                for k in range(MIX_RING):
                    sp.wait_ge(lo_ready, it * 12 + (2 * k + 2 - 12))
                    sp.dma_start(mixw[k][:], w_mix[ds(it * MIX_RING + k, 1)].rearrange("a p k c -> p (a k) c"))\
                        .then_inc(mix_loaded[k], 16)

            def gate_load(ot, n, at_value):
                sp.wait_ge(lo_ready, at_value)
                sp.dma_start(mixw[n][:], w_gt[ds(ot * 3 + n, 1)].rearrange("a p k c -> p (a k) c"))\
                    .then_inc(mix_loaded[n], 16)

            def br_load(ot):
                sp.wait_ge(lo_ready, ot * GATE_HALVES + MIX_HALVES)
                sp.dma_start(brw[:], w_br[ds(ot, 1)].rearrange("a p k c -> p (a k) c")).then_inc(br_loaded, 16)

            def ada_load(ot, j):
                sp.wait_ge(ada_used, ot * 4 + (32 + j - 1))
                sp.dma_start(adaw[j % 2][:], ada_src(ds(ot * 512 + ADA1_BLOCKS * 512, 512), j))\
                    .then_inc(ada_loaded[j % 2], 16)

            for n in range(3):
                gate_load(0, n, 2 * (MIX_TILES - MIX_RING + n) + 2)
            br_load(0)
            sp.wait_ge(mix_mm, WT)
            ada_load(0, 0)
            ada_load(0, 1)
            with sp.Fori(0, KT - 1) as ot:
                ada_load(ot, 2)
                ada_load(ot, 3)
                for n in range(3):
                    gate_load(ot + 1, n, ot * GATE_HALVES + (MIX_HALVES + 2 * n + 2))
                ada_load(ot + 1, 0)
                ada_load(ot + 1, 1)
                br_load(ot + 1)
            ada_load(KT - 1, 2)
            ada_load(KT - 1, 3)

            def wo_load(v, s):
                sp.wait_ge(lo_ready, v * 6 + (WO_BASE + 2 * s + 2 - 6))
                sp.dma_start(mixw[s][:], w_o[ds(v * 3 + s, 1)].rearrange("a p k c -> p (a k) c"))\
                    .then_inc(mix_loaded[s], 16)

            for s in range(3):
                sp.wait_ge(lo_ready, WO_BASE - GATE_HALVES + 2 * s + 2)
                sp.dma_start(mixw[s][:], w_o[s]).then_inc(mix_loaded[s], 16)

            def expert_load(n, c):
                k = (c + 3) % 12
                e = ds(n, 1)
                if c < 8:
                    src = (w_up if c % 2 else w_gate)[e].rearrange("a (k p) n -> p (a k) n", p=P)
                    sp.dma_start(ring8[k][:], src[:, 4 * (c // 2):4 * (c // 2) + 4, :]).then_inc(slot_loaded[k], 16)
                else:
                    src = w_down[e].rearrange("a (k p) n -> p (a k) n", p=P)
                    sp.dma_start(dring[k][:], src[:, c - 8, :]).then_inc(slot_loaded[k], 16)

            sp.wait_ge(lo_ready, WO_BASE)
            sp.wait_ge(ada_used, 32 + 4 * KT)
            for c in range(3):
                expert_load(0, c)
            sp.wait_ge(merged_ready, KT + 1)
            sp.dma_start(x1[:], x_in).then_inc(x1_loaded, 16)
            sp.wait_ge(ml_ready, 4)
            for c in (3, 4):
                expert_load(0, c)
            with sp.Fori(1, 5) as v:
                for s in range(3):
                    wo_load(v, s)
            wo_load(5, 0)
            sp.wait_ge(lo_ready, ALL_HALVES)
            sp.wait_ge(w_used, ALL_HALVES + NSPL)
            for c in range(5, 12):
                expert_load(0, c)
            with sp.Fori(1, NE) as n:
                for c in range(12):
                    sp.wait_ge(moe_used, n * 12 + (c + 1 - 12))
                    expert_load(n, c)
            sp.wait_ge(rounds_ready, 1)
            rounds = sp.value_load(rnd[0:1, 0:1], min_val=1, max_val=-(-T // CAP))
            with sp.If(rounds > 1):
                with sp.Fori(1, rounds) as r:
                    with sp.Fori(0, NE) as n:
                        for c in range(12):
                            sp.wait_ge(moe_used, r * (12 * NE) + n * 12 + (c + 1 - 12))
                            expert_load(n, c)
            for q in range(4):
                sp.wait_ge(y_ready, q + 1)
                sp.wait_ge(yp_ready, q + 1)
                sp.dma_start(y_out[:, 4 * q:4 * q + 4, :], h2[:, 4 * q:4 * q + 4, :]).then_inc(stores, 16)
            sp.wait_ge(stores, 16 * 4)
            sp.wait_ge(conv_stored, 16)
            sp.wait_ge(v_stored, 16)
            for k in range(2):
                sp.wait_ge(pst_stored[k], 16 * WT // 2)

        @block.gpsimd
        def _(gp):
            chain = Tally(gp, pch)

            def select(m, pattern, base_, mult, op, fill):
                return gp.affine_select(out=m, in_=m, compare_op=op, fill=fill, base=base_, pattern=pattern,
                                        channel_multiplier=mult)

            gp.memset(bd[:], 0.0)
            gp.memset(ident[:], 0.0)
            gp.memset(sel[:], 0.0)
            gp.memset(tri[:], 1.0)
            gp.memset(valid[:], 1.0)
            chain.link(gp.memset(ones[:], 1.0))
            select(ident[:], [[-1, P]], 0, 1, ALU.not_equal, 1.0)
            for q in range(4):
                chain.link(select(sel[:], [[-1, NR]], -32 * q, 1, ALU.not_equal, 1.0))
            select(tri[:], [[1, P]], 0, -1, ALU.is_gt, 0.0)
            select(valid[:, 2:3], [[0, 1]], TS, -1, ALU.is_gt, 0.0)
            gp.iota(w4[:], [[-1, 4]], base=4, channel_multiplier=0, allow_small_or_imprecise_dtypes=True)
            gp.iota(iota[:], [[1, CAP]], base=0, channel_multiplier=0,
                    allow_small_or_imprecise_dtypes=True).then_inc(consts, 1)

            gp.wait_ge(mixpar_loaded, 16 * (5 + NB))
            select(wst[:], [[0, WT], [1, P]], 0, -1, ALU.is_ge, 0.0)
            select(bd[:], [[0, WT], [1, TS]], 0, -1, ALU.is_ge, 0.0).then_inc(masked, 1)

            def smp(ap):
                return ap[:, TP:T].rearrange("p (b l) -> p b l", l=NL)

            for f in range(2):
                gp.dma_start(pps[f][:], pool_in[f]).then_inc(pps_loaded[f], 16)
            chain.link(gp.memset(pp[:, 0:16], 0.0))
            NPP = 16 + TP
            for f in range(WT):
                cg, hc, bg, p_t = (proj[:, 4 * f + k, :] for k in range(4))
                zs = zzs[:, f]
                cw = [par[:, C_CW + 3 * f + k:C_CW + 3 * f + k + 1] for k in range(3)]
                gp.wait_ge(tile_saved, MIX_RING + 4 * f + 3)
                chain.link(gp.tensor_tensor(cg, cg, hc, ALU.mult))
                chain.link(gp.tensor_copy(zs[:, :, 2:6], smp(cg)))
                gp.tensor_copy(cst[:, f, 0, :], cg[:, TP - 2:TP])
                gp.tensor_copy(cst[:, f, 1:1 + NB, :], zs[:, :, 4:6])
                chain.link(gp.tensor_scalar(hc, cg, cw[2], 0.0, ALU.mult, ALU.add))
                for k in (1, 0):
                    d = 2 - k
                    gp.tensor_scalar(smp(ctmp), zs[:, :, k:k + NL], cw[k], 0.0, ALU.mult, ALU.add)
                    chain.link(gp.tensor_scalar(ctmp[:, 0:TP - d], cg[:, 0:TP - d], cw[k], 0.0, ALU.mult, ALU.add))
                    gp.tensor_tensor(smp(hc), smp(hc), smp(ctmp), ALU.add)
                    chain.link(gp.tensor_tensor(hc[:, d:TP], hc[:, d:TP], ctmp[:, 0:TP - d], ALU.add))
                chain.link(gp.tensor_tensor(bg, bg, hc, ALU.mult))
                yh, yl = ysp[:, 4 * f, :], ysp[:, 4 * f + 1, :]
                chain.link(gp.tensor_copy(yh, bg))
                gp.tensor_tensor(yl, bg, yh.bitcast(F32), ALU.subtract).then_inc(ya_ready, 1)

                g, n = f // 2, f // 2 + 1
                p_s = smp(p_t)
                ps_ = pps[f % 2]
                st = pst[f % 2]
                gp.wait_ge(tile_saved, MIX_RING + 4 * f + 4)
                gp.wait_ge(pps_loaded[f % 2], 16 * (f // 2 + 1))
                gp.tensor_copy(pp[:, 16:NPP], p_t[:, 0:TP])
                chain.link(gp.tensor_copy(ps_[:, :, 16:20], p_s))
                if f >= 2:
                    gp.wait_ge(pst_stored[f % 2], 16 * (f // 2))
                gp.tensor_copy(st[:, 0:PST], p_t[:, TP - PST:TP])
                chain.link(gp.tensor_copy(st[:, PST:].rearrange("p (b l) -> p b l", l=PST), ps_[:, :, 5:20]))
                gp.dma_start(pool_out[f], st[:]).then_inc(pst_stored[f % 2], 16)
                src, src_s, bufs = pp[:], ps_[:], [pa, pb_]
                for k in range(n):
                    s_, lo = 1 << k, (1 << (k + 1)) - 1
                    dst = bufs[k % 2][:, 0:NPP]
                    dst_s = bufs[k % 2][:, NPP:].rearrange("p (b l) -> p b l", l=20)
                    gp.tensor_tensor(dst[:, lo:NPP], src[:, lo:NPP], src[:, lo - s_:NPP - s_], ALU.add)
                    chain.link(gp.tensor_tensor(dst_s[:, :, lo:20], src_s[:, :, lo:20], src_s[:, :, lo - s_:20 - s_],
                                                ALU.add))
                    src, src_s = dst, dst_s
                mean, mean_s = bufs[n % 2][:, 0:NPP], bufs[n % 2][:, NPP:].rearrange("p (b l) -> p b l", l=20)
                gp.tensor_scalar(mean[:, 32:NPP], src[:, 32:NPP], 1.0 / (1 << n), 0.0, ALU.mult, ALU.add)
                gp.tensor_tensor(mean[:, 16:32], src[:, 16:32], inv[:, g, :], ALU.mult)
                chain.link(gp.tensor_scalar(mean_s[:, :, 16:20], src_s[:, :, 16:20], 1.0 / (1 << n), 0.0,
                                            ALU.mult, ALU.add))
                chain.link(gp.tensor_tensor(p_t[:, 0:TP], mean[:, 16:NPP], pp[:, 16:NPP], ALU.subtract))
                gp.tensor_tensor(p_s, mean_s[:, :, 16:20], ps_[:, :, 16:20], ALU.subtract).then_inc(d_ready, 1)
                gp.wait_ge(d_ready, f + 1)
                if f + 2 < WT:
                    gp.dma_start(ps_[:], pool_in[f + 2]).then_inc(pps_loaded[f % 2], 16)
            gp.dma_start(conv_out, cst[:]).then_inc(conv_stored, 16)

            gp.wait_ge(vn_ready, WT)
            gp.dma_start(v_out, proj[:, 4 * WT:5 * WT, TP:T]).then_inc(v_stored, 16)

            for f in range(WT):
                gp.wait_ge(yb_ready, f + 1)
                gp.wait_ge(pool_mm, min(WT, 2 * (f // 2) + 2))
                gp.tensor_copy(ysp[:, 4 * f + 3, :], proj[:, 4 * f + 2, :]).then_inc(ybs_ready, 1)
                gp.wait_ge(ybs_ready, 2 * f + 1)
                gp.tensor_tensor(ysp[:, 4 * f + 2, :], proj[:, 4 * f + 2, :],
                                 ysp[:, 4 * f + 3, :].bitcast(F32), ALU.subtract).then_inc(ybs_ready, 1)
            gp.wait_ge(v_stored, 16)
            gp.wait_ge(vtr_done, 6)
            for f in range(WT):
                gp.wait_ge(yc_ready, f + 1)
                gp.tensor_copy(ysp[:, 4 * WT + f, :], proj[:, 5 * WT + f, :]).then_inc(ycs_ready, 1)
                gp.wait_ge(ycs_ready, 2 * f + 1)
                gp.tensor_tensor(ysp[:, 5 * WT + f, :], proj[:, 5 * WT + f, :],
                                 ysp[:, 4 * WT + f, :].bitcast(F32), ALU.subtract).then_inc(ycs_ready, 1)

            def add_squares(src, f, sq):
                if f == 0:
                    chain.link(gp.tensor_tensor(sqs[:], src, src, ALU.mult))
                    return
                chain.link(gp.tensor_tensor(sq, src, src, ALU.mult))
                last = gp.tensor_tensor(sqs[:], sqs[:], sq, ALU.add)
                chain.link(last) if f < KT - 1 else last.then_inc(sqs_ready, 1)

            gp.wait_ge(ada_sel, ADA1_BLOCKS + KT + 1)
            for f in range(KT):
                gp.wait_ge(x1_ready, 3 + f + 1)
                add_squares(x1[:, f, :], f, sqt[:])
            gp.wait_ge(rs_ready, 1)
            hs = h2[:, :, TP:T]
            gp.tensor_tensor(hs, x1[:, :, TP:T], v_rs[:, TP:T].unsqueeze(1).broadcast_to([P, KT, TS]), ALU.mult)\
                .then_inc(hs_ready, 1)
            hs4 = hs.rearrange("p f (b l) -> p f b l", l=NL)
            for k, by in enumerate((a2[:], mod[:, SH2:SH2 + KT, :])):
                gp.wait_ge(hs_ready, k + 1)
                gp.tensor_tensor(hs4, hs4, by[:, :, 1:NSEQ].unsqueeze(3).broadcast_to([P, KT, NB, NL]),
                                 (ALU.mult, ALU.add)[k]).then_inc(hs_ready, 1)
            for u in range(1, 12, 2):
                t_, q = UNITS[u]
                n = TT[t_][1]
                piece = ye[0:n, 512 * (u // 2 % 2):512 * (u // 2 % 2) + 512]
                gp.wait_ge(thi_ready, u + 1)
                gp.tensor_copy(thi[0:n, t_, 512 * q:512 * q + 512], piece).then_inc(tlp_ready, 1)
                gp.wait_ge(tlp_ready, u)
                for f in (0, 256):
                    f0 = 512 * q + f
                    last = gp.tensor_tensor(rest_rows(t_, f0, 256), piece[:, f:f + 256],
                                            thi[0:n, t_, f0:f0 + 256].bitcast(F32), ALU.subtract)
                last.then_inc(tlp_ready, 1)
            gp.wait_ge(tlp_ready, 12)
            gp.memset(ye[:], 0.0).then_inc(tlp_ready, 1)
            for j in range(8):
                gp.wait_ge(sq_ready, SQ_BEFORE + 2 * j + 2)
                if j == 0:
                    chain.link(gp.tensor_tensor(sqs[:], sq4[:, 0, :], sq4[:, 8, :], ALU.add))
                    continue
                chain.link(gp.tensor_tensor(sqs[:], sqs[:], sq4[:, j, :], ALU.add))
                last = gp.tensor_tensor(sqs[:], sqs[:], sq4[:, 8 + j, :], ALU.add)
                chain.link(last) if j < 7 else last.then_inc(sqs_ready, 1)
            for f in range(3, KT, 4):
                chain.link(gp.tensor_scalar(h2[:, f, :], x1[:, f, :], par[:, C_GF + f:C_GF + f + 1], 0.0, ALU.mult, ALU.add))
            gp.wait_ge(rs_ready, 2)
            for f in range(3, KT, 4):
                gp.tensor_tensor(h2[:, f, :], h2[:, f, :], v_rs[:], ALU.mult).then_inc(yp_ready, 1)

        @block.scalar
        def _(act):
            act.sem_inc(tile_saved, MIX_RING)
            act.sem_inc(sig_ready, 3)
            for s in from_one["scalar"]:
                act.sem_inc(s, 1)

            def split_hi(unit):
                src, loaded, value, u, b = unit
                act.wait_ge(loaded, value)
                act.wait_ge(w_used, u + 1)
                act.activation(wh[:, b], src, ACT.Copy).then_inc(hi_ready, 1)

            def root(n):
                act.wait_ge(var_ready, n)
                act.activation(v_rs[:], v_var[:], ACT.Sqrt).then_inc(std_ready, 1)

            def save_part(n):
                act.wait_ge(ada_used, n * 4 + 4)
                act.wait_ge(ada_sel, n + 1)
                act.activation(part[:], bank[6][:], ACT.Copy).then_inc(part_ready, 1)

            def modulate(x, a, shift, q, n):
                act.wait_ge(h_ready, n)
                for f in (4 * q, 4 * q + 2):
                    last = act.activation(x[:, f, 0:TP], x[:, f, 0:TP], ACT.Identity, scale=a[:, f, 0:1],
                                          bias=mod[:, shift + f, 0:1])
                last.then_inc(hp_ready, 1)

            act.wait_ge(x_loaded, 16)
            for q in range(4):
                act.activation(sq1[:, 4 * q:4 * q + 4, :], xa[:, 4 * q:4 * q + 4, :], ACT.Square).then_inc(sq_ready, 1)
            root(1)
            for q in range(4):
                save_part(2 * q)
                save_part(2 * q + 1)
                modulate(xa, a1, SH1, q, q + 1)
                act.wait_ge(hp_ready, q + 1)
                act.activation(hh[:, 4 * q:4 * q + 4, :], xa[:, 4 * q:4 * q + 4, :], ACT.Copy).then_inc(hh_ready, 1)
            for k in range(NSPL):
                split_hi(mix_unit(0, k))

            def mix_step(it, s, unit):
                split_hi(unit(it, 2 * s + 3))
                act.wait_ge(w_used, it * 12 + (2 * s + 2 + NSPL))
                act.activation(proj[:, ds(it * MIX_RING + s, 1), :].rearrange("p a t -> p (a t)"),
                               bank[s][:, 0:T], ACT.Copy).then_inc(tile_saved, 1)
                split_hi(unit(it, 2 * s + 4))

            with act.Fori(0, MIX_IT - 1) as it:
                for s in range(MIX_RING):
                    mix_step(it, s, mix_unit)

            def save_vtok(u):
                tt, half_ = u // 2, u % 2
                n = TT[tt][1]
                act.wait_ge(vtr_done, u + 1)
                act.activation(vtok[0:n, tt, 512 * half_:512 * half_ + 512], bank[6 + half_][0:n, :], ACT.Copy)\
                    .then_inc(vtok_a, 1)

            for s in range(MIX_RING):
                mix_step(MIX_IT - 1, s, mix_then_gates)
                if s == 0:
                    for f in range(WT):
                        act.wait_ge(pool_mm, f + 1)
                        act.activation(proj[:, 4 * f + 2, :], bank[6 + f % 2][:, 0:T], ACT.Copy,
                                       scale=par[:, C_PS + f:C_PS + f + 1]).then_inc(yb_ready, 1)
                    act.wait_ge(d_ready, WT)
                    for k in range(2):
                        act.wait_ge(pst_stored[k], 16 * WT // 2)
                    act.wait_ge(conv_stored, 16)
                    act.activation(vsq[:], proj[:, 4 * WT:5 * WT, :], ACT.Square).then_inc(sq_ready, 1)
                if s == 1:
                    root(2)
                if s >= 3:
                    save_vtok(2 * (s - 3))

            def merged_heads(q):
                act.wait_ge(merged_ready, 4 * q + 4 + 1)
                act.activation(mh[:, 4 * q:4 * q + 4, :], merged[:, 4 * q:4 * q + 4, :], ACT.Copy).then_inc(mh_ready, 1)

            def gates_step(ot, unit):
                for n in range(3):
                    split_hi(unit(ot, 2 * n + 3))
                    act.wait_ge(w_used, ot * GATE_HALVES + (MIX_HALVES + 2 * n + 2 + NSPL))
                    act.wait_ge(merged_ready, ot + 1)
                    act.activation(sig[:, n, :], bank[n][:, 0:T], ACT.Sigmoid).then_inc(sig_ready, 1)
                    split_hi(unit(ot, 2 * n + 4))
                save_part(ot + ADA1_BLOCKS)
                for k in (9, 10, 11):
                    split_hi(unit(ot, k))

            with act.Fori(0, KT - 1) as ot:
                gates_step(ot, gate_unit)
            gates_step(KT - 1, gates_then_wo)
            for q in range(3):
                merged_heads(q)
            merged_heads(3)
            with act.Fori(0, 4) as v:
                for k in range(3, 9):
                    split_hi(wo_unit(v, k))
            for k in range(3, 8):
                split_hi(wo_unit(4, k))

            root(3)
            for f in range(KT):
                act.wait_ge(h_ready, 4 + f + 1)
                act.activation(h2[:, f, 0:TP], h2[:, f, 0:TP], ACT.Identity, bias=mod[:, SH2 + f, 0:1])\
                    .then_inc(hp_ready, 1)
            act.wait_ge(logit_sums, 1)
            act.activation(lgp[:], bank[1][:, 0:T], ACT.Copy).then_inc(lgp_ready, 1)
            def take(u):
                t_, q = UNITS[u]
                n = TT[t_][1]
                act.wait_ge(htr_done, u + 1)
                b = bank[2 + u % 6]
                if u % 2 == 0:
                    last = act.activation(thi[0:n, t_, 512 * q:512 * q + 512], b[0:n, :], ACT.Copy)
                else:
                    if u >= 5:
                        act.wait_ge(tlp_ready, u - 3)
                    last = act.activation(ye[0:n, 512 * (u // 2 % 2):512 * (u // 2 % 2) + 512], b[0:n, :], ACT.Copy)
                last.then_inc(thi_ready, 1)

            for u in range(7):
                take(u)
            act.wait_ge(exp_in, 1)
            act.activation(sc[:, :, 31:36], sc[:, :, 26:31], ACT.Exp).then_inc(exp_ready, 1)
            for u in range(7, 12):
                take(u)

            def experts(i):
                for q in range(4):
                    act.wait_ge(gath_done, i * 8 + (2 * q + 1) + 1)
                    act.activation(xg[:, 4 * q:4 * q + 2, :],
                                   bank[4].rearrange("p (a n) -> p a n", a=2) if q % 2 == 0 else
                                   bank[6].rearrange("p (a n) -> p a n", a=2), ACT.Copy).then_inc(xg_a, 1)
                for e in range(EPG):
                    m1 = i * EPG + (e + 1)
                    act.wait_ge(moe_used, m1 * 12 - 4)
                    act.wait_ge(tr_done, i * EPG + e + 1)
                    act.activation(gus[:], bank[0][:], ACT.Copy).then_inc(gu_saved, 1)
                    act.wait_ge(st_done, m1 + 1)
                    act.activation(sT[e % 2][:], bank[0][:, 0:T], ACT.Copy).then_inc(st_ready, 1)
                    act.wait_ge(tr_done, m1 + 1)
                    act.wait_ge(hid_ready, i * EPG + e + 1)
                    act.activation(sg[:], bank[1].rearrange("p (f c) -> p f c", f=FT)[:, :, 0:CAP], ACT.Silu)\
                        .then_inc(sg_ready, 1)
                    act.wait_ge(moe_used, m1 * 12)
                    act.activation(ye[:, 0:512], bank[2][:], ACT.Copy).then_inc(ye_a, 1)

            act.wait_ge(rounds_ready, 1)
            rounds = act.value_load(rnd[0:1, 0:1], min_val=1, max_val=-(-T // CAP))
            with act.Fori(0, rounds) as r:
                with act.Fori(0, NG) as g:
                    experts(r * NG + g)
            for j in range(8):
                act.wait_ge(acc_ready, rounds * (8 * NE) + (j + 2))
                for f in (j, 8 + j):
                    act.activation(sq4[:, f, :], x1[:, f, :], ACT.Square).then_inc(sq_ready, 1)
            root(4)

        @block.vector
        def _(dve):
            chain = Tally(dve, dch)
            dve.sem_inc(x1_ready, 3)
            for s in from_one["vector"]:
                dve.sem_inc(s, 1)

            def tt(out, a, b, op):
                return dve.tensor_tensor(out, a, b, op)

            def split_lo(unit):
                src, _, _, u, b = unit
                dve.wait_ge(hi_ready, u + 1)
                tt(wl[:, b], src, wh[:, b].bitcast(F32), ALU.subtract).then_inc(lo_ready, 1)

            def rsqrt(sums, n, k):
                dve.tensor_scalar(v_var[:], sums, 1.0 / n, EPS, ALU.mult, ALU.add).then_inc(var_ready, 1)
                dve.wait_ge(std_ready, k)
                chain.link(dve.reciprocal(v_rs[:], v_rs[:]))
                chain.link(tt(v_t[:], v_rs[:], v_rs[:], ALU.mult))
                chain.link(tt(v_t[:], v_t[:], v_var[:], ALU.mult))
                chain.link(dve.tensor_scalar(v_t[:], v_t[:], -0.5, 1.5, ALU.mult, ALU.add))
                chain.link(tt(v_rs[:], v_rs[:], v_t[:], ALU.mult))

            def smp(ap):
                return ap.rearrange("p (b l) -> p b l", l=NL)

            def seqs(ap):
                return ap[:, 1:NSEQ].unsqueeze(2).broadcast_to([P, NB, NL])

            def save_mod(n, chunk):
                dve.wait_ge(ada_sel, n + 1 + 1)
                bias = par[:, ds(chunk, 4)].unsqueeze(2).broadcast_to([P, 4, NSEQ])
                tt(mod[:, ds(chunk, 4), :], bank[7][:, 0:4 * NSEQ].rearrange("p (c s) -> p c s", s=NSEQ), bias, ALU.add)\
                    .then_inc(mod_ready, 1)

            def scales(a, first, g, k0, n):
                chain.link(dve.scalar_tensor_tensor(
                    a[:, k0:k0 + n, :], mod[:, first + k0:first + k0 + n, :], 1.0,
                    par[:, g + k0:g + k0 + n].unsqueeze(2).broadcast_to([P, n, NSEQ]), ALU.add, ALU.mult))

            def modulate(x, a, shift, q):
                sl = slice(4 * q, 4 * q + 4)

                def seqs4(ap):
                    return ap[:, :, 1:NSEQ].unsqueeze(3).broadcast_to([P, 4, NB, NL])

                xs = x[:, sl, TP:T].rearrange("p f (b l) -> p f b l", l=NL)
                chain.link(tt(xs, xs, seqs4(a[:, sl, :]), ALU.mult))
                for f in (4 * q + 1, 4 * q + 3):
                    dve.tensor_scalar(x[:, f, 0:TP], x[:, f, 0:TP], a[:, f, 0:1], mod[:, shift + f, 0:1], ALU.mult, ALU.add)
                tt(xs, xs, seqs4(mod[:, shift + 4 * q:shift + 4 * q + 4, :]), ALU.add).then_inc(h_ready, 1)

            dve.wait_ge(sums_done, 1)
            rsqrt(bank[0][:, 0:T], D, 1)
            chain.link(tt(xa[:], xa[:], v_rs[:].unsqueeze(1).broadcast_to([P, KT, T]), ALU.mult))
            dve.wait_ge(par_loaded, 48)
            for q in range(4):
                save_mod(2 * q, SH1 + 4 * q)
                save_mod(2 * q + 1, SC1 + 4 * q)
                dve.wait_ge(mod_ready, 2 * q + 3)
                scales(a1, SC1, C_G1, 4 * q, 4)
                modulate(xa, a1, SH1, q)
                dve.wait_ge(hh_ready, q + 1)
                sl = slice(4 * q, 4 * q + 4)
                tt(hl[:, sl, :], xa[:, sl, :], hh[:, sl, :].bitcast(F32), ALU.subtract).then_inc(hl_ready, 1)
            for k in range(NSPL):
                split_lo(mix_unit(0, k))
            with dve.Fori(0, MIX_IT - 1) as it:
                for k in range(3, 15):
                    split_lo(mix_unit(it, k))
            for s in range(MIX_RING):
                for k in (2 * s + 3, 2 * s + 4):
                    split_lo(mix_then_gates(MIX_IT - 1, k))
                if s == 1:
                    dve.wait_ge(sums_done, 2)
                    rsqrt(bank[7][:, 0:T], W, 2)
                    for f in range(WT):
                        v = proj[:, 4 * WT + f, :]
                        dve.scalar_tensor_tensor(v, v, par[:, C_GV + f:C_GV + f + 1], v_rs[:], ALU.mult, ALU.mult)\
                            .then_inc(vn_ready, 1)
                if s >= 3:
                    u = 2 * (s - 3) + 1
                    n = TT[u // 2][1]
                    dve.wait_ge(vtr_done, u + 1)
                    dve.tensor_copy(vtok[0:n, u // 2, 512:1024], bank[7][0:n, :]).then_inc(vtok_d, 1)
            for h in range(WT):
                dve.wait_ge(mix_mm, h + 1)
                b = bank[4 + h % 4]
                u = proj[:, 5 * WT + h, :]
                tt(b[:, 0:TP].rearrange("p (n t) -> p n t", n=2), b[:, 0:TP].rearrange("p (n t) -> p n t", n=2),
                   bs[:, h, :].unsqueeze(1).broadcast_to([P, 2, P]), ALU.add)
                chain.link(tt(smp(b[:, TP:T]), smp(b[:, TP:T]), bs[:, h, 0:NL].unsqueeze(1).broadcast_to([P, NB, NL]),
                              ALU.add))
                tt(u, b[:, 0:T], u, ALU.mult).then_inc(yc_ready, 1)

            def merged_rests(q):
                dve.wait_ge(mh_ready, q + 1)
                sl = slice(4 * q, 4 * q + 4)
                tt(ml[:, sl, :], merged[:, sl, :], mh[:, sl, :].bitcast(F32), ALU.subtract).then_inc(ml_ready, 1)

            def gates_step(ot, unit):
                split_lo(unit(ot, 3))
                for k in range(4, 10):
                    split_lo(unit(ot, k))
                br0 = ot * GATE_HALVES + (MIX_HALVES + 6 + NSPL)
                dst = merged[:, ds(ot, 1), :].rearrange("p a t -> p (a t)")
                dve.wait_ge(sig_ready, ot * 3 + (3 + 3))
                dve.wait_ge(w_used, br0 + 1)
                tt(gt[:, 0, :], bank[3][:, 0:T], sig[:, 0, :], ALU.mult)
                split_lo(unit(ot, 10))
                dve.wait_ge(w_used, br0 + 2)
                chain.link(tt(gt[:, 1, :], bank[4][:, 0:T], sig[:, 1, :], ALU.mult))
                chain.link(tt(dst, gt[:, 0, :], gt[:, 1, :], ALU.add))
                split_lo(unit(ot, 11))
                if unit is gates_then_wo:
                    for q in range(3):
                        merged_rests(q)
                save_mod(ot + ADA1_BLOCKS, ot * 4 + 2 * KT)
                dve.wait_ge(w_used, br0 + 3)
                chain.link(tt(gt[:, 0, :], bank[5][:, 0:T], sig[:, 2, :], ALU.mult))
                tt(dst, dst, gt[:, 0, :], ALU.add).then_inc(merged_ready, 1)

            with dve.Fori(0, KT - 1) as ot:
                chain.loop(ot, 3)
                gates_step(ot, gate_unit)
            chain.end(KT - 1)
            gates_step(KT - 1, gates_then_wo)
            merged_rests(3)

            def save_x1(v, s):
                o1 = ds(v * 3 + s, 1)
                gate1 = mod[:, ds(v * 3 + (GT1 + s), 1), :].rearrange("p a s -> p (a s)")
                dst = x1[:, o1, :].rearrange("p a t -> p (a t)")
                dve.wait_ge(w_used, v * 6 + (WO_BASE + 2 * s + 2 + NSPL))
                dve.scalar_tensor_tensor(dst[:, 0:TP], bank[s][:, 0:TP], gate1[:, 0:1], dst[:, 0:TP], ALU.mult, ALU.add)
                dve.wait_ge(x1_ready, v * 3 + (s + 3))
                chain.link(tt(smp(v_t[:, 0:TS]), smp(bank[s][:, TP:T]), seqs(gate1), ALU.mult))
                tt(dst[:, TP:T], dst[:, TP:T], v_t[:, 0:TS], ALU.add).then_inc(x1_ready, 1)

            dve.wait_ge(x1_loaded, 16)
            with dve.Fori(0, 4) as v:
                chain.loop(v, 3)
                for s in range(3):
                    for k in (2 * s + 3, 2 * s + 4):
                        split_lo(wo_unit(v, k))
                    save_x1(v, s)
            chain.end(4)
            for s in range(3):
                for k in (2 * s + 3, 2 * s + 4)[:1 if s == 2 else 2]:
                    split_lo(wo_unit(4, k))
                save_x1(4, s)
            save_x1(5, 0)

            scales(a2, SC2, C_G2, 0, KT)
            dve.wait_ge(sums_done, 3)
            rsqrt(bank[0][:, 0:T], D, 3)
            dve.sem_inc(rs_ready, 1)
            for f in range(KT):
                dve.scalar_tensor_tensor(h2[:, f, 0:TP], x1[:, f, 0:TP], a2[:, f, 0:1], v_rs[:, 0:TP], ALU.mult,
                                         ALU.mult).then_inc(h_ready, 1)

            def rest(u):
                t_, q = UNITS[u]
                n = TT[t_][1]
                dve.wait_ge(thi_ready, u + 1)
                for f in (0, 256):
                    f0 = 512 * q + f
                    last = tt(rest_rows(t_, f0, 256), bank[2 + u % 6][0:n, f:f + 256],
                              thi[0:n, t_, f0:f0 + 256].bitcast(F32), ALU.subtract)
                last.then_inc(tlo_ready, 1)

            dve.memset(sT[1][:], 0.0)
            chain.link(dve.memset(lg[:], 0.0))
            rest(0)
            dve.wait_ge(logits_done, 1)
            for t_, (_, n) in enumerate(TT):
                last = tt(lg[0:n, t_, :], bank[0][0:n, 32 * t_:32 * t_ + NR], br[0:n, :], ALU.add)
            chain.link(last)

            def col(a, n=1):
                return sc[:, :, a:a + n]

            def wide(ap, n):
                return ap.broadcast_to([P, 3, n])

            def reduce(out, src, op):
                chain.link(dve.tensor_reduce(out, src, AX_X, op))

            def top_of(src, m, eq, one, w):
                reduce(col(m), src, ALU.max)
                chain.link(tt(col(eq, 4), src, wide(col(m), 4), ALU.is_equal))
                chain.link(tt(col(eq, 4), col(eq, 4), w4[:].unsqueeze(1).broadcast_to([P, 3, 4]), ALU.mult))
                reduce(col(w), col(eq, 4), ALU.max)
                chain.link(tt(col(one, 4), col(eq, 4), wide(col(w), 4), ALU.is_equal))

            G_MAX, EQ, OHG, FIRST, SEL, M1, OH1, M2, OH2 = 0, 1, 5, 9, 10, 14, 15, 19, 20
            top_of(lg[:, :, 0:4], G_MAX, EQ, OHG, FIRST)
            chain.link(tt(col(26, 4), lg[:, :, 0:4], wide(col(G_MAX), 4), ALU.subtract))
            by_group = mk[:].rearrange("p t (g j) -> p t g j", g=NG)

            def spread(dst, four):
                dve_ = dst.rearrange("p t (g j) -> p t g j", g=NG)
                return tt(dve_, col(OHG, 4).unsqueeze(3).broadcast_to([P, 3, NG, EPG]),
                          four.unsqueeze(2).broadcast_to([P, 3, NG, EPG]), ALU.mult)

            chain.link(tt(by_group, lg[:, :, 4:20].rearrange("p t (g j) -> p t g j", g=NG),
                          col(OHG, 4).unsqueeze(3).broadcast_to([P, 3, NG, EPG]), ALU.mult))
            reduce(col(SEL, 4), by_group.rearrange("p t g j -> p t j g"), ALU.add)
            top_of(col(SEL, 4), M1, EQ, OH1, FIRST)
            chain.link(dve.scalar_tensor_tensor(col(SEL, 4), col(OH1, 4), -BIG, col(SEL, 4), ALU.mult, ALU.add))
            top_of(col(SEL, 4), M2, EQ, OH2, FIRST)
            tt(col(30), col(M2), col(M1), ALU.subtract).then_inc(exp_in, 1)
            rest(2)
            dve.wait_ge(exp_ready, 1)
            reduce(col(36), col(31, 4), ALU.add)
            chain.link(dve.tensor_scalar(col(37), col(35), 1.0, None, ALU.add))
            chain.link(tt(col(36), col(36), col(37), ALU.mult))
            chain.link(dve.reciprocal(col(36), col(36)))
            chain.link(tt(col(37), col(36), col(35), ALU.mult))
            chain.link(tt(col(EQ, 4), col(OH1, 4), wide(col(36), 4), ALU.mult))
            chain.link(tt(col(26, 4), col(OH2, 4), wide(col(37), 4), ALU.mult))
            chain.link(tt(col(EQ, 4), col(EQ, 4), col(26, 4), ALU.add))
            chain.link(tt(col(OH1, 4), col(OH1, 4), col(OH2, 4), ALU.add))
            chain.link(tt(col(OHG, 4), col(OHG, 4), valid[:].unsqueeze(2).broadcast_to([P, 3, 4]), ALU.mult))
            spread(mk[:], col(OH1, 4)).then_inc(mk_ready, 1)
            chain.link(spread(cb[:], col(EQ, 4)))
            rest(4)
            rest(6)
            dve.wait_ge(rank_done, 1)
            chain.link(dve.scalar_tensor_tensor(rk[:, :, 0:NE], bank[1][:, 0:3 * NE].rearrange("p (t e) -> p t e", e=NE),
                                                1.0, mk[:], ALU.add, ALU.mult))
            chain.link(dve.tensor_scalar(rk[:, :, 0:NE], rk[:, :, 0:NE], -1.0, None, ALU.add))
            dve.tensor_scalar(rk[:, :, NE:NE + EPG], rk[:, :, 0:EPG], -float(CAP), None, ALU.add)

            def one_hot(four):
                tt(oh[:].rearrange("p t (e c) -> p t e c", e=EPG),
                   iota[:].unsqueeze(1).unsqueeze(1).broadcast_to([P, 3, EPG, CAP]),
                   rk[:, :, four].unsqueeze(3).broadcast_to([P, 3, EPG, CAP]), ALU.is_equal).then_inc(oh_ready, 1)

            one_hot(slice(0, EPG))
            chain.link(dve.tensor_reduce(sc[:, 0, 8:8 + NE], bank[1][:, 64:64 + 3 * NE].rearrange(
                "p (t e) -> p e t", e=NE), AX_X, ALU.add))
            dve.tensor_scalar(sc[:, 0, 1:6], iota[:, 0:5], float(CAP), None, ALU.mult)
            chain.link(dve.tensor_reduce(sc[:, 0, 0:1], sc[:, 0, 8:8 + NE], AX_X, ALU.max))
            chain.link(tt(sc[:, 0, 1:6], sc[:, 0, 0:1].broadcast_to([P, 5]), sc[:, 0, 1:6], ALU.is_gt))
            chain.link(dve.tensor_reduce(sc[:, 0, 6:7], sc[:, 0, 1:6], AX_X, ALU.add))
            dve.tensor_copy(rnd[:, 0:1], sc[:, 0, 6:7]).then_inc(rounds_ready, 1)
            rest(8)
            rest(10)

            def save_scat(j, total):
                dve.wait_ge(scat_done, total + (j + 1))
                b = 4 + 2 * (j % 2)
                for h in range(2):
                    last = tt(smp(scaled[:, j % 2, h, :]), smp(bank[b + h][:, TP:T]), seqs(mod[:, GT2 + 8 * h + j, :]), ALU.mult)
                last.then_inc(dch, 1)
                for h in range(2):
                    f = 8 * h + j
                    dve.scalar_tensor_tensor(x1[:, f, 0:TP], bank[b + h][:, 0:TP], mod[:, GT2 + f, 0:1], x1[:, f, 0:TP],
                                             ALU.mult, ALU.add)
                chain.after()
                tt(x1[:].rearrange("p (h j) t -> p h j t", h=2)[:, :, j, TP:T],
                   x1[:].rearrange("p (h j) t -> p h j t", h=2)[:, :, j, TP:T], scaled[:, j % 2], ALU.add).then_inc(acc_ready, 1)

            def experts(i, g):
                chain.loop(i, 8 * EPG)
                four = ds(g * EPG, EPG)
                dve.wait_ge(oh_ready, i + 1)
                dve.wait_ge(st_done, i * EPG + 1)
                tt(gc[:], oh[:].bitcast(F32).rearrange("p t (e c) -> p t e c", e=EPG),
                   cb[:, :, four].unsqueeze(3).broadcast_to([P, 3, EPG, CAP]), ALU.mult).then_inc(gc_ready, 1)
                for q in range(4):
                    dve.wait_ge(gath_done, i * 8 + (2 * q + 2) + 1)
                    dve.tensor_copy(xg[:, 4 * q + 2:4 * q + 4, :],
                                    bank[5 if q % 2 == 0 else 7].rearrange("p (a n) -> p a n", a=2)).then_inc(xg_d, 1)
                for e in range(EPG):
                    m1 = i * EPG + (e + 1)
                    for j in range(6):
                        save_scat(j, i * (8 * EPG) + 8 * e)
                    if e == EPG - 1:
                        dve.wait_ge(gc_ready, i + 1)
                        one_hot(ds(g * EPG + EPG, EPG))
                    dve.wait_ge(sg_ready, m1)
                    tt(hid[:], sg[:], bank[1].rearrange("p (f c) -> p f c", f=FT)[:, :, CAP:2 * CAP], ALU.mult)\
                        .then_inc(hid_ready, 1)
                    for j in (6, 7):
                        save_scat(j, i * (8 * EPG) + 8 * e)
                    dve.wait_ge(moe_used, m1 * 12)
                    dve.tensor_copy(ye[:, 512:1024], bank[3][:]).then_inc(ye_d, 1)

            dve.wait_ge(rounds_ready, 1)
            rounds = dve.value_load(rnd[0:1, 0:1], min_val=1, max_val=-(-T // CAP))
            with dve.Fori(0, rounds) as r:
                with dve.Fori(0, NG) as g:
                    experts(r * NG + g, g)
                dve.tensor_scalar(rk[:], rk[:], -float(CAP), None, ALU.add).then_inc(round_ready, 1)
                dve.wait_ge(round_ready, r + 1)
            chain.loop(rounds, 8 * EPG * NG)
            for j in range(8):
                save_scat(j, rounds * (8 * NE))

            dve.wait_ge(sums_done, 4)
            rsqrt(bank[0][:, 0:T], D, 4)
            dve.sem_inc(rs_ready, 1)
            for q in range(4):
                for f in range(4 * q, 4 * q + 3):
                    last = dve.scalar_tensor_tensor(h2[:, f, :], x1[:, f, :], par[:, C_GF + f:C_GF + f + 1], v_rs[:],
                                                    ALU.mult, ALU.mult)
                last.then_inc(y_ready, 1)

        @block.tensor
        def _(pe):
            pe.sem_inc(w_used, NSPL)
            for s in from_one["tensor"]:
                pe.sem_inc(s, 1)
            mm = pe.matmul

            def sums(src, n, b, q_of):
                for f in range(n):
                    if f % q_of == 0:
                        sums.quarter += 1
                        pe.wait_ge(sq_ready, sums.quarter)
                    last = mm(bank[b][:, 0:T], ones[:], src[:, f, :], start=f == 0, stop=f == n - 1)
                last.then_inc(sums_done, 1)

            sums.quarter = 0

            def ada_chunk(buf, j, loaded, value):
                pe.wait_ge(loaded, value)
                for q in range(4):
                    last = mm(bank[6][32 * q:32 * q + 32, :], cT[:, 4 * j + q, :], buf[:, q, :], start=j == 0,
                              stop=j == ADA_CHUNKS - 1, tile_position=(0, 32 * q))
                last.then_inc(ada_used, 1)

            def ada_select(n):
                pe.wait_ge(part_ready, n + 1 + 1)
                pe.wait_ge(mod_ready, n + 1)
                for c in range(4):
                    last = mm(bank[7][:, NSEQ * c:NSEQ * c + NSEQ], part[:, P * c:P * c + P], sel[:, 0:NSEQ], start=True, stop=True)
                last.then_inc(ada_sel, 1)

            pe.wait_ge(consts, 1)
            sums(sq1, KT, 0, 4)
            pe.wait_ge(c_loaded, 16)
            with pe.Fori(0, ADA1_BLOCKS // 2) as it:
                for b in range(2):
                    n = it * 2 + b
                    pe.wait_ge(part_ready, n + 1)
                    for j in range(ADA_CHUNKS):
                        ada_chunk(ring8[4 * b + j], j, slot_loaded[4 * b + j], it * 16 + 16)
                    ada_select(n)

            def half(unit, b, hi, lo, first, start, stop):
                _, _, _, u, s = unit
                pe.wait_ge(lo_ready, u + 1)
                for k in range(HALF):
                    out = bank[b][:, 0:T]
                    mm(out, wh[:, s, k, :], hi[:, first + k, :], start=start and k == 0, stop=False)
                    mm(out, wh[:, s, k, :], lo[:, first + k, :], start=False, stop=False)
                    last = mm(out, wl[:, s, k, :], hi[:, first + k, :], start=False, stop=stop and k == HALF - 1)
                last.then_inc(w_used, 1)

            def tile(unit_of, it, k, b, hi, lo):
                half(unit_of(it, k), b, hi, lo, 0, True, False)
                half(unit_of(it, k + 1), b, hi, lo, HALF, False, True)

            def mix_tile(it, s):
                pe.wait_ge(tile_saved, it * MIX_RING + (s + 1))
                pe.wait_ge(hl_ready, 2)
                half(mix_unit(it, 2 * s), s, hh, hl, 0, True, False)
                pe.wait_ge(hl_ready, 4)
                half(mix_unit(it, 2 * s + 1), s, hh, hl, HALF, False, True)

            with pe.Fori(0, MIX_IT - 1) as it:
                for s in range(MIX_RING):
                    mix_tile(it, s)

            def vtr(u):
                tt, half_ = u // 2, u % 2
                c0, n = TT[tt]
                if tt >= 1:
                    pe.wait_ge(vtok_a if half_ == 0 else vtok_d, tt)
                for f in range(4):
                    last = mm(bank[6 + half_][0:n, P * f:P * f + P], proj[:, 4 * WT + 4 * half_ + f, c0:c0 + n],
                              ident[:], start=True, stop=True)
                last.then_inc(vtr_done, 1)

            for s in range(MIX_RING):
                mix_tile(MIX_IT - 1, s)
                if s == 0:
                    pe.wait_ge(masked, 1)
                    for f in range(WT):
                        g = f // 2
                        pe.wait_ge(d_ready, 2 * g + 2)
                        if f >= 2:
                            pe.wait_ge(yb_ready, f - 1)
                        for k in range(2):
                            last = mm(bank[6 + f % 2][:, 0:T], pw[:, g, k, f % 2, :], proj[:, 4 * (2 * g + k) + 3, :],
                                      start=k == 0, stop=k == 1)
                        last.then_inc(pool_mm, 1)
                if s == 1:
                    pe.wait_ge(yb_ready, WT)
                    sums(vsq, WT, 7, WT)
                if s == 3:
                    pe.wait_ge(vn_ready, WT)
                if s >= 3:
                    vtr(2 * (s - 3))
                    vtr(2 * (s - 3) + 1)
            pe.wait_ge(vtok_a, 3)
            pe.wait_ge(vtok_d, 3)
            for h in range(WT):
                b = bank[4 + h % 4]
                if h >= 4:
                    pe.wait_ge(yc_ready, h - 3)
                elif h < 2:
                    pe.wait_ge(tile_saved, MIX_RING + MIX_TILES)
                for c in range(2):
                    mm(b[:, P * c:P * c + P], vtok[:, c, P * h:P * h + P], wst[:, h, :], start=True, stop=True)
                mm(b[:, TP:T], vtok[0:TS, 2, P * h:P * h + P], bd[:, h, :], start=True, stop=True).then_inc(mix_mm, 1)

            def branch(ot, n):
                pe.wait_ge([ya_ready, ybs_ready, ycs_ready][n], [WT, 2 * WT, 2 * WT][n])
                first = ysp[:, 0:4 * WT, :].rearrange("p (f k) t -> p k f t", k=4)
                hi, lo = [(first[:, 0], first[:, 1]), (first[:, 3], first[:, 2]),
                          (ysp[:, 4 * WT:5 * WT, :], ysp[:, 5 * WT:6 * WT, :])][n]
                half(gate_unit(ot, 6 + n), 3 + n, hi, lo, 0, True, True)

            def gates_step(ot):
                for n in range(3):
                    pe.wait_ge(sig_ready, ot * 3 + (n + 1))
                    tile(gate_unit, ot, 2 * n, n, hh, hl)
                    if n == 0:
                        pe.wait_ge(part_ready, ot + ADA1_BLOCKS + 1)
                        for j in range(2):
                            ada_chunk(adaw[j], j, ada_loaded[j], ot * 32 + 16)
                for j in range(2, 4):
                    ada_chunk(adaw[j % 2], j, ada_loaded[j % 2], ot * 32 + 32)
                pe.wait_ge(merged_ready, ot + 1)
                for n in range(3):
                    branch(ot, n)
                    if n == 1:
                        ada_select(ot + ADA1_BLOCKS)

            pe.wait_ge(yc_ready, WT)
            with pe.Fori(0, KT) as ot:
                gates_step(ot)

            with pe.Fori(0, 5) as v:
                for s in range(3):
                    pe.wait_ge(x1_ready, v * 3 + (s + 1))
                    pe.wait_ge(ml_ready, 2)
                    half(wo_unit(v, 2 * s), s, mh, ml, 0, True, False)
                    pe.wait_ge(ml_ready, 4)
                    half(wo_unit(v, 2 * s + 1), s, mh, ml, HALF, False, True)
            pe.wait_ge(x1_ready, 16)
            tile(wo_unit, 5, 0, 0, mh, ml)

            pe.wait_ge(sqs_ready, 1)
            mm(bank[0][:, 0:T], ones[:], sqs[:], start=True, stop=True).then_inc(sums_done, 1)

            def logits(q):
                for c in range(4):
                    pe.wait_ge(hp_ready, 4 + 4 * q + c + 1)
                    last = mm(bank[1][32 * c:32 * c + 32, 0:T], wr[:, 4 * q + c, :], h2[:, 4 * q + c, :], start=q == 0,
                              stop=q == 3, tile_position=(0, 32 * c))
                if q == 3:
                    last.then_inc(logit_sums, 1)

            def turn(units):
                for u in units:
                    t_, q = UNITS[u]
                    c0, n = TT[t_]
                    if u >= 6:
                        pe.wait_ge(*((thi_ready, u - 5) if u % 2 else (tlo_ready, u // 2 - 2)))
                    for f in range(4):
                        last = mm(bank[2 + u % 6][0:n, P * f:P * f + P], h2[:, 4 * q + f, c0:c0 + n], ident[:],
                                  start=True, stop=True)
                    last.then_inc(htr_done, 1)

            pe.wait_ge(hs_ready, 3)
            for q in range(4):
                logits(q)
                if q in (1, 2):
                    turn(range(3 * q - 3, 3 * q))
            pe.wait_ge(lgp_ready, 1)
            for t_, (c0, n) in enumerate(TT):
                last = mm(bank[0][0:n, 32 * t_:32 * t_ + NR], lgp[:, c0:c0 + n], sel[:], start=True, stop=True)
            last.then_inc(logits_done, 1)
            turn(range(6, 12))
            pe.wait_ge(mk_ready, 1)
            marks = mk[:].rearrange("p t e -> p (t e)")
            mm(bank[1][:, 0:3 * NE], tri[:], marks, start=True, stop=False)
            mm(bank[1][:, NE:3 * NE].rearrange("p (t e) -> p t e", e=NE), ones[:],
               mk[:, 0:1, :].broadcast_to([P, 2, NE]), start=False, stop=False)
            mm(bank[1][:, 2 * NE:3 * NE], ones[:], mk[:, 1, :], start=False, stop=True)
            mm(bank[1][:, 64:64 + 3 * NE], ones[:], marks, start=True, stop=True).then_inc(rank_done, 1)

            def scatter(j, e_before, total):
                b = 4 + 2 * (j % 2)
                pe.wait_ge(acc_ready, total + max(j - 1, 0) + 1)
                for h in range(2):
                    rows = slice(64 * h, 64 * h + 64)
                    last = mm(bank[b + h][:, 0:T], ye[rows, P * j:P * j + P], sT[e_before % 2][rows, :], start=True,
                              stop=True, tile_position=(64 * h, 0))
                last.then_inc(scat_done, 1)

            def experts(i):
                pe.wait_ge(oh_ready, i + 1)
                pe.wait_ge(acc_ready, i * (8 * EPG) + 1)
                for dp in range(8):
                    b = [4, 5, 6, 7][dp % 4]
                    if dp >= 4:
                        pe.wait_ge(xg_d if dp % 2 else xg_a, i * 4 + (dp // 2 - 1))
                    for d in range(2):
                        f0 = P * (2 * dp + d)
                        for t_, (_, n) in enumerate(TT):
                            mm(bank[b][:, 256 * d:256 * d + 256], thi[0:n, t_, f0:f0 + P], oh[0:n, t_, :],
                               start=t_ == 0, stop=False)
                            last = mm(bank[b][:, 256 * d:256 * d + 256], rest_rows(t_, f0, P), oh[0:n, t_, :],
                                      start=False, stop=t_ == 2)
                    last.then_inc(gath_done, 1)
                for e in range(EPG):
                    m = i * EPG + e
                    slots = slice(CAP * e, CAP * e + CAP)
                    pe.wait_ge(st_ready, m + 1)
                    if e == 0:
                        pe.wait_ge(gc_ready, i + 1)
                    for c in range(4):
                        pe.wait_ge(slot_loaded[(2 * c + 3) % 12], m * 16 + (16 + slot_uses((2 * c + 3) % 12)))
                        pe.wait_ge(slot_loaded[(2 * c + 4) % 12], m * 16 + (16 + slot_uses((2 * c + 4) % 12)))
                        gate, up = ring8[(2 * c + 3) % 12], ring8[(2 * c + 4) % 12]
                        if e == 0:
                            pe.wait_ge(xg_a, i * 4 + (c + 1))
                            pe.wait_ge(xg_d, i * 4 + (c + 1))
                        for k in range(4):
                            kt = 4 * c + k
                            a = mm(bank[0][0:CAP, :], xg[:, kt, slots], gate[:, k, :], start=kt == 0, stop=kt == KT - 1,
                                   tile_position=(0, 0))
                            b = mm(bank[0][CAP:2 * CAP, :], xg[:, kt, slots], up[:, k, :], start=kt == 0,
                                   stop=kt == KT - 1, tile_position=(0, CAP))
                        a.then_inc(moe_used, 1)
                        b.then_inc(moe_used, 1)
                        if c == 1:
                            if e == 0:
                                pe.wait_ge(xg_a, i * 4 + 4)
                                pe.wait_ge(xg_d, i * 4 + 4)
                            pe.wait_ge(ye_a, m + 1)
                            pe.wait_ge(ye_d, m + 1)
                        if c > 0:
                            scatter(c - 1, e + 1, m * 8)
                    for j in (3, 4, 5):
                        scatter(j, e + 1, m * 8)
                    pe.wait_ge(gu_saved, m + 1)
                    for t_, (c0, n) in enumerate(TT):
                        for h in range(2):
                            last = mm(bank[0][CAP * h:CAP * h + CAP, c0:c0 + n], gc[0:n, t_, e], ident[0:n, 0:n],
                                      start=True, stop=True, tile_position=(0, CAP * h))
                    last.then_inc(st_done, 1)
                    for f in range(FT):
                        last = mm(bank[1][:, P * f:P * f + P], gus[:, P * f:P * f + P], ident[:], start=True, stop=True)
                    last.then_inc(tr_done, 1)
                    for j in (6, 7):
                        scatter(j, e + 1, m * 8)
                    pe.wait_ge(hid_ready, m + 1 + 1)
                    for c in range(FT):
                        k = (c + 11) % 12
                        pe.wait_ge(slot_loaded[k], m * 16 + (16 + slot_uses(k)))
                        for b in range(2):
                            for h in range(2):
                                last = mm(bank[2 + b][CAP * h:CAP * h + CAP, :], hid[:, c, :],
                                          dring[k][:, 1024 * h + 512 * b:1024 * h + 512 * b + 512], start=c == 0,
                                          stop=c == FT - 1, tile_position=(0, CAP * h))
                        last.then_inc(moe_used, 1)

            pe.wait_ge(thi_ready, 12)
            pe.wait_ge(tlo_ready, 6)
            pe.wait_ge(tlp_ready, 13)
            pe.wait_ge(rounds_ready, 1)
            rounds = pe.value_load(rnd[0:1, 0:1], min_val=1, max_val=-(-T // CAP))
            with pe.Fori(0, rounds) as r:
                with pe.Fori(0, NG) as g:
                    experts(r * NG + g)
            pe.wait_ge(ye_a, rounds * NE + 1)
            pe.wait_ge(ye_d, rounds * NE + 1)
            for j in range(8):
                scatter(j, NE - 1, rounds * (8 * NE))
            pe.wait_ge(sqs_ready, 2)
            mm(bank[0][:, 0:T], ones[:], sqs[:], start=True, stop=True).then_inc(sums_done, 1)


def kernel(x_prompt, x_sample, c_prompt, c_sample, state_conv, state_pool, w_ada, b_ada, g_norm1, w_in,
           conv_w, pool_w, pool_scale, g_v, w_s, b_s, w_br, w_o, g_norm2, w_rg, b_rg, w_re, b_re,
           w_gate, w_up, w_down, g_final):
    import numpy as np
    import concourse.bacc as bacc
    from concourse.bass_utils import run_bass_kernel_spmd

    (x_prompt, x_sample, c_prompt, c_sample, state_conv, state_pool, w_ada, b_ada, g_norm1, w_in, conv_w, pool_w,
     pool_scale, g_v, w_s, b_s, w_br, w_o, g_norm2, w_rg, b_rg, w_re, b_re, w_gate, w_up, w_down, g_final) = (
        np.asarray(a) for a in (
            x_prompt, x_sample, c_prompt, c_sample, state_conv, state_pool, w_ada, b_ada, g_norm1, w_in, conv_w, pool_w,
            pool_scale, g_v, w_s, b_s, w_br, w_o, g_norm2, w_rg, b_rg, w_re, b_re, w_gate, w_up, w_down, g_final))

    def tiles(a):
        return a.reshape(-1, P, *a.shape[1:]).swapaxes(0, 1)

    x = np.concatenate([x_prompt.reshape(TP, D), x_sample.reshape(TS, D)]).T
    c = np.pad(np.concatenate([c_prompt, c_sample]).T, ((0, 0), (0, 32 - NSEQ)))
    conv = np.pad(tiles(state_conv[0].transpose(2, 0, 1)), ((0, 0), (0, 0), (0, 0), (0, NL)))
    pool = np.pad(tiles(state_pool[0].transpose(2, 0, 1)), ((0, 0), (0, 0), (0, 0), (1, NL))).swapaxes(0, 1)
    params = np.concatenate(
        [tiles(v[0]) for v in (b_ada, g_norm1, g_norm2)] + [tiles(g_final)] + [tiles(v[0]) for v in (g_v, pool_scale)]
        + [tiles(conv_w[0].T).reshape(P, -1)], axis=1)
    inv = np.array([[1.0 / min(t + 1, 2 << g) for t in range(16)] for g in range(NPAR)], np.float32)
    inv = np.broadcast_to(inv, (P, NPAR, 16))
    w_t = w_in[0].reshape(KT, P, -1, P).transpose(2, 1, 0, 3)
    bg, cg, hc, pl, u, v = (w_t[WT * k:WT * k + WT] for k in range(6))
    w_mix = np.concatenate([np.stack([cg, hc, bg, pl], axis=1).reshape(4 * WT, P, KT, P), v, u])
    w_gt = w_t[MIX_TILES:].reshape(3, KT, P, KT, P).swapaxes(0, 1).reshape(3 * KT, P, KT, P)
    w_brt = w_br[0].reshape(3 * WT, P, KT, P).transpose(2, 1, 0, 3)
    w_ot = w_o[0].reshape(KT, P, KT, P).transpose(2, 1, 0, 3)
    pw = pool_w[0].reshape(NPAR, 2, P, 2, P).transpose(2, 0, 1, 3, 4)
    arrays = {
        "x": tiles(x), "c": tiles(c), "conv": conv, "pool": pool, "params": params, "inv": inv, "w_ada": w_ada[0],
        "w_mix": w_mix, "w_gt": w_gt, "w_br": w_brt, "w_o": w_ot, "pool_w": pw, "w_s": w_s[0].transpose(2, 0, 1),
        "b_s": b_s[0], "w_r": tiles(np.pad(np.concatenate([w_rg[0], w_re[0]], axis=1), ((0, 0), (0, 32 - NR)))),
        "b_r": np.concatenate([b_rg[0], b_re[0]]), "w_gate": w_gate[0], "w_up": w_up[0], "w_down": w_down[0],
    }
    arrays = {f"in_{k}": np.ascontiguousarray(a) for k, a in arrays.items()}
    outs = {"y": (P, KT, T), "conv_state": (P, WT, 1 + NB, 2), "pool_state": (WT, P, (1 + NB) * PST), "v": (P, WT, TS)}

    nc = bacc.Bacc("TRN2", target_bir_lowering=False, num_devices=1)
    args = [nc.dram_tensor(k, a.shape, mybir.dt.from_np(a.dtype), kind="ExternalInput").ap() for k, a in arrays.items()]
    args += [nc.dram_tensor(f"out_{k}", s, F32, kind="ExternalOutput").ap() for k, s in outs.items()]
    build(nc, *args)
    got = run_bass_kernel_spmd(nc, [arrays], core_ids=[0]).results[0]

    y = got["out_y"].transpose(2, 1, 0).reshape(T, D)
    conv = got["out_conv_state"].transpose(2, 3, 1, 0).reshape(1 + NB, 2, W)
    pool = got["out_pool_state"].reshape(WT, P, 1 + NB, PST).transpose(2, 3, 0, 1).reshape(1 + NB, PST, W)
    v = got["out_v"].transpose(2, 1, 0).reshape(1, NB, NL, W)
    return (y[:TP].reshape(1, TP, D), y[TP:].reshape(NB, NL, D), conv[:1][None], pool[:1][None], conv[1:][None],
            pool[1:][None], v)
```

```python
from contextlib import ExitStack

import concourse.bass as bass
from concourse import mybir
from concourse.bass import ds

F32 = mybir.dt.float32
F32R = mybir.dt.float32r
I32 = mybir.dt.int32
ALU = mybir.AluOpType
ACT = mybir.ActivationFunctionType
AX_X = mybir.AxisListType.X

P = 128
D = 2048
KT = D // P
TP = 256
NB, NL = 8, 4
TS = NB * NL
T = TP + TS
TT = [(0, P), (P, P), (TP, TS)]
NSEQ = 1 + NB
W = D // 2
WT = W // P
NPAR = 4
PST = 15
HALF = 8
NSPL = 3
NE, EPG, NG = 16, 4, 4
NR = NG + NE
FF = D // 4
FT = FF // P
CAP = 64
TLO_A = 1536
EPS = 1e-6
BIG = 3.0e38

KB = 1024
SQ_BEFORE = 5
ADA1_BLOCKS = 8
ADA_CHUNKS = 4
MIX_TILES = 48
MIX_RING = 6
MIX_IT = MIX_TILES // MIX_RING
MIX_HALVES = 2 * MIX_TILES
GATE_HALVES = 9
WO_BASE = MIX_HALVES + KT * GATE_HALVES
WO_HALVES = 2 * KT
ALL_HALVES = WO_BASE + WO_HALVES

C_BADA, C_G1, C_G2, C_GF, C_GV, C_PS, C_CW = 0, 96, 112, 128, 144, 152, 160
N_PAR = 184
SH1, SC1, GT1, SH2, SC2, GT2 = (KT * i for i in range(6))


class Tally:

    def __init__(self, eng, sem):
        self.eng, self.sem, self.n, self.at = eng, sem, 0, None

    def loop(self, reg, per):
        self.at, self.reg, self.per, self.k = self.n, reg, per, 0

    def end(self, count):
        assert self.k == self.per, (self.k, self.per)
        self.n, self.at = self.at + self.per * count, None

    def link(self, ins):
        ins.then_inc(self.sem, 1)
        self.after()

    def after(self):
        if self.at is None:
            self.n += 1
            self.eng.wait_ge(self.sem, self.n)
        else:
            self.k += 1
            self.eng.wait_ge(self.sem, self.reg * self.per + (self.at + self.k))


def build(nc, x_in, c_in, conv_in, pool_in, par_in, inv_in, w_ada, w_mix, w_gt, w_br, w_o, pool_w, w_s, b_s,
          w_r, b_r, w_gate, w_up, w_down, y_out, conv_out, pool_out, v_out):
    ctx = ExitStack()
    with ctx:
        base = (nc.sbuf_base + 31) // 32 * 32

        def at(name, off, shape, dt=F32):
            return nc.alloc_sbuf_tensor_at(name, shape, dt, offset=base + off)

        def size(shape):
            n = 4
            for s in shape[1:]:
                n *= s
            return n

        def region(off, end, *parts):
            out = []
            for name, shape, dt in parts:
                out.append(at(name, off, shape, dt))
                off += (size(shape) + 31) // 32 * 32
            assert off <= end, (parts[0][0], off, end)
            return out

        UNITS = [(t_, q) for q in range(4) for t_ in range(3)]
        BANK_OF = (2, 3, 4, 5, 6, 7, 4, 5, 6, 7, 2, 3)
        BY_GPSIMD = (0, 2, 4, 7)

        o_m = 52 * KB
        o_s = o_m + KT * T * 4
        o_h = o_s + 2 * NSPL * HALF * P * 4 + 2 * KB
        o_y = o_h + 2 * KT * T * 4
        o_p = o_y + 3 * KT * T * 4
        o_end = 229344 - base

        ring8 = [at(f"ring{k}", 8 * KB * k, [P, 4, 512]) for k in range(12)]
        mixw = [at(f"mixw{k}", 8 * KB * k, [P, KT, P]) for k in range(MIX_RING)]
        brw = at("brw", 24 * KB, [P, 3 * WT, P])
        adaw = [at(f"adaw{k}", (36 + 8 * k) * KB, [P, 4, 512]) for k in range(2)]
        dring = [at(f"dring{k}", 8 * KB * k, [P, D]) for k in range(12)]

        wst, = region(48 * KB, 52 * KB, ("wst", [P, WT, P], F32))
        merged, = region(o_m, o_s, ("merged", [P, KT, T], F32))
        o_x = o_m
        zzs, cst, ctmp, pp, pa, pb_, pps0, pps1, pst0, pst1 = region(
            o_x, o_x + 3 * 4 * KB,
            ("zzs", [P, WT, NB, 6], F32), ("cst", [P, WT, 1 + NB, 2], F32), ("ctmp", [P, T], F32),
            ("pp", [P, 16 + TP], F32),
            ("pa", [P, 16 + TP + NB * 20], F32), ("pb_", [P, 16 + TP + NB * 20], F32),
            ("pps0", [P, NB, 20], F32), ("pps1", [P, NB, 20], F32),
            ("pst0", [P, (1 + NB) * PST], F32), ("pst1", [P, (1 + NB) * PST], F32))
        pps, pst = [pps0, pps1], [pst0, pst1]
        vsq, = region(o_x, o_x + 12 * KB, ("vsq", [P, WT, T], F32))
        vtok, = region(o_x, o_x + 12 * KB, ("vtok", [P, 3, W], F32))
        bd, bs = region(o_x + 12 * KB, o_s, ("bd", [TS, WT, TS], F32), ("bs", [P, WT, P], F32))
        wh, wl = region(o_s, o_h, ("wh", [P, NSPL, HALF, P], F32R), ("wl", [P, NSPL, HALF, P], F32R))
        hh, hl = region(o_h, o_y, ("hh", [P, KT, T], F32R), ("hl", [P, KT, T], F32R))
        mh, ml = region(o_h, o_y, ("mh", [P, KT, T], F32R), ("ml", [P, KT, T], F32R))
        proj, = region(o_y, o_p, ("proj", [P, MIX_TILES, T], F32))
        ysp, = region(o_y, o_p, ("ysp", [P, MIX_TILES, T], F32R))
        xa, sq1 = region(o_y, o_p, ("xa", [P, KT, T], F32), ("sq1", [P, KT, T], F32))
        x1, = region(o_y, o_p, ("x1", [P, KT, T], F32))
        h2, = region(o_y + 2 * KT * T * 4, o_p, ("h2", [P, KT, T], F32))
        thi, yhi, sT0, tlo_a = region(
            o_h, o_y, ("thi", [P, 3, D], F32R), ("yhi", [P, D // 2], F32R), ("sT0", [P, T], F32R),
            ("tlo_a", [P, TLO_A], F32R))
        sq4, = region(o_h, o_y, ("sq4", [P, KT, T], F32))
        tlo, gus = region(o_y + KT * T * 4, o_y + 2 * KT * T * 4, ("tlo", [P, 2, D], F32R), ("gus", [P, FF], F32))
        xg, hid, sg = region(o_y + 2 * KT * T * 4, o_p, ("xg", [P, KT, EPG * CAP], F32), ("hid", [P, FT, CAP], F32),
                             ("sg", [P, FT, CAP], F32))
        lasting = (
            ("wr", [P, KT, 32], F32), ("mod", [P, 6 * KT, NSEQ], F32), ("par", [P, N_PAR], F32), ("ident", [P, P], F32),
            ("ones", [P, P], F32), ("tri", [P, P], F32), ("iota", [P, CAP], F32), ("sel", [P, NR], F32),
            ("w4", [P, 4], F32), ("br", [P, NR], F32), ("valid", [P, 3], F32), ("lg", [P, 3, NR], F32),
            ("mk", [P, 3, NE], F32), ("cb", [P, 3, NE], F32), ("rk", [P, 3, NE + EPG], F32),
            ("sc", [P, 3, 40], F32), ("rnd", [P, 8], I32))
        wr, mod, par, ident, ones, tri, iota, sel, w4, br, valid, lg, mk, cb, rk, sc, rnd = region(o_p, o_end, *lasting)
        scaled, wb = region(o_p, o_p + size([P, KT, 32]), ("scaled", [P, 2, 2, TS], F32),
                            ("wb", [P, EPG * CAP], F32))
        sT1, = region(o_p + size([P, KT, 32]), o_p + size([P, KT, 32]) + size([P, SH2, NSEQ]), ("sT1", [P, T], F32R))
        sT = [sT0, sT1]
        o_q = o_p + sum((size(shape) + 31) // 32 * 32 for _, shape, _ in lasting)
        cT, part = region(o_q, o_end, ("cT", [P, KT, 32], F32), ("part", [P, 512], F32))
        o_q2 = o_q + 4 * KB
        a1, a2, v_var, v_rs, v_t = region(
            o_q2, o_end, ("a1", [P, KT, NSEQ], F32), ("a2", [P, KT, NSEQ], F32), ("v_var", [P, T], F32),
            ("v_rs", [P, T], F32), ("v_t", [P, T], F32))
        sig, gt = region(o_q2, o_end, ("sig", [P, 3, T], F32), ("gt", [P, 2, T], F32))
        pw, inv = region(o_q2, o_end, ("pw", [P, NPAR, 2, 2, P], F32), ("inv", [P, NPAR, 16], F32))
        sqs, sqt, lgp = region(o_q, o_q2, ("sqs", [P, T], F32), ("sqt", [P, T], F32), ("lgp", [P, T], F32))
        oh, gc, tlo_b, ylo = region(o_q, o_end, ("oh", [P, 3, EPG * CAP], F32R), ("gc", [P, 3, EPG, CAP], F32),
                                    ("tlo_b", [P, D - TLO_A], F32R), ("ylo", [P, D // 2], F32R))
        pieces, = region(o_h + size([P, 3, D]), o_y, ("pieces", [P, 2, 512], F32))

        def rest_rows(t_, f0, n):
            if t_ < 2:
                return tlo[:, t_, f0:f0 + n]
            return tlo_a[0:TS, f0:f0 + n] if f0 < TLO_A else tlo_b[0:TS, f0 - TLO_A:f0 - TLO_A + n]

        bank = [ctx.enter_context(nc.psum_tensor(f"bank{k}", [P, 512], F32)) for k in range(8)]

        def sem(name):
            return ctx.enter_context(nc.semaphore(name))

        x_loaded, c_loaded, par_loaded, mixpar_loaded, x1_loaded = (
            sem(n) for n in ("x_loaded", "c_loaded", "par_loaded", "mixpar_loaded", "x1_loaded"))
        slot_loaded = [sem(f"slot_loaded{k}") for k in range(12)]
        mix_loaded = [sem(f"mix_loaded{k}") for k in range(MIX_RING)]
        br_loaded = sem("br_loaded")
        ada_loaded = [sem("ada_loaded0"), sem("ada_loaded1")]
        pps_loaded = [sem("pps_loaded0"), sem("pps_loaded1")]
        stores = sem("stores")
        pst_stored = [sem("pst_stored0"), sem("pst_stored1")]
        v_stored, conv_stored = sem("v_stored"), sem("conv_stored")
        w_used = sem("w_used")
        ada_used = sem("ada_used")
        ada_sel = sem("ada_sel")
        sums_done, pool_mm, vtr_done, mix_mm = (sem(n) for n in ("sums_done", "pool_mm", "vtr_done", "mix_mm"))
        logit_sums, logits_done, htr_done, rank_done = (
            sem(n) for n in ("logit_sums", "logits_done", "htr_done", "rank_done"))
        gath_done, tr_done, st_done, scat_done, moe_used, wb_done = (
            sem(n) for n in ("gath_done", "tr_done", "st_done", "scat_done", "moe_used", "wb_done"))
        sq_ready, std_ready, part_ready, hh_ready, hi_ready = (
            sem(n) for n in ("sq_ready", "std_ready", "part_ready", "hh_ready", "hi_ready"))
        hp_ready = sem("hp_ready")
        tile_saved = sem("tile_saved")
        yb_ready, vtok_a, sig_ready, mh_ready, thi_ready, exp_ready, lgp_ready = (
            sem(n) for n in ("yb_ready", "vtok_a", "sig_ready", "mh_ready", "thi_ready", "exp_ready", "lgp_ready"))
        xg_a, gu_saved, sg_ready, st_ready, yhi_ready = (
            sem(n) for n in ("xg_a", "gu_saved", "sg_ready", "st_ready", "yhi_ready"))
        dch, var_ready, mod_ready, h_ready, hl_ready, lo_ready, rs_ready = (
            sem(n) for n in ("dch", "var_ready", "mod_ready", "h_ready", "hl_ready", "lo_ready", "rs_ready"))
        vn_ready, vtok_d, yc_ready, merged_ready, ml_ready, x1_ready, tlo_ready, sq15_ready = (
            sem(n) for n in ("vn_ready", "vtok_d", "yc_ready", "merged_ready", "ml_ready", "x1_ready",
                             "tlo_ready", "sq15_ready"))
        exp_in, mk_ready, rounds_ready, oh_ready, gc_ready, xg_d, wb_ready = (
            sem(n) for n in ("exp_in", "mk_ready", "rounds_ready", "oh_ready", "gc_ready", "xg_d", "wb_ready"))
        sgw_ready, hid_ready, ylo_ready, scat_added, round_ready, y_ready = (
            sem(n) for n in ("sgw_ready", "hid_ready", "ylo_ready", "scat_added", "round_ready", "y_ready"))
        pch, consts, masked, ya_ready, d_ready, ybs_ready, ycs_ready, sqs_ready, hs_ready, tlp_ready, yp_ready = (
            sem(n) for n in ("pch", "consts", "masked", "ya_ready", "d_ready", "ybs_ready", "ycs_ready", "sqs_ready",
                             "hs_ready", "tlp_ready", "yp_ready"))

        def mix_unit(it, k):
            if k >= 2 * MIX_RING:
                it, k = it + 1, k - 2 * MIX_RING
            s, h = k // 2, k % 2
            return (mixw[s][:, HALF * h:HALF * (h + 1), :], mix_loaded[s], it * 16 + 16, it * (2 * MIX_RING) + k,
                    k % NSPL)

        def gate_unit(ot, k):
            if k >= GATE_HALVES:
                ot, k = ot + 1, k - GATE_HALVES
            u = ot * GATE_HALVES + (MIX_HALVES + k)
            if k < 6:
                return (mixw[k // 2][:, HALF * (k % 2):HALF * (k % 2 + 1), :], mix_loaded[k // 2],
                        ot * 16 + 16 * (MIX_IT + 1), u, k % NSPL)
            return brw[:, HALF * (k - 6):HALF * (k - 5), :], br_loaded, ot * 16 + 16, u, k % NSPL

        def wo_unit(v, k):
            if k >= 6:
                v, k = v + 1, k - 6
            s, h = k // 2, k % 2
            return (mixw[s][:, HALF * h:HALF * (h + 1), :], mix_loaded[s], v * 16 + 16 * (MIX_IT + KT + 1),
                    v * 6 + (WO_BASE + k), k % NSPL)

        def mix_then_gates(it, k):
            return mix_unit(it, k) if it < MIX_IT - 1 or k < 2 * MIX_RING else gate_unit(0, k - 2 * MIX_RING)

        def gates_then_wo(ot, k):
            return gate_unit(ot, k) if ot < KT - 1 or k < GATE_HALVES else wo_unit(0, k - GATE_HALVES)

        from_one = {
            "tensor": (ada_sel, tr_done, gath_done, st_done), "scalar": (part_ready, st_ready),
            "vector": (mod_ready, merged_ready, hid_ready, scat_added, ylo_ready)}

        def slot_uses(k):
            return 16 * (ADA1_BLOCKS // 2) if k < 8 else 0

        block = ctx.enter_context(nc.Block())

        @block.sync
        def _(sp):
            sp.dma_start(xa[:], x_in).then_inc(x_loaded, 16)
            sp.dma_start(cT[:], c_in).then_inc(c_loaded, 16)
            sp.dma_start(par[:], par_in).then_inc(par_loaded, 16)
            sp.dma_start(wr[:], w_r).then_inc(par_loaded, 16)
            sp.dma_start(br[:], b_r.partition_broadcast(P)).then_inc(par_loaded, 16)

            def ada_src(blk, j):
                return w_ada[blk, j:j + 1].rearrange("a b p k n -> p (a b k) n")

            for k in range(8):
                sp.dma_start(ring8[k][:], ada_src(slice(4 * (k // 4), 4 * (k // 4) + 1), k % 4))\
                    .then_inc(slot_loaded[k], 16)
            with sp.Fori(0, 3) as it:
                for k in range(8):
                    sp.wait_ge(ada_used, it * 8 + (k + 1))
                    sp.dma_start(ring8[k][:], ada_src(ds(it + (1 + 4 * (k // 4)), 1), k % 4))\
                        .then_inc(slot_loaded[k], 16)

            for k in range(MIX_RING):
                sp.wait_ge(ada_used, 24 + k + 1)
                sp.dma_start(mixw[k][:], w_mix[k]).then_inc(mix_loaded[k], 16)
            sp.wait_ge(ada_used, 32)
            sp.dma_start(wst[:], w_s).then_inc(mixpar_loaded, 16)
            sp.dma_start(bs[:], b_s.partition_broadcast(P)).then_inc(mixpar_loaded, 16)
            sp.dma_start(zzs[:], conv_in).then_inc(mixpar_loaded, 16)
            sp.wait_ge(h_ready, 4)
            sp.wait_ge(hp_ready, 4)
            sp.dma_start(pw[:], pool_w).then_inc(mixpar_loaded, 16)
            sp.dma_start(inv[:], inv_in).then_inc(mixpar_loaded, 16)
            sp.wait_ge(consts, 1)
            for b in range(NB):
                sp.dma_start(bd[NL * b:NL * b + NL, :, NL * b:NL * b + NL], w_s[0:NL, :, 0:NL])\
                    .then_inc(mixpar_loaded, 16)
            with sp.Fori(1, MIX_IT) as it:
                for k in range(MIX_RING):
                    sp.wait_ge(lo_ready, it * 12 + (2 * k + 2 - 12))
                    sp.dma_start(mixw[k][:], w_mix[ds(it * MIX_RING + k, 1)].rearrange("a p k c -> p (a k) c"))\
                        .then_inc(mix_loaded[k], 16)

            def gate_load(ot, n, at_value):
                sp.wait_ge(lo_ready, at_value)
                sp.dma_start(mixw[n][:], w_gt[ds(ot * 3 + n, 1)].rearrange("a p k c -> p (a k) c"))\
                    .then_inc(mix_loaded[n], 16)

            def br_load(ot):
                sp.wait_ge(lo_ready, ot * GATE_HALVES + MIX_HALVES)
                sp.dma_start(brw[:], w_br[ds(ot, 1)].rearrange("a p k c -> p (a k) c")).then_inc(br_loaded, 16)

            def ada_load(ot, j):
                sp.wait_ge(ada_used, ot * 4 + (32 + j - 1))
                sp.dma_start(adaw[j % 2][:], ada_src(ds(ot + ADA1_BLOCKS, 1), j))\
                    .then_inc(ada_loaded[j % 2], 16)

            for n in range(3):
                gate_load(0, n, 2 * (MIX_TILES - MIX_RING + n) + 2)
            br_load(0)
            sp.wait_ge(mix_mm, WT)
            ada_load(0, 0)
            ada_load(0, 1)
            with sp.Fori(0, KT - 1) as ot:
                ada_load(ot, 2)
                ada_load(ot, 3)
                for n in range(3):
                    gate_load(ot + 1, n, ot * GATE_HALVES + (MIX_HALVES + 2 * n + 2))
                ada_load(ot + 1, 0)
                ada_load(ot + 1, 1)
                br_load(ot + 1)
            ada_load(KT - 1, 2)
            ada_load(KT - 1, 3)

            def wo_load(v, s):
                sp.wait_ge(lo_ready, v * 6 + (WO_BASE + 2 * s + 2 - 6))
                sp.dma_start(mixw[s][:], w_o[ds(v * 3 + s, 1)].rearrange("a p k c -> p (a k) c"))\
                    .then_inc(mix_loaded[s], 16)

            for s in range(3):
                sp.wait_ge(lo_ready, WO_BASE - GATE_HALVES + 2 * s + 2)
                sp.dma_start(mixw[s][:], w_o[s]).then_inc(mix_loaded[s], 16)

            def expert_load(n, c):
                k = (c + 3) % 12
                e = ds(n, 1)
                if c < 8:
                    src = (w_up if c % 2 else w_gate)[e, c // 2:c // 2 + 1].rearrange("a b p k n -> p (a b k) n")
                    sp.dma_start(ring8[k][:], src).then_inc(slot_loaded[k], 16)
                else:
                    src = w_down[e].rearrange("a (k p) n -> p (a k) n", p=P)
                    sp.dma_start(dring[k][:], src[:, c - 8, :]).then_inc(slot_loaded[k], 16)

            sp.wait_ge(lo_ready, WO_BASE)
            sp.wait_ge(ada_used, 32 + 4 * KT)
            for c in range(3):
                expert_load(0, c)
            sp.wait_ge(merged_ready, KT + 1)
            sp.dma_start(x1[:], x_in).then_inc(x1_loaded, 16)
            sp.wait_ge(ml_ready, 4)
            for c in (3, 4):
                expert_load(0, c)
            with sp.Fori(1, 5) as v:
                for s in range(3):
                    wo_load(v, s)
            wo_load(5, 0)
            sp.wait_ge(lo_ready, ALL_HALVES)
            sp.wait_ge(w_used, ALL_HALVES + NSPL)
            for c in range(5, 12):
                expert_load(0, c)
            with sp.Fori(1, NE) as n:
                for c in range(12):
                    sp.wait_ge(moe_used, n * 12 + (c + 1 - 12))
                    expert_load(n, c)
            sp.wait_ge(rounds_ready, 1)
            rounds = sp.value_load(rnd[0:1, 0:1], min_val=1, max_val=-(-T // CAP))
            with sp.If(rounds > 1):
                with sp.Fori(1, rounds) as r:
                    with sp.Fori(0, NE) as n:
                        for c in range(12):
                            sp.wait_ge(moe_used, r * (12 * NE) + n * 12 + (c + 1 - 12))
                            expert_load(n, c)
            for q in range(4):
                sp.wait_ge(y_ready, q + 1)
                sp.wait_ge(yp_ready, q + 1)
                sp.dma_start(y_out[:, 4 * q:4 * q + 4, :], h2[:, 4 * q:4 * q + 4, :]).then_inc(stores, 16)
            sp.wait_ge(stores, 16 * 4)
            sp.wait_ge(conv_stored, 16)
            sp.wait_ge(v_stored, 16)
            for k in range(2):
                sp.wait_ge(pst_stored[k], 16 * WT // 2)

        @block.gpsimd
        def _(gp):
            chain = Tally(gp, pch)

            def select(m, pattern, base_, mult, op, fill):
                return gp.affine_select(out=m, in_=m, compare_op=op, fill=fill, base=base_, pattern=pattern,
                                        channel_multiplier=mult)

            gp.memset(bd[:], 0.0)
            gp.memset(ident[:], 0.0)
            gp.memset(sel[:], 0.0)
            gp.memset(tri[:], 1.0)
            gp.memset(valid[:], 1.0)
            chain.link(gp.memset(ones[:], 1.0))
            select(ident[:], [[-1, P]], 0, 1, ALU.not_equal, 1.0)
            for q in range(4):
                chain.link(select(sel[:], [[-1, NR]], -32 * q, 1, ALU.not_equal, 1.0))
            select(tri[:], [[1, P]], 0, -1, ALU.is_gt, 0.0)
            select(valid[:, 2:3], [[0, 1]], TS, -1, ALU.is_gt, 0.0)
            gp.iota(w4[:], [[-1, 4]], base=4, channel_multiplier=0, allow_small_or_imprecise_dtypes=True)
            gp.iota(iota[:], [[1, CAP]], base=0, channel_multiplier=0,
                    allow_small_or_imprecise_dtypes=True).then_inc(consts, 1)

            gp.wait_ge(mixpar_loaded, 16 * (5 + NB))
            select(wst[:], [[0, WT], [1, P]], 0, -1, ALU.is_ge, 0.0)
            select(bd[:], [[0, WT], [1, TS]], 0, -1, ALU.is_ge, 0.0).then_inc(masked, 1)

            def smp(ap):
                return ap[:, TP:T].rearrange("p (b l) -> p b l", l=NL)

            for f in range(2):
                gp.dma_start(pps[f][:], pool_in[f]).then_inc(pps_loaded[f], 16)
            chain.link(gp.memset(pp[:, 0:16], 0.0))
            NPP = 16 + TP
            for f in range(WT):
                cg, hc, bg, p_t = (proj[:, 4 * f + k, :] for k in range(4))
                zs = zzs[:, f]
                cw = [par[:, C_CW + 3 * f + k:C_CW + 3 * f + k + 1] for k in range(3)]
                gp.wait_ge(tile_saved, MIX_RING + 4 * f + 3)
                chain.link(gp.tensor_tensor(cg, cg, hc, ALU.mult))
                chain.link(gp.tensor_copy(zs[:, :, 2:6], smp(cg)))
                gp.tensor_copy(cst[:, f, 0, :], cg[:, TP - 2:TP])
                gp.tensor_copy(cst[:, f, 1:1 + NB, :], zs[:, :, 4:6])
                chain.link(gp.tensor_scalar(hc, cg, cw[2], 0.0, ALU.mult, ALU.add))
                for k in (1, 0):
                    d = 2 - k
                    gp.tensor_scalar(smp(ctmp), zs[:, :, k:k + NL], cw[k], 0.0, ALU.mult, ALU.add)
                    chain.link(gp.tensor_scalar(ctmp[:, 0:TP - d], cg[:, 0:TP - d], cw[k], 0.0, ALU.mult, ALU.add))
                    gp.tensor_tensor(smp(hc), smp(hc), smp(ctmp), ALU.add)
                    chain.link(gp.tensor_tensor(hc[:, d:TP], hc[:, d:TP], ctmp[:, 0:TP - d], ALU.add))
                chain.link(gp.tensor_tensor(bg, bg, hc, ALU.mult))
                yh, yl = ysp[:, 4 * f, :], ysp[:, 4 * f + 1, :]
                chain.link(gp.tensor_copy(yh, bg))
                gp.tensor_tensor(yl, bg, yh.bitcast(F32), ALU.subtract).then_inc(ya_ready, 1)

                g, n = f // 2, f // 2 + 1
                p_s = smp(p_t)
                ps_ = pps[f % 2]
                st = pst[f % 2]
                gp.wait_ge(tile_saved, MIX_RING + 4 * f + 4)
                gp.wait_ge(pps_loaded[f % 2], 16 * (f // 2 + 1))
                gp.tensor_copy(pp[:, 16:NPP], p_t[:, 0:TP])
                chain.link(gp.tensor_copy(ps_[:, :, 16:20], p_s))
                if f >= 2:
                    gp.wait_ge(pst_stored[f % 2], 16 * (f // 2))
                gp.tensor_copy(st[:, 0:PST], p_t[:, TP - PST:TP])
                chain.link(gp.tensor_copy(st[:, PST:].rearrange("p (b l) -> p b l", l=PST), ps_[:, :, 5:20]))
                gp.dma_start(pool_out[f], st[:]).then_inc(pst_stored[f % 2], 16)
                src, src_s, bufs = pp[:], ps_[:], [pa, pb_]
                for k in range(n):
                    s_, lo = 1 << k, (1 << (k + 1)) - 1
                    dst = bufs[k % 2][:, 0:NPP]
                    dst_s = bufs[k % 2][:, NPP:].rearrange("p (b l) -> p b l", l=20)
                    gp.tensor_tensor(dst[:, lo:NPP], src[:, lo:NPP], src[:, lo - s_:NPP - s_], ALU.add)
                    chain.link(gp.tensor_tensor(dst_s[:, :, lo:20], src_s[:, :, lo:20], src_s[:, :, lo - s_:20 - s_],
                                                ALU.add))
                    src, src_s = dst, dst_s
                mean, mean_s = bufs[n % 2][:, 0:NPP], bufs[n % 2][:, NPP:].rearrange("p (b l) -> p b l", l=20)
                gp.tensor_scalar(mean[:, 32:NPP], src[:, 32:NPP], 1.0 / (1 << n), 0.0, ALU.mult, ALU.add)
                gp.tensor_tensor(mean[:, 16:32], src[:, 16:32], inv[:, g, :], ALU.mult)
                chain.link(gp.tensor_scalar(mean_s[:, :, 16:20], src_s[:, :, 16:20], 1.0 / (1 << n), 0.0,
                                            ALU.mult, ALU.add))
                chain.link(gp.tensor_tensor(p_t[:, 0:TP], mean[:, 16:NPP], pp[:, 16:NPP], ALU.subtract))
                gp.tensor_tensor(p_s, mean_s[:, :, 16:20], ps_[:, :, 16:20], ALU.subtract).then_inc(d_ready, 1)
                gp.wait_ge(d_ready, f + 1)
                if f + 2 < WT:
                    gp.dma_start(ps_[:], pool_in[f + 2]).then_inc(pps_loaded[f % 2], 16)
            gp.dma_start(conv_out, cst[:]).then_inc(conv_stored, 16)

            gp.wait_ge(vn_ready, WT)
            gp.dma_start(v_out, proj[:, 4 * WT:5 * WT, TP:T]).then_inc(v_stored, 16)

            for f in range(WT):
                gp.wait_ge(yb_ready, f + 1)
                gp.wait_ge(pool_mm, min(WT, 2 * (f // 2) + 2))
                gp.tensor_copy(ysp[:, 4 * f + 3, :], proj[:, 4 * f + 2, :]).then_inc(ybs_ready, 1)
                gp.wait_ge(ybs_ready, 2 * f + 1)
                gp.tensor_tensor(ysp[:, 4 * f + 2, :], proj[:, 4 * f + 2, :],
                                 ysp[:, 4 * f + 3, :].bitcast(F32), ALU.subtract).then_inc(ybs_ready, 1)
            gp.wait_ge(v_stored, 16)
            gp.wait_ge(vtr_done, 6)
            for f in range(WT):
                gp.wait_ge(yc_ready, f + 1)
                gp.tensor_copy(ysp[:, 4 * WT + f, :], proj[:, 5 * WT + f, :]).then_inc(ycs_ready, 1)
                gp.wait_ge(ycs_ready, 2 * f + 1)
                gp.tensor_tensor(ysp[:, 5 * WT + f, :], proj[:, 5 * WT + f, :],
                                 ysp[:, 4 * WT + f, :].bitcast(F32), ALU.subtract).then_inc(ycs_ready, 1)

            gp.wait_ge(ada_sel, ADA1_BLOCKS + KT + 1)
            for f in range(KT - 1):
                gp.wait_ge(x1_ready, 3 + f + 1)
                chain.link(gp.tensor_tensor(sqt[:] if f else sqs[:], x1[:, f, :], x1[:, f, :], ALU.mult))
                if f:
                    last = gp.tensor_tensor(sqs[:], sqs[:], sqt[:], ALU.add)
                    chain.link(last) if f < KT - 2 else last.then_inc(sqs_ready, 1)
            gp.wait_ge(rs_ready, 1)
            hs = h2[:, :, TP:T]
            gp.tensor_tensor(hs, hs, v_rs[:, TP:T].unsqueeze(1).broadcast_to([P, KT, TS]), ALU.mult)\
                .then_inc(hs_ready, 1)
            hs4 = hs.rearrange("p f (b l) -> p f b l", l=NL)
            gp.wait_ge(hs_ready, 1)
            gp.tensor_tensor(hs4, hs4, mod[:, SH2:SH2 + KT, 1:NSEQ].unsqueeze(3).broadcast_to([P, KT, NB, NL]),
                             ALU.add).then_inc(hs_ready, 1)
            for k, u in enumerate(BY_GPSIMD):
                t_, q = UNITS[u]
                n = TT[t_][1]
                piece = pieces[0:n, k % 2, :]
                gp.wait_ge(thi_ready, u + 1)
                gp.tensor_copy(thi[0:n, t_, 512 * q:512 * q + 512], piece).then_inc(tlp_ready, 1)
                gp.wait_ge(tlp_ready, 2 * k + 1)
                gp.tensor_tensor(rest_rows(t_, 512 * q, 512), piece, thi[0:n, t_, 512 * q:512 * q + 512].bitcast(F32),
                                 ALU.subtract).then_inc(tlp_ready, 1)
            gp.wait_ge(tlp_ready, 2 * len(BY_GPSIMD))
            gp.memset(yhi[:].bitcast(F32), 0.0).then_inc(tlp_ready, 1)
            for j in range(8):
                gp.wait_ge(sq_ready, SQ_BEFORE + 2 * j + 2)
                gp.tensor_tensor(sq4[:, j, :], sq4[:, j, :], sq4[:, 8 + j, :], ALU.add).then_inc(sqs_ready, 1)
            for f in range(3, KT, 4):
                gain = par[:, C_GF + f:C_GF + f + 1]
                chain.link(gp.tensor_scalar(h2[:, f, :], x1[:, f, :], gain, 0.0, ALU.mult, ALU.add))
            gp.wait_ge(rs_ready, 2)
            for f in range(3, KT, 4):
                gp.tensor_tensor(h2[:, f, :], h2[:, f, :], v_rs[:], ALU.mult).then_inc(yp_ready, 1)

        @block.scalar
        def _(act):
            act.sem_inc(tile_saved, MIX_RING)
            act.sem_inc(sig_ready, 3)
            for s in from_one["scalar"]:
                act.sem_inc(s, 1)

            def split_hi(unit):
                src, loaded, value, u, b = unit
                act.wait_ge(loaded, value)
                act.wait_ge(w_used, u + 1)
                act.activation(wh[:, b], src, ACT.Copy).then_inc(hi_ready, 1)

            def root(n):
                act.wait_ge(var_ready, n)
                act.activation(v_rs[:], v_var[:], ACT.Sqrt).then_inc(std_ready, 1)

            def save_part(n):
                act.wait_ge(ada_used, n * 4 + 4)
                act.wait_ge(ada_sel, n + 1)
                act.activation(part[:], bank[6][:], ACT.Copy).then_inc(part_ready, 1)

            def modulate(x, a, shift, q, n):
                act.wait_ge(h_ready, n)
                for f in (4 * q, 4 * q + 2):
                    last = act.activation(x[:, f, 0:TP], x[:, f, 0:TP], ACT.Identity, scale=a[:, f, 0:1],
                                          bias=mod[:, shift + f, 0:1])
                last.then_inc(hp_ready, 1)

            act.wait_ge(x_loaded, 16)
            for q in range(4):
                act.activation(sq1[:, 4 * q:4 * q + 4, :], xa[:, 4 * q:4 * q + 4, :], ACT.Square).then_inc(sq_ready, 1)
            root(1)
            for q in range(4):
                save_part(2 * q)
                save_part(2 * q + 1)
                modulate(xa, a1, SH1, q, q + 1)
                act.wait_ge(hp_ready, q + 1)
                act.activation(hh[:, 4 * q:4 * q + 4, :], xa[:, 4 * q:4 * q + 4, :], ACT.Copy).then_inc(hh_ready, 1)
            for k in range(NSPL):
                split_hi(mix_unit(0, k))

            def mix_step(it, s, unit):
                split_hi(unit(it, 2 * s + 3))
                act.wait_ge(w_used, it * 12 + (2 * s + 2 + NSPL))
                act.activation(proj[:, ds(it * MIX_RING + s, 1), :].rearrange("p a t -> p (a t)"),
                               bank[s][:, 0:T], ACT.Copy).then_inc(tile_saved, 1)
                split_hi(unit(it, 2 * s + 4))

            with act.Fori(0, MIX_IT - 1) as it:
                for s in range(MIX_RING):
                    mix_step(it, s, mix_unit)

            def save_vtok(u):
                tt, half_ = u // 2, u % 2
                n = TT[tt][1]
                act.wait_ge(vtr_done, u + 1)
                act.activation(vtok[0:n, tt, 512 * half_:512 * half_ + 512], bank[6 + half_][0:n, :], ACT.Copy)\
                    .then_inc(vtok_a, 1)

            for s in range(MIX_RING):
                mix_step(MIX_IT - 1, s, mix_then_gates)
                if s == 0:
                    for f in range(WT):
                        act.wait_ge(pool_mm, f + 1)
                        act.activation(proj[:, 4 * f + 2, :], bank[6 + f % 2][:, 0:T], ACT.Copy,
                                       scale=par[:, C_PS + f:C_PS + f + 1]).then_inc(yb_ready, 1)
                    act.wait_ge(d_ready, WT)
                    for k in range(2):
                        act.wait_ge(pst_stored[k], 16 * WT // 2)
                    act.wait_ge(conv_stored, 16)
                    act.activation(vsq[:], proj[:, 4 * WT:5 * WT, :], ACT.Square).then_inc(sq_ready, 1)
                if s == 1:
                    root(2)
                if s >= 3:
                    save_vtok(2 * (s - 3))

            def merged_heads(q):
                act.wait_ge(merged_ready, 4 * q + 4 + 1)
                act.activation(mh[:, 4 * q:4 * q + 4, :], merged[:, 4 * q:4 * q + 4, :], ACT.Copy).then_inc(mh_ready, 1)

            def gates_step(ot, unit):
                for n in range(3):
                    split_hi(unit(ot, 2 * n + 3))
                    act.wait_ge(w_used, ot * GATE_HALVES + (MIX_HALVES + 2 * n + 2 + NSPL))
                    act.wait_ge(merged_ready, ot + 1)
                    act.activation(sig[:, n, :], bank[n][:, 0:T], ACT.Sigmoid).then_inc(sig_ready, 1)
                    split_hi(unit(ot, 2 * n + 4))
                save_part(ot + ADA1_BLOCKS)
                for k in (9, 10, 11):
                    split_hi(unit(ot, k))

            with act.Fori(0, KT - 1) as ot:
                gates_step(ot, gate_unit)
            gates_step(KT - 1, gates_then_wo)
            for q in range(3):
                merged_heads(q)
            merged_heads(3)
            with act.Fori(0, 4) as v:
                for k in range(3, 9):
                    split_hi(wo_unit(v, k))
            for k in range(3, 8):
                split_hi(wo_unit(4, k))

            root(3)
            for f in range(KT):
                act.wait_ge(h_ready, 4 + f + 1)
                act.activation(h2[:, f, 0:TP], h2[:, f, 0:TP], ACT.Identity, bias=mod[:, SH2 + f, 0:1])\
                    .then_inc(hp_ready, 1)
            act.wait_ge(logit_sums, 1)
            act.activation(lgp[:], bank[1][:, 0:T], ACT.Copy).then_inc(lgp_ready, 1)
            def take(u):
                t_, q = UNITS[u]
                n = TT[t_][1]
                act.wait_ge(htr_done, u + 1)
                b = bank[BANK_OF[u]]
                if u not in BY_GPSIMD:
                    last = act.activation(thi[0:n, t_, 512 * q:512 * q + 512], b[0:n, :], ACT.Copy)
                else:
                    k = BY_GPSIMD.index(u)
                    if k >= 2:
                        act.wait_ge(tlp_ready, 2 * k - 2)
                    last = act.activation(pieces[0:n, k % 2, :], b[0:n, :], ACT.Copy)
                last.then_inc(thi_ready, 1)

            for u in range(8):
                take(u)
            act.wait_ge(exp_in, 1)
            act.activation(sc[:, :, 31:36], sc[:, :, 26:31], ACT.Exp).then_inc(exp_ready, 1)
            for u in range(8, 12):
                take(u)

            def experts(i):
                for q in range(4):
                    act.wait_ge(gath_done, i * 8 + (2 * q + 1) + 1)
                    act.activation(xg[:, 4 * q:4 * q + 2, :],
                                   bank[4].rearrange("p (a n) -> p a n", a=2) if q % 2 == 0 else
                                   bank[6].rearrange("p (a n) -> p a n", a=2), ACT.Copy).then_inc(xg_a, 1)
                for e in range(EPG):
                    m1 = i * EPG + (e + 1)
                    act.wait_ge(moe_used, m1 * 12 - 4)
                    act.wait_ge(tr_done, i * EPG + e + 1)
                    act.activation(gus[:], bank[0][:], ACT.Copy).then_inc(gu_saved, 1)
                    act.wait_ge(st_done, m1 + 1)
                    act.activation(sT[e % 2][:], bank[0][:, 0:T], ACT.Copy).then_inc(st_ready, 1)
                    act.wait_ge(tr_done, m1 + 1)
                    act.wait_ge(hid_ready, i * EPG + e + 1)
                    act.activation(sg[:], bank[1].rearrange("p (f c) -> p f c", f=FT)[:, :, 0:CAP], ACT.Silu)\
                        .then_inc(sg_ready, 1)
                    act.wait_ge(moe_used, m1 * 12)
                    for b in range(2):
                        act.activation(yhi[:, 512 * b:512 * b + 512], bank[2 + b][:], ACT.Copy).then_inc(yhi_ready, 1)

            act.wait_ge(rounds_ready, 1)
            rounds = act.value_load(rnd[0:1, 0:1], min_val=1, max_val=-(-T // CAP))
            with act.Fori(0, rounds) as r:
                with act.Fori(0, NG) as g:
                    experts(r * NG + g)
            for j in range(8):
                act.wait_ge(scat_added, rounds * (8 * NE) + (j + 2))
                for f in (j, 8 + j):
                    act.activation(sq4[:, f, :], x1[:, f, :], ACT.Square).then_inc(sq_ready, 1)
            root(4)

        @block.vector
        def _(dve):
            chain = Tally(dve, dch)
            dve.sem_inc(x1_ready, 3)
            for s in from_one["vector"]:
                dve.sem_inc(s, 1)

            def tt(out, a, b, op):
                return dve.tensor_tensor(out, a, b, op)

            def split_lo(unit):
                src, _, _, u, b = unit
                dve.wait_ge(hi_ready, u + 1)
                tt(wl[:, b], src, wh[:, b].bitcast(F32), ALU.subtract).then_inc(lo_ready, 1)

            def rsqrt(sums, n, k):
                dve.tensor_scalar(v_var[:], sums, 1.0 / n, EPS, ALU.mult, ALU.add).then_inc(var_ready, 1)
                dve.wait_ge(std_ready, k)
                chain.link(dve.reciprocal(v_rs[:], v_rs[:]))
                chain.link(dve.scalar_tensor_tensor(v_t[:], v_rs[:], -0.5, v_rs[:], ALU.mult, ALU.mult))
                chain.link(tt(v_t[:], v_t[:], v_var[:], ALU.mult))
                chain.link(dve.scalar_tensor_tensor(v_rs[:], v_t[:], 1.5, v_rs[:], ALU.add, ALU.mult))

            def smp(ap):
                return ap.rearrange("p (b l) -> p b l", l=NL)

            def seqs(ap):
                return ap[:, 1:NSEQ].unsqueeze(2).broadcast_to([P, NB, NL])

            def save_mod(n, chunk):
                dve.wait_ge(ada_sel, n + 2)
                bias = par[:, ds(chunk, 4)].unsqueeze(2).broadcast_to([P, 4, NSEQ])
                got = bank[7][:, 0:4 * NSEQ].rearrange("p (c s) -> p c s", s=NSEQ)
                tt(mod[:, ds(chunk, 4), :], got, bias, ALU.add).then_inc(mod_ready, 1)

            def scales(a, first, g, k0, n):
                chain.link(dve.scalar_tensor_tensor(
                    a[:, k0:k0 + n, :], mod[:, first + k0:first + k0 + n, :], 1.0,
                    par[:, g + k0:g + k0 + n].unsqueeze(2).broadcast_to([P, n, NSEQ]), ALU.add, ALU.mult))

            def modulate(x, a, shift, q):
                sl = slice(4 * q, 4 * q + 4)

                def seqs4(ap):
                    return ap[:, :, 1:NSEQ].unsqueeze(3).broadcast_to([P, 4, NB, NL])

                xs = x[:, sl, TP:T].rearrange("p f (b l) -> p f b l", l=NL)
                chain.link(tt(xs, xs, seqs4(a[:, sl, :]), ALU.mult))
                for f in (4 * q + 1, 4 * q + 3):
                    dve.tensor_scalar(x[:, f, 0:TP], x[:, f, 0:TP], a[:, f, 0:1], mod[:, shift + f, 0:1], ALU.mult,
                                      ALU.add)
                tt(xs, xs, seqs4(mod[:, shift + 4 * q:shift + 4 * q + 4, :]), ALU.add).then_inc(h_ready, 1)

            dve.wait_ge(sums_done, 1)
            rsqrt(bank[0][:, 0:T], D, 1)
            chain.link(tt(xa[:], xa[:], v_rs[:].unsqueeze(1).broadcast_to([P, KT, T]), ALU.mult))
            dve.wait_ge(par_loaded, 48)
            for q in range(4):
                save_mod(2 * q, SH1 + 4 * q)
                save_mod(2 * q + 1, SC1 + 4 * q)
                dve.wait_ge(mod_ready, 2 * q + 3)
                scales(a1, SC1, C_G1, 4 * q, 4)
                modulate(xa, a1, SH1, q)
                dve.wait_ge(hh_ready, q + 1)
                sl = slice(4 * q, 4 * q + 4)
                tt(hl[:, sl, :], xa[:, sl, :], hh[:, sl, :].bitcast(F32), ALU.subtract).then_inc(hl_ready, 1)
            for k in range(NSPL):
                split_lo(mix_unit(0, k))
            with dve.Fori(0, MIX_IT - 1) as it:
                for k in range(3, 15):
                    split_lo(mix_unit(it, k))
            for s in range(MIX_RING):
                for k in (2 * s + 3, 2 * s + 4):
                    split_lo(mix_then_gates(MIX_IT - 1, k))
                if s == 1:
                    dve.wait_ge(sums_done, 2)
                    rsqrt(bank[7][:, 0:T], W, 2)
                    for f in range(WT):
                        v = proj[:, 4 * WT + f, :]
                        dve.scalar_tensor_tensor(v, v, par[:, C_GV + f:C_GV + f + 1], v_rs[:], ALU.mult, ALU.mult)\
                            .then_inc(vn_ready, 1)
                if s >= 3:
                    u = 2 * (s - 3) + 1
                    n = TT[u // 2][1]
                    dve.wait_ge(vtr_done, u + 1)
                    dve.tensor_copy(vtok[0:n, u // 2, 512:1024], bank[7][0:n, :]).then_inc(vtok_d, 1)
            for h in range(WT):
                dve.wait_ge(mix_mm, h + 1)
                b = bank[4 + h % 4]
                u = proj[:, 5 * WT + h, :]
                tt(b[:, 0:TP].rearrange("p (n t) -> p n t", n=2), b[:, 0:TP].rearrange("p (n t) -> p n t", n=2),
                   bs[:, h, :].unsqueeze(1).broadcast_to([P, 2, P]), ALU.add)
                chain.link(tt(smp(b[:, TP:T]), smp(b[:, TP:T]), bs[:, h, 0:NL].unsqueeze(1).broadcast_to([P, NB, NL]),
                              ALU.add))
                tt(u, b[:, 0:T], u, ALU.mult).then_inc(yc_ready, 1)

            def merged_rests(q):
                dve.wait_ge(mh_ready, q + 1)
                sl = slice(4 * q, 4 * q + 4)
                tt(ml[:, sl, :], merged[:, sl, :], mh[:, sl, :].bitcast(F32), ALU.subtract).then_inc(ml_ready, 1)

            def gates_step(ot, unit):
                split_lo(unit(ot, 3))
                for k in range(4, 10):
                    split_lo(unit(ot, k))
                br0 = ot * GATE_HALVES + (MIX_HALVES + 6 + NSPL)
                dst = merged[:, ds(ot, 1), :].rearrange("p a t -> p (a t)")
                dve.wait_ge(sig_ready, ot * 3 + (3 + 3))
                dve.wait_ge(w_used, br0 + 1)
                tt(gt[:, 0, :], bank[3][:, 0:T], sig[:, 0, :], ALU.mult)
                split_lo(unit(ot, 10))
                dve.wait_ge(w_used, br0 + 2)
                chain.link(tt(gt[:, 1, :], bank[4][:, 0:T], sig[:, 1, :], ALU.mult))
                chain.link(tt(dst, gt[:, 0, :], gt[:, 1, :], ALU.add))
                split_lo(unit(ot, 11))
                if unit is gates_then_wo:
                    for q in range(3):
                        merged_rests(q)
                save_mod(ot + ADA1_BLOCKS, ot * 4 + 2 * KT)
                dve.wait_ge(w_used, br0 + 3)
                chain.link(tt(gt[:, 0, :], bank[5][:, 0:T], sig[:, 2, :], ALU.mult))
                tt(dst, dst, gt[:, 0, :], ALU.add).then_inc(merged_ready, 1)

            with dve.Fori(0, KT - 1) as ot:
                chain.loop(ot, 3)
                gates_step(ot, gate_unit)
            chain.end(KT - 1)
            gates_step(KT - 1, gates_then_wo)
            merged_rests(3)

            def save_x1(v, s):
                o1 = ds(v * 3 + s, 1)
                gate1 = mod[:, ds(v * 3 + (GT1 + s), 1), :].rearrange("p a s -> p (a s)")
                dst = x1[:, o1, :].rearrange("p a t -> p (a t)")
                dve.wait_ge(w_used, v * 6 + (WO_BASE + 2 * s + 2 + NSPL))
                dve.scalar_tensor_tensor(dst[:, 0:TP], bank[s][:, 0:TP], gate1[:, 0:1], dst[:, 0:TP], ALU.mult, ALU.add)
                dve.wait_ge(x1_ready, v * 3 + (s + 3))
                chain.link(tt(smp(v_t[:, 0:TS]), smp(bank[s][:, TP:T]), seqs(gate1), ALU.mult))
                tt(dst[:, TP:T], dst[:, TP:T], v_t[:, 0:TS], ALU.add).then_inc(x1_ready, 1)

            dve.wait_ge(x1_loaded, 16)
            with dve.Fori(0, 4) as v:
                chain.loop(v, 3)
                for s in range(3):
                    for k in (2 * s + 3, 2 * s + 4):
                        split_lo(wo_unit(v, k))
                    save_x1(v, s)
            chain.end(4)
            for s in range(3):
                for k in (2 * s + 3, 2 * s + 4)[:1 if s == 2 else 2]:
                    split_lo(wo_unit(4, k))
                save_x1(4, s)
            save_x1(5, 0)
            dve.wait_ge(x1_ready, 3 + KT)

            tt(lgp[:], x1[:, KT - 1, :], x1[:, KT - 1, :], ALU.mult).then_inc(sq15_ready, 1)
            scales(a2, SC2, C_G2, 0, KT)
            chain.link(tt(h2[:, :, TP:T].rearrange("p f (b l) -> p f b l", l=NL),
                          x1[:, :, TP:T].rearrange("p f (b l) -> p f b l", l=NL),
                          a2[:, :, 1:NSEQ].unsqueeze(3).broadcast_to([P, KT, NB, NL]), ALU.mult))
            dve.wait_ge(sums_done, 3)
            rsqrt(bank[2][:, 0:T], D, 3)
            dve.sem_inc(rs_ready, 1)
            for f in range(KT):
                dve.scalar_tensor_tensor(h2[:, f, 0:TP], x1[:, f, 0:TP], a2[:, f, 0:1], v_rs[:, 0:TP], ALU.mult,
                                         ALU.mult).then_inc(h_ready, 1)

            def rest(u):
                t_, q = UNITS[u]
                n = TT[t_][1]
                dve.wait_ge(thi_ready, u + 1)
                head = thi[0:n, t_, 512 * q:512 * q + 512].bitcast(F32)
                tt(rest_rows(t_, 512 * q, 512), bank[BANK_OF[u]][0:n, :], head, ALU.subtract).then_inc(tlo_ready, 1)

            dve.memset(ylo[:].bitcast(F32), 0.0)
            dve.memset(sT[1][:].bitcast(F32), 0.0)
            chain.link(dve.memset(lg[:], 0.0))
            rest(1)
            dve.wait_ge(logits_done, 1)
            for t_, (_, n) in enumerate(TT):
                last = tt(lg[0:n, t_, :], bank[0][0:n, 32 * t_:32 * t_ + NR], br[0:n, :], ALU.add)
            chain.link(last)

            def col(a, n=1):
                return sc[:, :, a:a + n]

            def wide(ap, n):
                return ap.broadcast_to([P, 3, n])

            def reduce(out, src, op):
                chain.link(dve.tensor_reduce(out, src, AX_X, op))

            def top_of(src, m, eq, one, w):
                reduce(col(m), src, ALU.max)
                chain.link(tt(col(eq, 4), src, wide(col(m), 4), ALU.is_equal))
                chain.link(tt(col(eq, 4), col(eq, 4), w4[:].unsqueeze(1).broadcast_to([P, 3, 4]), ALU.mult))
                reduce(col(w), col(eq, 4), ALU.max)
                chain.link(tt(col(one, 4), col(eq, 4), wide(col(w), 4), ALU.is_equal))

            G_MAX, EQ, OHG, FIRST, SEL, M1, OH1, M2, OH2 = 0, 1, 5, 9, 10, 14, 15, 19, 20
            top_of(lg[:, :, 0:4], G_MAX, EQ, OHG, FIRST)
            chain.link(tt(col(26, 4), lg[:, :, 0:4], wide(col(G_MAX), 4), ALU.subtract))
            by_group = mk[:].rearrange("p t (g j) -> p t g j", g=NG)

            def spread(dst, four):
                dve_ = dst.rearrange("p t (g j) -> p t g j", g=NG)
                return tt(dve_, col(OHG, 4).unsqueeze(3).broadcast_to([P, 3, NG, EPG]),
                          four.unsqueeze(2).broadcast_to([P, 3, NG, EPG]), ALU.mult)

            chain.link(tt(by_group, lg[:, :, 4:20].rearrange("p t (g j) -> p t g j", g=NG),
                          col(OHG, 4).unsqueeze(3).broadcast_to([P, 3, NG, EPG]), ALU.mult))
            reduce(col(SEL, 4), by_group.rearrange("p t g j -> p t j g"), ALU.add)
            top_of(col(SEL, 4), M1, EQ, OH1, FIRST)
            chain.link(dve.scalar_tensor_tensor(col(SEL, 4), col(OH1, 4), -BIG, col(SEL, 4), ALU.mult, ALU.add))
            top_of(col(SEL, 4), M2, EQ, OH2, FIRST)
            tt(col(30), col(M2), col(M1), ALU.subtract).then_inc(exp_in, 1)
            rest(3)
            rest(5)
            dve.wait_ge(exp_ready, 1)
            reduce(col(36), col(31, 4), ALU.add)
            chain.link(dve.tensor_scalar(col(37), col(35), 1.0, None, ALU.add))
            chain.link(tt(col(36), col(36), col(37), ALU.mult))
            chain.link(dve.reciprocal(col(36), col(36)))
            chain.link(tt(col(37), col(36), col(35), ALU.mult))
            chain.link(tt(col(EQ, 4), col(OH1, 4), wide(col(36), 4), ALU.mult))
            chain.link(tt(col(26, 4), col(OH2, 4), wide(col(37), 4), ALU.mult))
            chain.link(tt(col(EQ, 4), col(EQ, 4), col(26, 4), ALU.add))
            chain.link(tt(col(OH1, 4), col(OH1, 4), col(OH2, 4), ALU.add))
            chain.link(tt(col(OHG, 4), col(OHG, 4), valid[:].unsqueeze(2).broadcast_to([P, 3, 4]), ALU.mult))
            spread(mk[:], col(OH1, 4)).then_inc(mk_ready, 1)
            chain.link(spread(cb[:], col(EQ, 4)))
            rest(6)
            dve.wait_ge(rank_done, 1)
            before = bank[1][:, 0:3 * NE].rearrange("p (t e) -> p t e", e=NE)
            chain.link(dve.scalar_tensor_tensor(rk[:, :, 0:NE], before, 1.0, mk[:], ALU.add, ALU.mult))
            chain.link(dve.tensor_scalar(rk[:, :, 0:NE], rk[:, :, 0:NE], -1.0, None, ALU.add))
            dve.tensor_scalar(rk[:, :, NE:NE + EPG], rk[:, :, 0:EPG], -float(CAP), None, ALU.add)

            def one_hot(four):
                tt(oh[:].rearrange("p t (e c) -> p t e c", e=EPG),
                   iota[:].unsqueeze(1).unsqueeze(1).broadcast_to([P, 3, EPG, CAP]),
                   rk[:, :, four].unsqueeze(3).broadcast_to([P, 3, EPG, CAP]), ALU.is_equal).then_inc(oh_ready, 1)

            one_hot(slice(0, EPG))
            chain.link(dve.tensor_reduce(sc[:, 0, 8:8 + NE], bank[1][:, 64:64 + 3 * NE].rearrange(
                "p (t e) -> p e t", e=NE), AX_X, ALU.add))
            dve.tensor_scalar(sc[:, 0, 1:6], iota[:, 0:5], float(CAP), None, ALU.mult)
            chain.link(dve.tensor_reduce(sc[:, 0, 0:1], sc[:, 0, 8:8 + NE], AX_X, ALU.max))
            chain.link(tt(sc[:, 0, 1:6], sc[:, 0, 0:1].broadcast_to([P, 5]), sc[:, 0, 1:6], ALU.is_gt))
            chain.link(dve.tensor_reduce(sc[:, 0, 6:7], sc[:, 0, 1:6], AX_X, ALU.add))
            dve.tensor_copy(rnd[:, 0:1], sc[:, 0, 6:7]).then_inc(rounds_ready, 1)
            for u in range(8, 12):
                rest(u)

            def save_scat(j, total):
                dve.wait_ge(scat_done, total + (j + 1))
                b = 4 + 2 * (j % 2)
                for h in range(2):
                    last = tt(smp(scaled[:, j % 2, h, :]), smp(bank[b + h][:, TP:T]), seqs(mod[:, GT2 + 8 * h + j, :]),
                              ALU.mult)
                last.then_inc(dch, 1)
                for h in range(2):
                    f = 8 * h + j
                    dve.scalar_tensor_tensor(x1[:, f, 0:TP], bank[b + h][:, 0:TP], mod[:, GT2 + f, 0:1], x1[:, f, 0:TP],
                                             ALU.mult, ALU.add)
                chain.after()
                pair = x1[:].rearrange("p (h j) t -> p h j t", h=2)[:, :, j, TP:T]
                tt(pair, pair, scaled[:, j % 2], ALU.add).then_inc(scat_added, 1)

            def experts(i, g):
                chain.loop(i, 8 * EPG)
                four = ds(g * EPG, EPG)
                dve.wait_ge(oh_ready, i + 1)
                dve.wait_ge(st_done, i * EPG + 1)
                tt(gc[:], oh[:].bitcast(F32).rearrange("p t (e c) -> p t e c", e=EPG),
                   cb[:, :, four].unsqueeze(3).broadcast_to([P, 3, EPG, CAP]), ALU.mult).then_inc(gc_ready, 1)
                for q in range(4):
                    dve.wait_ge(gath_done, i * 8 + (2 * q + 2) + 1)
                    dve.tensor_copy(xg[:, 4 * q + 2:4 * q + 4, :],
                                    bank[5 if q % 2 == 0 else 7].rearrange("p (a n) -> p a n", a=2)).then_inc(xg_d, 1)
                dve.wait_ge(wb_done, i + 1)
                dve.tensor_copy(wb[:], bank[1][:, 0:EPG * CAP]).then_inc(wb_ready, 1)
                for e in range(EPG):
                    m1 = i * EPG + (e + 1)
                    for j in range(6):
                        save_scat(j, i * (8 * EPG) + 8 * e)
                    if e == 0:
                        dve.wait_ge(wb_ready, i + 1)
                    dve.wait_ge(sg_ready, m1)
                    tt(sg[:], sg[:], wb[:, CAP * e:CAP * e + CAP].unsqueeze(1).broadcast_to([P, FT, CAP]), ALU.mult)\
                        .then_inc(sgw_ready, 1)
                    dve.wait_ge(sgw_ready, m1)
                    tt(hid[:], sg[:], bank[1].rearrange("p (f c) -> p f c", f=FT)[:, :, CAP:2 * CAP], ALU.mult)\
                        .then_inc(hid_ready, 1)
                    for j in (6, 7):
                        save_scat(j, i * (8 * EPG) + 8 * e)
                    if e == EPG - 1:
                        dve.wait_ge(gc_ready, i + 1)
                        dve.wait_ge(st_done, m1 + 1)
                        one_hot(ds(g * EPG + EPG, EPG))
                    for b in range(2):
                        dve.wait_ge(yhi_ready, i * (2 * EPG) + (2 * e + b + 1))
                        tt(ylo[:, 512 * b:512 * b + 512], bank[2 + b][:], yhi[:, 512 * b:512 * b + 512].bitcast(F32),
                           ALU.subtract).then_inc(ylo_ready, 1)

            dve.wait_ge(rounds_ready, 1)
            rounds = dve.value_load(rnd[0:1, 0:1], min_val=1, max_val=-(-T // CAP))
            with dve.Fori(0, rounds) as r:
                with dve.Fori(0, NG) as g:
                    experts(r * NG + g, g)
                dve.wait_ge(oh_ready, r * NG + (NG + 1))
                dve.tensor_scalar(rk[:], rk[:], -float(CAP), None, ALU.add).then_inc(round_ready, 1)
                dve.wait_ge(round_ready, r + 1)
            chain.loop(rounds, 8 * EPG * NG)
            for j in range(8):
                save_scat(j, rounds * (8 * NE))

            dve.wait_ge(sums_done, 4)
            rsqrt(bank[0][:, 0:T], D, 4)
            dve.sem_inc(rs_ready, 1)
            for q in range(4):
                for f in range(4 * q, 4 * q + 3):
                    last = dve.scalar_tensor_tensor(h2[:, f, :], x1[:, f, :], par[:, C_GF + f:C_GF + f + 1], v_rs[:],
                                                    ALU.mult, ALU.mult)
                last.then_inc(y_ready, 1)

        @block.tensor
        def _(pe):
            pe.sem_inc(w_used, NSPL)
            for s in from_one["tensor"]:
                pe.sem_inc(s, 1)
            mm = pe.matmul

            def sums(src, n, b, q_of):
                for f in range(n):
                    if f % q_of == 0:
                        sums.quarter += 1
                        pe.wait_ge(sq_ready, sums.quarter)
                    last = mm(bank[b][:, 0:T], ones[:], src[:, f, :], start=f == 0, stop=f == n - 1)
                last.then_inc(sums_done, 1)

            sums.quarter = 0

            def ada_chunk(buf, j, loaded, value):
                pe.wait_ge(loaded, value)
                for q in range(4):
                    last = mm(bank[6][32 * q:32 * q + 32, :], cT[:, 4 * j + q, :], buf[:, q, :], start=j == 0,
                              stop=j == ADA_CHUNKS - 1, tile_position=(0, 32 * q))
                last.then_inc(ada_used, 1)

            def ada_select(n):
                pe.wait_ge(part_ready, n + 2)
                pe.wait_ge(mod_ready, n + 1)
                for c in range(4):
                    last = mm(bank[7][:, NSEQ * c:NSEQ * c + NSEQ], part[:, P * c:P * c + P], sel[:, 0:NSEQ],
                              start=True, stop=True)
                last.then_inc(ada_sel, 1)

            pe.wait_ge(consts, 1)
            sums(sq1, KT, 0, 4)
            pe.wait_ge(c_loaded, 16)
            with pe.Fori(0, ADA1_BLOCKS // 2) as it:
                for b in range(2):
                    n = it * 2 + b
                    pe.wait_ge(part_ready, n + 1)
                    for j in range(ADA_CHUNKS):
                        ada_chunk(ring8[4 * b + j], j, slot_loaded[4 * b + j], it * 16 + 16)
                    ada_select(n)

            def half(unit, b, hi, lo, first, start, stop):
                _, _, _, u, s = unit
                pe.wait_ge(lo_ready, u + 1)
                for k in range(HALF):
                    out = bank[b][:, 0:T]
                    mm(out, wh[:, s, k, :], hi[:, first + k, :], start=start and k == 0, stop=False)
                    mm(out, wh[:, s, k, :], lo[:, first + k, :], start=False, stop=False)
                    last = mm(out, wl[:, s, k, :], hi[:, first + k, :], start=False, stop=stop and k == HALF - 1)
                last.then_inc(w_used, 1)

            def tile(unit_of, it, k, b, hi, lo):
                half(unit_of(it, k), b, hi, lo, 0, True, False)
                half(unit_of(it, k + 1), b, hi, lo, HALF, False, True)

            def mix_tile(it, s):
                pe.wait_ge(tile_saved, it * MIX_RING + (s + 1))
                pe.wait_ge(hl_ready, 2)
                half(mix_unit(it, 2 * s), s, hh, hl, 0, True, False)
                pe.wait_ge(hl_ready, 4)
                half(mix_unit(it, 2 * s + 1), s, hh, hl, HALF, False, True)

            with pe.Fori(0, MIX_IT - 1) as it:
                for s in range(MIX_RING):
                    mix_tile(it, s)

            def vtr(u):
                tt, half_ = u // 2, u % 2
                c0, n = TT[tt]
                if tt >= 1:
                    pe.wait_ge(vtok_a if half_ == 0 else vtok_d, tt)
                for f in range(4):
                    last = mm(bank[6 + half_][0:n, P * f:P * f + P], proj[:, 4 * WT + 4 * half_ + f, c0:c0 + n],
                              ident[:], start=True, stop=True)
                last.then_inc(vtr_done, 1)

            for s in range(MIX_RING):
                mix_tile(MIX_IT - 1, s)
                if s == 0:
                    pe.wait_ge(masked, 1)
                    for f in range(WT):
                        g = f // 2
                        pe.wait_ge(d_ready, 2 * g + 2)
                        if f >= 2:
                            pe.wait_ge(yb_ready, f - 1)
                        for k in range(2):
                            last = mm(bank[6 + f % 2][:, 0:T], pw[:, g, k, f % 2, :], proj[:, 4 * (2 * g + k) + 3, :],
                                      start=k == 0, stop=k == 1)
                        last.then_inc(pool_mm, 1)
                if s == 1:
                    pe.wait_ge(yb_ready, WT)
                    sums(vsq, WT, 7, WT)
                if s == 3:
                    pe.wait_ge(vn_ready, WT)
                if s >= 3:
                    vtr(2 * (s - 3))
                    vtr(2 * (s - 3) + 1)
            pe.wait_ge(vtok_a, 3)
            pe.wait_ge(vtok_d, 3)
            for h in range(WT):
                b = bank[4 + h % 4]
                if h >= 4:
                    pe.wait_ge(yc_ready, h - 3)
                elif h < 2:
                    pe.wait_ge(tile_saved, MIX_RING + MIX_TILES)
                for c in range(2):
                    mm(b[:, P * c:P * c + P], vtok[:, c, P * h:P * h + P], wst[:, h, :], start=True, stop=True)
                mm(b[:, TP:T], vtok[0:TS, 2, P * h:P * h + P], bd[:, h, :], start=True, stop=True).then_inc(mix_mm, 1)

            def branch(ot, n):
                pe.wait_ge([ya_ready, ybs_ready, ycs_ready][n], [WT, 2 * WT, 2 * WT][n])
                first = ysp[:, 0:4 * WT, :].rearrange("p (f k) t -> p k f t", k=4)
                hi, lo = [(first[:, 0], first[:, 1]), (first[:, 3], first[:, 2]),
                          (ysp[:, 4 * WT:5 * WT, :], ysp[:, 5 * WT:6 * WT, :])][n]
                half(gate_unit(ot, 6 + n), 3 + n, hi, lo, 0, True, True)

            def gates_step(ot):
                for n in range(3):
                    pe.wait_ge(sig_ready, ot * 3 + (n + 1))
                    tile(gate_unit, ot, 2 * n, n, hh, hl)
                    if n == 0:
                        pe.wait_ge(part_ready, ot + ADA1_BLOCKS + 1)
                        for j in range(2):
                            ada_chunk(adaw[j], j, ada_loaded[j], ot * 32 + 16)
                for j in range(2, 4):
                    ada_chunk(adaw[j % 2], j, ada_loaded[j % 2], ot * 32 + 32)
                pe.wait_ge(merged_ready, ot + 1)
                for n in range(3):
                    branch(ot, n)
                    if n == 1:
                        ada_select(ot + ADA1_BLOCKS)

            pe.wait_ge(yc_ready, WT)
            with pe.Fori(0, KT) as ot:
                gates_step(ot)

            with pe.Fori(0, 5) as v:
                for s in range(3):
                    pe.wait_ge(x1_ready, v * 3 + (s + 1))
                    pe.wait_ge(ml_ready, 2)
                    half(wo_unit(v, 2 * s), s, mh, ml, 0, True, False)
                    pe.wait_ge(ml_ready, 4)
                    half(wo_unit(v, 2 * s + 1), s, mh, ml, HALF, False, True)
            pe.wait_ge(x1_ready, 16)
            tile(wo_unit, 5, 0, 0, mh, ml)

            pe.wait_ge(sqs_ready, 1)
            mm(bank[2][:, 0:T], ones[:], sqs[:], start=True, stop=False)
            pe.wait_ge(sq15_ready, 1)
            mm(bank[2][:, 0:T], ones[:], lgp[:], start=False, stop=True).then_inc(sums_done, 1)

            def logits(q):
                for c in range(4):
                    pe.wait_ge(hp_ready, 4 + 4 * q + c + 1)
                    last = mm(bank[1][32 * c:32 * c + 32, 0:T], wr[:, 4 * q + c, :], h2[:, 4 * q + c, :], start=q == 0,
                              stop=q == 3, tile_position=(0, 32 * c))
                if q == 3:
                    last.then_inc(logit_sums, 1)

            def pieces_read(n):
                pe.wait_ge(thi_ready, n)
                pe.wait_ge(tlo_ready, sum(u not in BY_GPSIMD for u in range(n)))

            def turn(units):
                for u in units:
                    t_, q = UNITS[u]
                    c0, n = TT[t_]
                    if u >= 6:
                        pieces_read(BANK_OF[:u].index(BANK_OF[u]) + 1)
                    for f in range(4):
                        last = mm(bank[BANK_OF[u]][0:n, P * f:P * f + P], h2[:, 4 * q + f, c0:c0 + n], ident[:],
                                  start=True, stop=True)
                    last.then_inc(htr_done, 1)

            pe.wait_ge(hs_ready, 2)
            for q in range(4):
                logits(q)
            turn((0,))
            pe.wait_ge(lgp_ready, 1)
            for t_, (c0, n) in enumerate(TT):
                last = mm(bank[0][0:n, 32 * t_:32 * t_ + NR], lgp[:, c0:c0 + n], sel[:], start=True, stop=True)
            last.then_inc(logits_done, 1)
            turn(range(1, 10))
            pe.wait_ge(mk_ready, 1)
            marks = mk[:].rearrange("p t e -> p (t e)")
            mm(bank[1][:, 0:3 * NE], tri[:], marks, start=True, stop=False)
            mm(bank[1][:, NE:3 * NE].rearrange("p (t e) -> p t e", e=NE), ones[:],
               mk[:, 0:1, :].broadcast_to([P, 2, NE]), start=False, stop=False)
            mm(bank[1][:, 2 * NE:3 * NE], ones[:], mk[:, 1, :], start=False, stop=True)
            mm(bank[1][:, 64:64 + 3 * NE], ones[:], marks, start=True, stop=True).then_inc(rank_done, 1)
            turn((10, 11))

            def scatter(j, e_before, total):
                b = 4 + 2 * (j % 2)
                pe.wait_ge(scat_added, total + max(j - 1, 0) + 1)
                for h in range(2):
                    rows = slice(64 * h, 64 * h + 64)
                    for part_, y in enumerate((yhi, ylo)):
                        last = mm(bank[b + h][:, 0:T], y[rows, P * j:P * j + P], sT[e_before % 2][rows, :],
                                  start=part_ == 0, stop=part_ == 1, tile_position=(64 * h, 0))
                last.then_inc(scat_done, 1)

            def experts(i):
                pe.wait_ge(oh_ready, i + 1)
                pe.wait_ge(scat_added, i * (8 * EPG) + 1)
                def gather(dp):
                    b = 4 + dp % 4
                    if dp >= 4:
                        pe.wait_ge(xg_d if dp % 2 else xg_a, i * 4 + (dp // 2 - 1))
                    for d in range(2):
                        f0 = P * (2 * dp + d)
                        for t_, (_, n) in enumerate(TT):
                            mm(bank[b][:, 256 * d:256 * d + 256], thi[0:n, t_, f0:f0 + P], oh[0:n, t_, :],
                               start=t_ == 0, stop=False)
                            last = mm(bank[b][:, 256 * d:256 * d + 256], rest_rows(t_, f0, P), oh[0:n, t_, :],
                                      start=False, stop=t_ == 2)
                    last.then_inc(gath_done, 1)

                for dp in range(4):
                    if dp == 2:
                        pieces_read(10)
                    gather(dp)
                for e in range(EPG):
                    m = i * EPG + e
                    slots = slice(CAP * e, CAP * e + CAP)
                    pe.wait_ge(st_ready, m + 1)
                    if e == 0:
                        pe.wait_ge(gc_ready, i + 1)
                        for t_, (_, n) in enumerate(TT):
                            last = mm(bank[1][:, 0:EPG * CAP], ones[0:n, :], gc[0:n, t_].rearrange("p e c -> p (e c)"),
                                      start=t_ == 0, stop=t_ == 2)
                        last.then_inc(wb_done, 1)
                    for c in range(4):
                        pe.wait_ge(slot_loaded[(2 * c + 3) % 12], m * 16 + (16 + slot_uses((2 * c + 3) % 12)))
                        pe.wait_ge(slot_loaded[(2 * c + 4) % 12], m * 16 + (16 + slot_uses((2 * c + 4) % 12)))
                        gate, up = ring8[(2 * c + 3) % 12], ring8[(2 * c + 4) % 12]
                        if e == 0:
                            pe.wait_ge(xg_a, i * 4 + (c + 1))
                            pe.wait_ge(xg_d, i * 4 + (c + 1))
                        for k in range(4):
                            kt = 4 * c + k
                            a = mm(bank[0][0:CAP, :], xg[:, kt, slots], gate[:, k, :], start=kt == 0, stop=kt == KT - 1,
                                   tile_position=(0, 0))
                            b = mm(bank[0][CAP:2 * CAP, :], xg[:, kt, slots], up[:, k, :], start=kt == 0,
                                   stop=kt == KT - 1, tile_position=(0, CAP))
                        a.then_inc(moe_used, 1)
                        b.then_inc(moe_used, 1)
                        if c == 0 and e == 0:
                            pieces_read(12)
                            pe.wait_ge(tlp_ready, 2 * len(BY_GPSIMD) + 1)
                            for dp in range(4, 8):
                                gather(dp)
                        if c == 1:
                            if e == 0:
                                pe.wait_ge(xg_a, i * 4 + 4)
                                pe.wait_ge(xg_d, i * 4 + 4)
                            pe.wait_ge(ylo_ready, 2 * m + 1)
                        for j in ((), (0, 1), (2, 3), (4,))[c]:
                            scatter(j, e + 1, m * 8)
                    scatter(5, e + 1, m * 8)
                    pe.wait_ge(gu_saved, m + 1)
                    for t_, (c0, n) in enumerate(TT):
                        for h in range(2):
                            last = mm(bank[0][CAP * h:CAP * h + CAP, c0:c0 + n], oh[0:n, t_, slots].bitcast(F32),
                                      ident[0:n, 0:n], start=True, stop=True, tile_position=(0, CAP * h))
                    last.then_inc(st_done, 1)
                    if e == 0:
                        pe.wait_ge(wb_ready, i + 1)
                    for f in range(FT):
                        last = mm(bank[1][:, P * f:P * f + P], gus[:, P * f:P * f + P], ident[:], start=True, stop=True)
                    last.then_inc(tr_done, 1)
                    for j in (6, 7):
                        scatter(j, e + 1, m * 8)
                    pe.wait_ge(hid_ready, m + 2)
                    for c in range(FT):
                        k = (c + 11) % 12
                        pe.wait_ge(slot_loaded[k], m * 16 + (16 + slot_uses(k)))
                        for b in range(2):
                            for h in range(2):
                                last = mm(bank[2 + b][CAP * h:CAP * h + CAP, :], hid[:, c, :],
                                          dring[k][:, 1024 * h + 512 * b:1024 * h + 512 * b + 512], start=c == 0,
                                          stop=c == FT - 1, tile_position=(0, CAP * h))
                        last.then_inc(moe_used, 1)

            pieces_read(8)
            pe.wait_ge(tlp_ready, 6)
            pe.wait_ge(rounds_ready, 1)
            rounds = pe.value_load(rnd[0:1, 0:1], min_val=1, max_val=-(-T // CAP))
            with pe.Fori(0, rounds) as r:
                with pe.Fori(0, NG) as g:
                    experts(r * NG + g)
            pe.wait_ge(ylo_ready, rounds * (2 * NE) + 1)
            for j in range(11):
                if j < 8:
                    scatter(j, NE - 1, rounds * (8 * NE))
                if j >= 3:
                    pe.wait_ge(sqs_ready, j - 3 + 2)
                    last = mm(bank[0][:, 0:T], ones[:], sq4[:, j - 3, :], start=j == 3, stop=j == 10)
            last.then_inc(sums_done, 1)


def kernel(x_prompt, x_sample, c_prompt, c_sample, state_conv, state_pool, w_ada, b_ada, g_norm1, w_in,
           conv_w, pool_w, pool_scale, g_v, w_s, b_s, w_br, w_o, g_norm2, w_rg, b_rg, w_re, b_re,
           w_gate, w_up, w_down, g_final):
    import numpy as np
    import concourse.bacc as bacc
    from concourse.bass_utils import run_bass_kernel_spmd

    (x_prompt, x_sample, c_prompt, c_sample, state_conv, state_pool, w_ada, b_ada, g_norm1, w_in, conv_w, pool_w,
     pool_scale, g_v, w_s, b_s, w_br, w_o, g_norm2, w_rg, b_rg, w_re, b_re, w_gate, w_up, w_down, g_final) = (
        np.asarray(a) for a in (
            x_prompt, x_sample, c_prompt, c_sample, state_conv, state_pool, w_ada, b_ada, g_norm1, w_in, conv_w, pool_w,
            pool_scale, g_v, w_s, b_s, w_br, w_o, g_norm2, w_rg, b_rg, w_re, b_re, w_gate, w_up, w_down, g_final))

    def tiles(a):
        return a.reshape(-1, P, *a.shape[1:]).swapaxes(0, 1)

    def chunks(a):
        return a.reshape(ADA_CHUNKS, 4, P, -1, 512).transpose(3, 0, 2, 1, 4)

    x = np.concatenate([x_prompt.reshape(TP, D), x_sample.reshape(TS, D)]).T
    c = np.pad(np.concatenate([c_prompt, c_sample]).T, ((0, 0), (0, 32 - NSEQ)))
    conv = np.pad(tiles(state_conv[0].transpose(2, 0, 1)), ((0, 0), (0, 0), (0, 0), (0, NL)))
    pool = np.pad(tiles(state_pool[0].transpose(2, 0, 1)), ((0, 0), (0, 0), (0, 0), (1, NL))).swapaxes(0, 1)
    params = np.concatenate(
        [tiles(v[0]) for v in (b_ada, g_norm1, g_norm2)] + [tiles(g_final)] + [tiles(v[0]) for v in (g_v, pool_scale)]
        + [tiles(conv_w[0].T).reshape(P, -1)], axis=1)
    inv = np.array([[1.0 / min(t + 1, 2 << g) for t in range(16)] for g in range(NPAR)], np.float32)
    inv = np.broadcast_to(inv, (P, NPAR, 16))
    w_t = w_in[0].reshape(KT, P, -1, P).transpose(2, 1, 0, 3)
    bg, cg, hc, pl, u, v = (w_t[WT * k:WT * k + WT] for k in range(6))
    w_mix = np.concatenate([np.stack([cg, hc, bg, pl], axis=1).reshape(4 * WT, P, KT, P), v, u])
    w_gt = w_t[MIX_TILES:].reshape(3, KT, P, KT, P).swapaxes(0, 1).reshape(3 * KT, P, KT, P)
    w_brt = w_br[0].reshape(3 * WT, P, KT, P).transpose(2, 1, 0, 3)
    w_ot = w_o[0].reshape(KT, P, KT, P).transpose(2, 1, 0, 3)
    pw = pool_w[0].reshape(NPAR, 2, P, 2, P).transpose(2, 0, 1, 3, 4)
    w_r = np.pad(np.concatenate([w_rg[0], w_re[0]], axis=1), ((0, 0), (0, 32 - NR)))
    experts_gate, experts_up = (np.stack([chunks(a)[0] for a in w[0]]) for w in (w_gate, w_up))
    arrays = {
        "x": tiles(x), "c": tiles(c), "conv": conv, "pool": pool, "params": params, "inv": inv,
        "w_ada": chunks(w_ada[0]), "w_mix": w_mix, "w_gt": w_gt, "w_br": w_brt, "w_o": w_ot, "pool_w": pw,
        "w_s": w_s[0].transpose(2, 0, 1), "b_s": b_s[0], "w_r": tiles(w_r),
        "b_r": np.concatenate([b_rg[0], b_re[0]]), "w_gate": experts_gate, "w_up": experts_up, "w_down": w_down[0],
    }
    arrays = {f"in_{k}": np.ascontiguousarray(a) for k, a in arrays.items()}
    outs = {"y": (P, KT, T), "conv_state": (P, WT, 1 + NB, 2), "pool_state": (WT, P, (1 + NB) * PST), "v": (P, WT, TS)}

    nc = bacc.Bacc("TRN2", target_bir_lowering=False, num_devices=1)
    args = [nc.dram_tensor(k, a.shape, mybir.dt.from_np(a.dtype), kind="ExternalInput").ap() for k, a in arrays.items()]
    args += [nc.dram_tensor(f"out_{k}", s, F32, kind="ExternalOutput").ap() for k, s in outs.items()]
    build(nc, *args)
    got = run_bass_kernel_spmd(nc, [arrays], core_ids=[0]).results[0]

    y = got["out_y"].transpose(2, 1, 0).reshape(T, D)
    conv = got["out_conv_state"].transpose(2, 3, 1, 0).reshape(1 + NB, 2, W)
    pool = got["out_pool_state"].reshape(WT, P, 1 + NB, PST).transpose(2, 3, 0, 1).reshape(1 + NB, PST, W)
    v = got["out_v"].transpose(2, 1, 0).reshape(1, NB, NL, W)
    return (y[:TP].reshape(1, TP, D), y[TP:].reshape(NB, NL, D), conv[:1][None], pool[:1][None], conv[1:][None],
            pool[1:][None], v)
```
